# Optimizing a Trainium2 kernel written in Bass

```python
import functools
import jax, jax.numpy as jnp
from jax import lax
import numpy as np

D_MODEL = 1024
BATCH = 1
SEQ = 1024
DEPTH = 1
DEC_BATCH = 8
DEC_SEQ = 4
PAST_LEN = 4096
PAGE_SIZE = 128

HEAD_DIM = 64
N_HEADS_A = 8
N_KV_A = 4
GQA_GROUP = N_HEADS_A // N_KV_A
N_HEADS_B = 8
DILATED_BRANCHES = ((128, 1), (512, 4), (2048, 16))
MAX_WINDOW = 2048
Q_BLOCK = 128
D_FF = 2816
CONV_W = 3
PLE_DIM = 256
RMS_EPS = 1e-6
NEG_INF = -1e30
ATTN_SCALE = HEAD_DIM ** -0.5
WIDTH_A_Q = N_HEADS_A * HEAD_DIM
WIDTH_A_KV = N_KV_A * HEAD_DIM
WIDTH_B = N_HEADS_B * HEAD_DIM
D_MIX = WIDTH_A_Q + WIDTH_B
D_IN = WIDTH_A_Q + 2 * WIDTH_A_KV + N_HEADS_A + 3 * WIDTH_B
SPLIT_POINTS = (WIDTH_A_Q,
                WIDTH_A_Q + WIDTH_A_KV,
                WIDTH_A_Q + 2 * WIDTH_A_KV,
                WIDTH_A_Q + 2 * WIDTH_A_KV + N_HEADS_A,
                WIDTH_A_Q + 2 * WIDTH_A_KV + N_HEADS_A + WIDTH_B,
                WIDTH_A_Q + 2 * WIDTH_A_KV + N_HEADS_A + 2 * WIDTH_B)

kernel_name = 'hymba_fox_dilated_convffn_step'

def rmsnorm(x, g):
    xf = x.astype(jnp.float32)
    y = xf * lax.rsqrt(jnp.mean(xf * xf, axis=-1, keepdims=True) + RMS_EPS)
    return (y * g.astype(jnp.float32)).astype(x.dtype)

def alibi_slopes(n):
    return 2.0 ** (-8.0 * jnp.arange(1, n + 1, dtype=jnp.float32) / n)

def project(x, g, w_in, b_f):
    bsz, t = x.shape[:2]
    z = jnp.einsum('btd,de->bte', rmsnorm(x, g), w_in)
    aq, ak, av, af, bq, bk, bv = jnp.split(z, SPLIT_POINTS, axis=-1)
    heads = lambda a, n: a.reshape(bsz, t, n, HEAD_DIM)
    logf = jax.nn.log_sigmoid(af.astype(jnp.float32) + b_f.astype(jnp.float32))
    return (heads(aq, N_HEADS_A), heads(ak, N_KV_A), heads(av, N_KV_A), logf,
            heads(bq, N_HEADS_B), heads(bk, N_HEADS_B), heads(bv, N_HEADS_B))

def fox_prompt(q, k, v, logf):
    bsz, s_len = q.shape[:2]
    nblk = s_len // Q_BLOCK
    c_t = jnp.cumsum(logf, axis=1).reshape(bsz, s_len, N_KV_A, GQA_GROUP)
    c_key = c_t.transpose(0, 2, 3, 1)
    qb = q.reshape(bsz, nblk, Q_BLOCK, N_KV_A, GQA_GROUP, HEAD_DIM).swapaxes(0, 1)
    cb = c_t.reshape(bsz, nblk, Q_BLOCK, N_KV_A, GQA_GROUP).swapaxes(0, 1)
    key_pos = jnp.arange(s_len)

    def block(args):
        qi, ci, bi = args
        q_pos = bi * Q_BLOCK + jnp.arange(Q_BLOCK)
        s = jnp.einsum('bqkgd,bskd->bkgqs', qi, k, preferred_element_type=jnp.float32) * ATTN_SCALE
        s = s + ci.transpose(0, 2, 3, 1)[..., None] - c_key[:, :, :, None, :]
        s = jnp.where(key_pos[None, :] <= q_pos[:, None], s, NEG_INF)
        p = jax.nn.softmax(s, axis=-1)
        return jnp.einsum('bkgqs,bskd->bqkgd', p.astype(v.dtype), v,
                          preferred_element_type=jnp.float32).astype(v.dtype)

    o = lax.map(block, (qb, cb, jnp.arange(nblk)))
    return o.swapaxes(0, 1).reshape(bsz, s_len, WIDTH_A_Q)

def fox_sample(q, k_new, v_new, logf_new, k_pool, v_pool, logf_pool, page_table):
    bsz, t = q.shape[:2]
    past = page_table.shape[1] * PAGE_SIZE
    k_past = k_pool[page_table].reshape(bsz, past, N_KV_A, HEAD_DIM)
    v_past = v_pool[page_table].reshape(bsz, past, N_KV_A, HEAD_DIM)
    lf_past = logf_pool[page_table].reshape(bsz, past, N_HEADS_A).astype(jnp.float32)
    c = jnp.cumsum(jnp.concatenate([lf_past, logf_new], axis=1), axis=1)
    c_key = c.reshape(bsz, past + t, N_KV_A, GQA_GROUP).transpose(0, 2, 3, 1)
    qg = q.reshape(bsz, t, N_KV_A, GQA_GROUP, HEAD_DIM)
    s = jnp.concatenate([
        jnp.einsum('btkgd,bskd->bkgts', qg, k_past, preferred_element_type=jnp.float32),
        jnp.einsum('btkgd,bskd->bkgts', qg, k_new, preferred_element_type=jnp.float32)], axis=-1) * ATTN_SCALE
    s = s + c_key[..., past:, None] - c_key[:, :, :, None, :]
    mask = jnp.arange(past + t)[None, :] <= past + jnp.arange(t)[:, None]
    s = jnp.where(mask, s, NEG_INF)
    p = jax.nn.softmax(s, axis=-1).astype(v_new.dtype)
    o = (jnp.einsum('bkgts,bskd->btkgd', p[..., :past], v_past, preferred_element_type=jnp.float32)
         + jnp.einsum('bkgts,bskd->btkgd', p[..., past:], v_new, preferred_element_type=jnp.float32))
    return o.astype(v_new.dtype).reshape(bsz, t, WIDTH_A_Q)

def dilated_branch_prompt(q, k, v, window, dil, slopes):
    bsz, s_len, nh, dh = q.shape
    n_units = window // dil
    sub_len = s_len // dil
    nblk = -(-sub_len // Q_BLOCK)
    sub_pad = nblk * Q_BLOCK

    def to_blocks(a):
        a = a.reshape(bsz, sub_len, dil, nh, dh).transpose(0, 2, 1, 3, 4)
        a = jnp.pad(a, ((0, 0), (0, 0), (0, sub_pad - sub_len), (0, 0), (0, 0)))
        return a.reshape(bsz, dil, nblk, Q_BLOCK, nh, dh)

    def with_prev(a):
        prev = jnp.pad(a, ((0, 0), (0, 0), (1, 0), (0, 0), (0, 0), (0, 0)))[:, :, :-1]
        return jnp.concatenate([prev, a], axis=3)

    qb = to_blocks(q)
    k2 = with_prev(to_blocks(k))
    v2 = with_prev(to_blocks(v))
    s = jnp.einsum('brnqhd,brnkhd->brnhqk', qb, k2, preferred_element_type=jnp.float32) * ATTN_SCALE
    qi = jnp.arange(Q_BLOCK)[:, None]
    ki = jnp.arange(2 * Q_BLOCK)[None, :]
    dist = qi + Q_BLOCK - ki
    blk = jnp.arange(nblk)[:, None, None]
    valid = (dist >= 0) & (dist <= n_units) & (blk * Q_BLOCK - Q_BLOCK + ki >= 0)
    bias = -slopes[:, None, None] * (dist * dil).astype(jnp.float32)
    s = jnp.where(valid[:, None], s + bias, NEG_INF)
    m = jnp.max(s, axis=-1, keepdims=True)
    e = jnp.exp(s - m)
    l = jnp.sum(e, axis=-1)
    o = jnp.einsum('brnhqk,brnkhd->brnqhd', e.astype(v.dtype), v2, preferred_element_type=jnp.float32)

    def from_blocks(a):
        tail = a.shape[4:]
        a = a.reshape(bsz, dil, sub_pad, *tail)[:, :, :sub_len]
        return jnp.swapaxes(a, 1, 2).reshape(bsz, s_len, *tail)

    return (from_blocks(jnp.swapaxes(m[..., 0], 3, 4)), from_blocks(jnp.swapaxes(l, 3, 4)), from_blocks(o))

def dilated_branch_sample(q, k_cat, v_cat, window, dil, slopes, buf_len, past_len):
    t = q.shape[1]
    n_units = window // dil
    j = jnp.arange(t)[:, None]
    dist = jnp.arange(n_units + 1)[None, :] * dil
    local = buf_len + j - dist
    valid = (past_len + j - dist >= 0) & (local >= 0)
    idx = jnp.clip(local, 0, None)
    kg = jnp.take(k_cat, idx, axis=1)
    vg = jnp.take(v_cat, idx, axis=1)
    s = jnp.einsum('bthd,btkhd->bhtk', q, kg, preferred_element_type=jnp.float32) * ATTN_SCALE
    s = jnp.where(valid, s - slopes[:, None, None] * dist.astype(jnp.float32), NEG_INF)
    m = jnp.max(s, axis=-1, keepdims=True)
    e = jnp.exp(s - m)
    l = jnp.sum(e, axis=-1)
    o = jnp.einsum('bhtk,btkhd->bthd', e.astype(v_cat.dtype), vg, preferred_element_type=jnp.float32)
    return (jnp.swapaxes(m[..., 0], 1, 2), jnp.swapaxes(l, 1, 2), o)

def merge_branches(parts):
    ms = jnp.stack([pt[0] for pt in parts])
    ls = jnp.stack([pt[1] for pt in parts])
    os_ = jnp.stack([pt[2] for pt in parts])
    w = jnp.exp(ms - jnp.max(ms, axis=0, keepdims=True))
    num = jnp.sum(w[..., None] * os_, axis=0)
    den = jnp.sum(w * ls, axis=0)
    return num / den[..., None]

def layer_tail(x, mix, p, conv_prev, w_out, g_attn_post, g_ffn_pre, w_up, conv_w, conv_b, w_down,
               g_ffn_post, g_ple, w_ple_gate, w_ple):
    x = x + rmsnorm(jnp.einsum('btm,md->btd', mix, w_out), g_attn_post)
    t = x.shape[1]
    u = jnp.einsum('btd,df->btf', rmsnorm(x, g_ffn_pre), w_up)
    ext = jnp.concatenate([conv_prev.astype(u.dtype), u], axis=1)
    hcv = conv_b + conv_w[0] * ext[:, 0:t]
    for j in range(1, CONV_W):
        hcv = hcv + conv_w[j] * ext[:, j:j + t]
    a, b = jnp.split(hcv, 2, axis=-1)
    y = jnp.einsum('btf,fd->btd', jax.nn.gelu(a, approximate=True) * b, w_down)
    x = x + rmsnorm(y, g_ffn_post)
    gate = jax.nn.sigmoid(jnp.einsum('btd,de->bte', rmsnorm(x, g_ple), w_ple_gate))
    x = x + gate * jnp.einsum('btp,pd->btd', p, w_ple)
    return x, ext[:, t:]

def setup_inputs(seed: int = 0) -> dict:
    key = jax.random.key(seed)
    ks = iter(jax.random.split(key, 40))
    nrm = lambda shape, scale: scale * jax.random.normal(next(ks), shape, jnp.float32)
    gain = lambda: 1.0 + nrm((DEPTH, D_MODEL), 0.1)
    n_pages = PAST_LEN // PAGE_SIZE
    n_pool = (DEC_BATCH * n_pages * 5) // 4
    win_len = min(MAX_WINDOW, PAST_LEN)
    perm = jax.random.permutation(next(ks), n_pool)
    page_table = perm[:DEC_BATCH * n_pages].reshape(DEC_BATCH, n_pages).astype(jnp.int32)
    return {
        'x_prompt': nrm((BATCH, SEQ, D_MODEL), 1.0),
        'x_sample': nrm((DEC_BATCH, DEC_SEQ, D_MODEL), 1.0),
        'p_prompt': nrm((DEPTH, BATCH, SEQ, PLE_DIM), 1.0),
        'p_sample': nrm((DEPTH, DEC_BATCH, DEC_SEQ, PLE_DIM), 1.0),
        'cache_fox_k': nrm((DEPTH, n_pool, PAGE_SIZE, N_KV_A, HEAD_DIM), 1.0),
        'cache_fox_v': nrm((DEPTH, n_pool, PAGE_SIZE, N_KV_A, HEAD_DIM), 1.0),
        'cache_fox_logf': jax.nn.log_sigmoid(2.5 + nrm((DEPTH, n_pool, PAGE_SIZE, N_HEADS_A), 1.0)),
        'cache_win_k': nrm((DEPTH, DEC_BATCH, win_len, N_HEADS_B, HEAD_DIM), 1.0),
        'cache_win_v': nrm((DEPTH, DEC_BATCH, win_len, N_HEADS_B, HEAD_DIM), 1.0),
        'state_conv': nrm((DEPTH, DEC_BATCH, CONV_W - 1, 2 * D_FF), 1.0),
        'page_table': page_table,
        'g_attn_pre': gain(),
        'w_in': nrm((DEPTH, D_MODEL, D_IN), D_MODEL ** -0.5),
        'b_forget': jax.random.uniform(next(ks), (DEPTH, N_HEADS_A), jnp.float32, 1.0, 4.0),
        'w_out': nrm((DEPTH, D_MIX, D_MODEL), D_MIX ** -0.5),
        'g_attn_post': gain(),
        'g_ffn_pre': gain(),
        'w_up': nrm((DEPTH, D_MODEL, 2 * D_FF), D_MODEL ** -0.5),
        'conv_w': nrm((DEPTH, CONV_W, 2 * D_FF), CONV_W ** -0.5),
        'conv_b': nrm((DEPTH, 2 * D_FF), 0.01),
        'w_down': nrm((DEPTH, D_FF, D_MODEL), D_FF ** -0.5),
        'g_ffn_post': gain(),
        'g_ple': gain(),
        'w_ple_gate': nrm((DEPTH, D_MODEL, D_MODEL), D_MODEL ** -0.5),
        'w_ple': nrm((DEPTH, PLE_DIM, D_MODEL), PLE_DIM ** -0.5),
    }

def reference(x_prompt, x_sample, p_prompt, p_sample, cache_fox_k, cache_fox_v, cache_fox_logf,
              cache_win_k, cache_win_v, state_conv, page_table, g_attn_pre, w_in, b_forget, w_out,
              g_attn_post, g_ffn_pre, w_up, conv_w, conv_b, w_down, g_ffn_post, g_ple, w_ple_gate, w_ple):
    slopes = alibi_slopes(N_HEADS_B)
    past_len = page_table.shape[1] * PAGE_SIZE
    xp, xs = x_prompt, x_sample
    bsz_p, seq = xp.shape[:2]
    bsz_s, t_s = xs.shape[:2]
    win_p = min(MAX_WINDOW, seq)
    fk_p, fv_p, fl_p, wk_p, wv_p, cv_p = [], [], [], [], [], []
    fk_s, fv_s, fl_s, wk_s, wv_s, cv_s = [], [], [], [], [], []
    for i in range(DEPTH):
        tail = functools.partial(layer_tail, w_out=w_out[i], g_attn_post=g_attn_post[i], g_ffn_pre=g_ffn_pre[i],
                                 w_up=w_up[i], conv_w=conv_w[i], conv_b=conv_b[i], w_down=w_down[i],
                                 g_ffn_post=g_ffn_post[i], g_ple=g_ple[i], w_ple_gate=w_ple_gate[i], w_ple=w_ple[i])
        aq, ak, av, lf, bq, bk, bv = project(xp, g_attn_pre[i], w_in[i], b_forget[i])
        o_a = fox_prompt(aq, ak, av, lf)
        o_b = merge_branches([dilated_branch_prompt(bq, bk, bv, w, d, slopes) for (w, d) in DILATED_BRANCHES])
        mix = jnp.concatenate([o_a, o_b.reshape(bsz_p, seq, WIDTH_B).astype(xp.dtype)], axis=-1)
        xp, conv_new = tail(xp, mix, p_prompt[i], jnp.zeros((bsz_p, CONV_W - 1, 2 * D_FF), xp.dtype))
        fk_p.append(ak); fv_p.append(av); fl_p.append(lf)
        wk_p.append(bk[:, seq - win_p:]); wv_p.append(bv[:, seq - win_p:]); cv_p.append(conv_new)
        aq, ak, av, lf, bq, bk, bv = project(xs, g_attn_pre[i], w_in[i], b_forget[i])
        o_a = fox_sample(aq, ak, av, lf, cache_fox_k[i], cache_fox_v[i], cache_fox_logf[i], page_table)
        buf_len = cache_win_k.shape[2]
        k_cat = jnp.concatenate([cache_win_k[i], bk], axis=1)
        v_cat = jnp.concatenate([cache_win_v[i], bv], axis=1)
        o_b = merge_branches([dilated_branch_sample(bq, k_cat, v_cat, w, d, slopes, buf_len, past_len)
                              for (w, d) in DILATED_BRANCHES])
        mix = jnp.concatenate([o_a, o_b.reshape(bsz_s, t_s, WIDTH_B).astype(xs.dtype)], axis=-1)
        xs, conv_new = tail(xs, mix, p_sample[i], state_conv[i])
        fk_s.append(ak); fv_s.append(av); fl_s.append(lf)
        wk_s.append(bk); wv_s.append(bv); cv_s.append(conv_new)
    y_prompt = xp
    y_sample = xs
    new_fox_k_prompt = jnp.stack(fk_p)
    new_fox_v_prompt = jnp.stack(fv_p)
    new_fox_logf_prompt = jnp.stack(fl_p)
    new_win_k_prompt = jnp.stack(wk_p)
    new_win_v_prompt = jnp.stack(wv_p)
    new_conv_prompt = jnp.stack(cv_p)
    new_fox_k_sample = jnp.stack(fk_s)
    new_fox_v_sample = jnp.stack(fv_s)
    new_fox_logf_sample = jnp.stack(fl_s)
    new_win_k_sample = jnp.stack(wk_s)
    new_win_v_sample = jnp.stack(wv_s)
    new_conv_sample = jnp.stack(cv_s)
    return (y_prompt, y_sample, new_fox_k_prompt, new_fox_v_prompt, new_fox_logf_prompt, new_win_k_prompt,
            new_win_v_prompt, new_conv_prompt, new_fox_k_sample, new_fox_v_sample, new_fox_logf_sample,
            new_win_k_sample, new_win_v_sample, new_conv_sample)


_drawn_inputs = setup_inputs


def setup_inputs(seed=0):
    import zlib

    import numpy as np

    out = dict(_drawn_inputs(seed))
    spreads = {}
    factors = {'conv_b': 7.087, 'g_ple': 4.817}
    for name, (base, spread) in spreads.items():
        noise = np.random.default_rng([zlib.crc32(name.encode()), seed]).standard_normal(out[name].shape)
        drawn = base * np.exp(spread * noise) if base else spread * noise
        out[name] = __import__('jax').numpy.asarray(drawn.astype(out[name].dtype))
    for name, factor in factors.items():
        out[name] = (out[name] * factor).astype(out[name].dtype)
    return out
```

```python
import numpy as np
import concourse.bass as bass
from concourse import mybir
from contextlib import ExitStack

F32 = mybir.dt.float32
F32R = mybir.dt.float32r
BF16 = mybir.dt.bfloat16
I32 = mybir.dt.int32
ALU = mybir.AluOpType
ACT = mybir.ActivationFunctionType
AX = mybir.AxisListType
ds = bass.ds

D_MODEL = 1024
SEQ = 1024
DEC_BATCH = 8
DEC_SEQ = 4
PAST_LEN = 4096
PAGE = 128
HEAD = 64
HEADS_A = 8
KV_A = 4
GROUP_A = HEADS_A // KV_A
HEADS_B = 8
WINDOW = 2048
D_FF = 2816
PLE = 256
EPS = 1e-6
SCALE = HEAD ** -0.5
NEG = -1e30
N_PAGES = PAST_LEN // PAGE

P = 128
N_NEW = DEC_BATCH * DEC_SEQ
TOK = SEQ + N_NEW
KT = D_MODEL // P
TILES = [(t * P, P) for t in range(SEQ // P)] + [(SEQ, N_NEW)]
NT = len(TILES)
NPT = SEQ // P
CH = 512
LOGF_COL = 2 * CH
CHUNK_COLS = [0, CH, LOGF_COL + HEADS_A, LOGF_COL + HEADS_A + CH, LOGF_COL + HEADS_A + 2 * CH]
NC = len(CHUNK_COLS)
DENSE_ROWS = 4
WIN_ROWS = DENSE_ROWS + (WINDOW - DENSE_ROWS * P) // (P * 16 // DEC_SEQ)
RMAX = bass.bass_isa.ReduceOp.max
RADD = bass.bass_isa.ReduceOp.add


def norm_and_project(nc, d, sh):
    with ExitStack() as ctx:
        sb = lambda n, s, t=F32: ctx.enter_context(nc.sbuf_tensor(n, s, t))
        pb = lambda n, s, t=F32: ctx.enter_context(nc.psum_tensor(n, s, t))
        sem = lambda n: nc.alloc_semaphore(n)
        x_in = sb("p_x_in", [P, 2, D_MODEL])
        gain = sb("p_gain", [P, D_MODEL])
        x_norm = sb("p_x_norm", [P, 2, D_MODEL])
        square = sb("p_square", [P, D_MODEL])
        mean_sq = sb("p_mean_sq", [P, NT])
        rms = sb("p_rms", [P, NT])
        rstd = sb("p_rstd", [P, NT])
        xt_hi = sb("p_xt_hi", [P, KT, TOK], F32R)
        xt_lo = sb("p_xt_lo", [P, KT, TOK], F32R)
        w_raw = sb("p_w_raw", [P, 2, KT, CH])
        w_hi = sb("p_w_hi", [P, 2, KT, CH], F32R)
        w_lo = sb("p_w_lo", [P, 2, KT, CH], F32R)
        wf_raw = sb("p_wf_raw", [P, KT, HEADS_A])
        wf_hi = sb("p_wf_hi", [P, KT, HEADS_A], F32R)
        wf_lo = sb("p_wf_lo", [P, KT, HEADS_A], F32R)
        z_out = sb("p_z_out", [P, 3, CH])
        b_f = sb("p_b_f", [P, HEADS_A])
        lf_pre = sb("p_lf_pre", [P, NT, HEADS_A])
        lf_tmp = sb("p_lf_tmp", [P, NT, HEADS_A])
        lf_min = sb("p_lf_min", [P, NT, HEADS_A])
        pt = pb("p_pt", [P, 2, D_MODEL])
        pz = pb("p_pz", [P, 3, CH])
        pf = pb("p_pf", [P, NT, HEADS_A])

        x_loaded = [sem(f"p_x_loaded{i}") for i in range(2)]
        gain_loaded = sem("p_gain_loaded")
        w_loaded = [sem(f"p_w_loaded{i}") for i in range(2)]
        wf_loaded = sem("p_wf_loaded")
        bf_loaded = sem("p_bf_loaded")
        stored = [sem(f"p_stored{i}") for i in range(3)]
        lf_stored = sem("p_lf_stored")
        squared = sem("p_squared")
        mean_ready = sem("p_mean_ready")
        rooted = sem("p_rooted")
        rstd_ready = sem("p_rstd_ready")
        normed = sem("p_normed")
        transposed = sem("p_transposed")
        hi_ready = sem("p_hi_ready")
        lo_ready = sem("p_lo_ready")
        w_hi_ready = sem("p_w_hi_ready")
        w_lo_ready = sem("p_w_lo_ready")
        wf_hi_ready = sem("p_wf_hi_ready")
        wf_lo_ready = sem("p_wf_lo_ready")
        z_done = sem("p_z_done")
        z_act = sem("p_z_act")
        z_dve = sem("p_z_dve")
        pf_done = sem("p_pf_done")
        lf_step = sem("p_lf_step")
        lf_act = sem("p_lf_act")
        ident_ready = sem("p_ident_ready")

        w_in = d["w_in"][0].rearrange("(k p) n -> p k n", p=P)
        act_tiles = [t for t in range(NT) if t % 2 == 0]
        dve_tiles = [t for t in range(NT) if t % 2 == 1]

        def evacuated(eng, c, t):
            if t % 2 == 0:
                eng.wait_ge(z_act, len(act_tiles) * c + t // 2 + 1)
            else:
                eng.wait_ge(z_dve, len(dve_tiles) * c + t // 2 + 1)

        def rows_of(name_p, name_s, t, c0, cols):
            t0, n = TILES[t]
            return d[name_p][t0:t0 + n, c0:c0 + cols] if t < NPT else d[name_s][0:n, c0:c0 + cols]

        def destinations(c, t):
            if c == 0 or c == 2:
                t0, n = TILES[t]
                return [(0, CH, d["q_scratch"][t0:t0 + n, (c // 2) * CH:(c // 2 + 1) * CH])]
            if c == 1:
                return [(0, CH // 2, rows_of("fk_p", "fk_s", t, 0, CH // 2)),
                        (CH // 2, CH // 2, rows_of("fv_p", "fv_s", t, 0, CH // 2))]
            pair = ("wk_p", "wk_s") if c == 3 else ("wv_p", "wv_s")
            return [(0, CH, rows_of(*pair, t, 0, CH))]

        def store_count(c, t, through):
            n = 0
            for cc in range(c + 1):
                for tt in range(t % 3, NT, 3):
                    if (cc, tt) < (c, t) or (through and (cc, tt) == (c, t)):
                        n += 16 * len(destinations(cc, tt))
            return n

        with nc.Block() as block:
            @block.sync
            def _(sp):
                def load_x(t):
                    t0, n = TILES[t]
                    if t >= 2:
                        sp.wait_ge(normed, t - 1)
                    sp.dma_start(x_in[:n, t % 2, :], d["x"](t)).then_inc(x_loaded[t % 2], 16)

                def load_w(c):
                    if c >= 2:
                        sp.wait_ge(w_hi_ready, c - 1)
                        sp.wait_ge(w_lo_ready, c - 1)
                    sp.dma_start(w_raw[:, c % 2], w_in[:, :, CHUNK_COLS[c]:CHUNK_COLS[c] + CH])\
                        .then_inc(w_loaded[c % 2], 16)

                load_x(0)
                sp.dma_start(gain[:, :], d["g_attn_pre"][0].partition_broadcast(P)).then_inc(gain_loaded, 16)
                load_x(1)
                load_w(0)
                load_x(2)
                load_w(1)
                load_x(3)
                sp.dma_start(wf_raw[:, :, :], w_in[:, :, LOGF_COL:LOGF_COL + HEADS_A]).then_inc(wf_loaded, 16)
                sp.dma_start(b_f[:, :], d["b_forget"][0].partition_broadcast(P)).then_inc(bf_loaded, 16)
                for c in range(NC):
                    for t in range(NT):
                        if t == 4 and c + 2 < NC:
                            load_w(c + 2)
                        evacuated(sp, c, t)
                        for c0, cols, rows in destinations(c, t):
                            sp.dma_start(rows, z_out[:TILES[t][1], t % 3, c0:c0 + cols]).then_inc(stored[t % 3], 16)
                        if c == 0 and t + 4 < NT:
                            load_x(t + 4)
                sp.wait_ge(lf_step, 4)
                sp.dma_start(d["fl_p"].rearrange("(t p) h -> p t h", p=P), sh["logf"][:, 0:NPT, :])\
                    .then_inc(lf_stored, 16)
                sp.dma_start(d["fl_s"], sh["logf"][:N_NEW, NPT, :]).then_inc(lf_stored, 16)
                for s in range(3):
                    sp.wait_ge(stored[s], store_count(NC - 1, NT - 3 + s, True))
                sp.wait_ge(lf_stored, 32)

            @block.gpsimd
            def _(pool):
                nc.gpsimd.memset(sh["ident"][:, :], 0.0).then_inc(ident_ready, 1)
                pool.wait_ge(ident_ready, 1)
                nc.gpsimd.affine_select(out=sh["ident"][:, :], in_=sh["ident"][:, :], compare_op=ALU.not_equal,
                                        fill=1.0, base=0, pattern=[[-1, P]], channel_multiplier=1)\
                    .then_inc(ident_ready, 1)

            @block.scalar
            def _(act):
                def split_w(c):
                    act.wait_ge(w_loaded[c % 2], 16 * (c // 2 + 1))
                    if c >= 2:
                        act.wait_ge(z_done, NT * (c - 1))
                    nc.scalar.activation(w_hi[:, c % 2], w_raw[:, c % 2], ACT.Copy).then_inc(w_hi_ready, 1)

                def evacuate_z(c, t):
                    n = TILES[t][1]
                    act.wait_ge(z_done, NT * c + t + 1)
                    if store_count(c, t, False):
                        act.wait_ge(stored[t % 3], store_count(c, t, False))
                    nc.scalar.copy(z_out[:n, t % 3, :], pz[:n, t % 3, :]).then_inc(z_act, 1)

                def square_tile(t):
                    n = TILES[t][1]
                    act.wait_ge(x_loaded[t % 2], 16 * (t // 2 + 1))
                    nc.scalar.activation(square[:n, :], x_in[:n, t % 2, :], ACT.Square,
                                         accum_out=mean_sq[:n, t:t + 1]).then_inc(squared, 1)
                    act.wait_ge(mean_ready, t + 1)
                    nc.scalar.activation(rstd[:n, t:t + 1], rms[:n, t:t + 1], ACT.Sqrt).then_inc(rooted, 1)

                def split_hi(t):
                    t0, n = TILES[t]
                    act.wait_ge(transposed, t + 1)
                    nc.scalar.activation(xt_hi[:, :, t0:t0 + n],
                                         pt[:, t % 2, :].rearrange("p (k m) -> p k m", k=KT)[:, :, 0:n],
                                         ACT.Copy).then_inc(hi_ready, 1)

                square_tile(0)
                split_w(0)
                square_tile(1)
                split_hi(0)
                for c in range(NC):
                    for t in range(NT):
                        if c == 0 and t + 2 < NT:
                            square_tile(t + 2)
                        if c == 0 and t + 1 < NT:
                            split_hi(t + 1)
                        if c == 1 and t == 0:
                            act.wait_ge(wf_loaded, 16)
                            nc.scalar.activation(wf_hi[:, :, :], wf_raw[:, :, :], ACT.Copy).then_inc(wf_hi_ready, 1)
                        if t == 2 and c + 1 < NC:
                            split_w(c + 1)
                        if t % 2 == 0:
                            evacuate_z(c, t)
                act.wait_ge(lf_step, 2)
                nc.scalar.activation(lf_tmp[:, :, :], lf_pre[:, :, :], ACT.Abs).then_inc(lf_act, 1)
                act.wait_ge(lf_act, 1)
                nc.scalar.activation(lf_tmp[:, :, :], lf_tmp[:, :, :], ACT.Exp, scale=-1.0).then_inc(lf_act, 1)
                act.wait_ge(lf_act, 2)
                nc.scalar.activation(lf_tmp[:, :, :], lf_tmp[:, :, :], ACT.Ln, bias=1.0).then_inc(lf_act, 1)

            @block.vector
            def _(dve):
                def split_w(c):
                    dve.wait_ge(w_hi_ready, c + 1)
                    if c >= 2:
                        dve.wait_ge(z_done, NT * (c - 1))
                    nc.vector.tensor_tensor(w_lo[:, c % 2], w_raw[:, c % 2], w_hi[:, c % 2].bitcast(F32),
                                            ALU.subtract).then_inc(w_lo_ready, 1)

                def norm_tile(t):
                    n = TILES[t][1]
                    dve.wait_ge(squared, t + 1)
                    nc.vector.tensor_scalar(rms[:n, t:t + 1], mean_sq[:n, t:t + 1], 1.0 / D_MODEL, EPS,
                                            ALU.mult, ALU.add).then_inc(mean_ready, 1)
                    dve.wait_ge(rooted, t + 1)
                    nc.vector.reciprocal(rstd[:n, t:t + 1], rstd[:n, t:t + 1]).then_inc(rstd_ready, 1)
                    dve.wait_ge(rstd_ready, t + 1)
                    if t == 0:
                        dve.wait_ge(gain_loaded, 16)
                    if t >= 2:
                        dve.wait_ge(transposed, t - 1)
                    nc.vector.scalar_tensor_tensor(out=x_norm[:n, t % 2, :], in0=x_in[:n, t % 2, :],
                                                   scalar=rstd[:n, t:t + 1], in1=gain[:n, :],
                                                   op0=ALU.mult, op1=ALU.mult).then_inc(normed, 1)

                def split_lo(t):
                    t0, n = TILES[t]
                    dve.wait_ge(hi_ready, t + 1)
                    nc.vector.tensor_tensor(xt_lo[:, :, t0:t0 + n],
                                            pt[:, t % 2, :].rearrange("p (k m) -> p k m", k=KT)[:, :, 0:n],
                                            xt_hi[:, :, t0:t0 + n].bitcast(F32), ALU.subtract).then_inc(lo_ready, 1)

                def evacuate_z(c, t):
                    n = TILES[t][1]
                    dve.wait_ge(z_done, NT * c + t + 1)
                    if store_count(c, t, False):
                        dve.wait_ge(stored[t % 3], store_count(c, t, False))
                    nc.vector.tensor_copy(z_out[:n, t % 3, :], pz[:n, t % 3, :]).then_inc(z_dve, 1)

                nc.vector.memset(lf_pre[:, :, :], 0.0).then_inc(lf_step, 1)
                norm_tile(0)
                split_w(0)
                norm_tile(1)
                split_lo(0)
                for c in range(NC):
                    for t in range(NT):
                        if c == 0 and t + 2 < NT:
                            norm_tile(t + 2)
                        if c == 0 and t + 1 < NT:
                            split_lo(t + 1)
                        if c == 1 and t == 0:
                            dve.wait_ge(wf_hi_ready, 1)
                            nc.vector.tensor_tensor(wf_lo[:, :, :], wf_raw[:, :, :], wf_hi[:, :, :].bitcast(F32),
                                                    ALU.subtract).then_inc(wf_lo_ready, 1)
                        if t == 3 and c + 1 < NC:
                            split_w(c + 1)
                        if t % 2 == 1:
                            evacuate_z(c, t)
                dve.wait_ge(pf_done, 1)
                dve.wait_ge(bf_loaded, 16)
                dve.wait_ge(lf_step, 1)
                bias = b_f[:, None, :].broadcast_to([P, NT, HEADS_A])
                nc.vector.tensor_tensor(lf_pre[:, 0:NPT, :], pf[:, 0:NPT, :], bias[:, 0:NPT, :], ALU.add)
                nc.vector.tensor_tensor(lf_pre[:N_NEW, NPT, :], pf[:N_NEW, NPT, :], bias[:N_NEW, NPT, :], ALU.add)\
                    .then_inc(lf_step, 1)
                dve.wait_ge(lf_step, 2)
                nc.vector.tensor_scalar(lf_min[:, :, :], lf_pre[:, :, :], 0.0, None, ALU.min).then_inc(lf_step, 1)
                dve.wait_ge(lf_step, 3)
                dve.wait_ge(lf_act, 3)
                nc.vector.tensor_tensor(sh["logf"][:, :, :], lf_min[:, :, :], lf_tmp[:, :, :], ALU.subtract)\
                    .then_inc(lf_step, 1)

            @block.tensor
            def _(pe):
                def transpose_tile(t):
                    n = TILES[t][1]
                    pe.wait_ge(normed, t + 1)
                    if t >= 2:
                        pe.wait_ge(lo_ready, t - 1)
                    for k in range(KT):
                        last = nc.tensor.transpose(pt[:, t % 2, k * P:k * P + n], x_norm[:n, t % 2, k * P:(k + 1) * P],
                                                   sh["ident"][:n, :n])
                    last.then_inc(transposed, 1)

                def project(c, t, hi, lo, out):
                    t0, n = TILES[t]
                    for k in range(KT):
                        for a, b, part in ((xt_hi, hi, 0), (xt_hi, lo, 1), (xt_lo, hi, 2)):
                            last = nc.tensor.matmul(out, a[:, k, t0:t0 + n], b[:, k, :],
                                                    start=(k == 0 and part == 0), stop=(k == KT - 1 and part == 2))
                    return last

                pe.wait_ge(ident_ready, 2)
                transpose_tile(0)
                for c in range(NC):
                    pe.wait_ge(w_lo_ready, c + 1)
                    for t in range(NT):
                        if c == 0:
                            if t + 1 < NT:
                                transpose_tile(t + 1)
                            pe.wait_ge(lo_ready, t + 1)
                        if (c, t) >= (0, 3):
                            evacuated(pe, c if t >= 3 else c - 1, t - 3 if t >= 3 else NT - 3 + t)
                        project(c, t, w_hi[:, c % 2], w_lo[:, c % 2], pz[:TILES[t][1], t % 3, :]).then_inc(z_done, 1)
                pe.wait_ge(wf_lo_ready, 1)
                for t in range(NT):
                    last = project(NC, t, wf_hi, wf_lo, pf[:TILES[t][1], t, :])
                last.then_inc(pf_done, 1)


def build_tables(nc, d, sh):
    with ExitStack() as ctx:
        sb = lambda n, s, t=F32: ctx.enter_context(nc.sbuf_tensor(n, s, t))
        sem = lambda n: nc.alloc_semaphore(n)
        dist_i = sb("t_dist_i", [P, SEQ], I32)
        bits_i = sb("t_bits_i", [P, SEQ], I32)
        near = sb("t_near", [P, SEQ])
        count = sb("t_count", [P, SEQ])
        term = sb("t_term", [P, SEQ])
        carry = sb("t_carry", [P, HEADS_A, NPT])
        totals = sb("t_totals", [P, HEADS_A, NPT])
        sums = sb("t_sums", [P, HEADS_A, NPT])
        p_within = ctx.enter_context(nc.psum_tensor("t_p_within", [P, HEADS_A, NPT], F32))
        p_totals = ctx.enter_context(nc.psum_tensor("t_p_totals", [P, HEADS_A, NPT], F32))
        pool_step = sem("t_pool_step")
        dve_step = sem("t_dve_step")
        act_step = sem("t_act_step")
        sums_ready = sem("t_sums_ready")

        with nc.Block() as block:
            @block.gpsimd
            def _(pool):
                nc.gpsimd.iota(dist_i[:, :], pattern=[[-1, SEQ]], base=SEQ - P, channel_multiplier=1).then_inc(pool_step, 1)
                nc.gpsimd.memset(sh["ones"][:, :], 1.0).then_inc(pool_step, 1)
                nc.gpsimd.memset(sh["ident_bf"][:, :], 0.0).then_inc(pool_step, 1)
                nc.gpsimd.memset(sh["mask_bf"][:, :], 0.0).then_inc(pool_step, 1)
                pool.wait_ge(pool_step, 4)
                nc.gpsimd.affine_select(out=sh["ident_bf"][:, :], in_=sh["ident_bf"][:, :], compare_op=ALU.not_equal,
                                        fill=1.0, base=0, pattern=[[-1, P]], channel_multiplier=1).then_inc(pool_step, 1)
                nc.gpsimd.affine_select(out=sh["tri"][:, :], in_=sh["ones"][:, :], compare_op=ALU.is_ge,
                                        fill=0.0, base=0, pattern=[[1, P]], channel_multiplier=-1).then_inc(pool_step, 1)
                nc.gpsimd.affine_select(out=sh["mask_bf"][:, :], in_=sh["mask_bf"][:, :], compare_op=ALU.is_ge,
                                        fill=NEG, base=0, pattern=[[-1, P]], channel_multiplier=1).then_inc(pool_step, 1)

            @block.tensor
            def _(pe):
                pe.wait_ge(pool_step, 6)
                lf = sh["logf"][:, 0:NPT, :].rearrange("p t h -> p h t")
                nc.tensor.matmul(p_within[:, :, :], sh["tri"][:, :], lf, start=True, stop=True)
                nc.tensor.matmul(p_totals[:, :, :], sh["ones"][:, :], lf, start=True, stop=True).then_inc(sums_ready, 1)

            @block.vector
            def _(dve):
                steps = [0]

                def chained(ins):
                    steps[0] += 1
                    ins.then_inc(dve_step, 1)
                    dve.wait_ge(dve_step, steps[0])

                dve.wait_ge(pool_step, 1)
                chained(nc.vector.tensor_copy(sh["dist"][:, :], dist_i[:, :]))
                chained(nc.vector.tensor_scalar(count[:, :], sh["dist"][:, :], 128.0, None, ALU.is_le))
                for n, reach in ((3, 512.0), (15, 2048.0)):
                    chained(nc.vector.tensor_scalar(bits_i[:, :], dist_i[:, :], n, None, ALU.bitwise_and))
                    chained(nc.vector.tensor_scalar(near[:, :], bits_i[:, :], 0.0, None, ALU.is_equal))
                    chained(nc.vector.scalar_tensor_tensor(out=term[:, :], in0=sh["dist"][:, :], scalar=reach,
                                                           in1=near[:, :], op0=ALU.is_le, op1=ALU.mult))
                    chained(nc.vector.tensor_tensor(count[:, :], count[:, :], term[:, :], ALU.add))
                chained(nc.vector.scalar_tensor_tensor(out=count[:, :], in0=sh["dist"][:, :], scalar=0.0,
                                                       in1=count[:, :], op0=ALU.is_ge, op1=ALU.mult))
                chained(nc.vector.tensor_scalar(near[:, :], count[:, :], 1.0, None, ALU.max))
                dve.wait_ge(act_step, 1)
                chained(nc.vector.tensor_scalar(term[:, :], count[:, :], 0.0, NEG, ALU.is_equal, ALU.mult))
                chained(nc.vector.tensor_tensor(sh["log_count"][:, :], near[:, :], term[:, :], ALU.add))
                for h in range(HEADS_B):
                    last = nc.vector.memset(sh["neg_slope"][:, h:h + 1], -2.0 ** (-8.0 * (h + 1) / HEADS_B))
                chained(last)
                chained(nc.vector.memset(carry[:, :, :], 1.0))
                chained(nc.vector.memset(carry[:, :, 0:1], 0.0))
                dve.wait_ge(sums_ready, 1)
                chained(nc.vector.tensor_copy(totals[:, :, :], p_totals[:, :, :]))
                flat = lambda a: a[:, :, :].rearrange("p h t -> p (h t)")
                chained(nc.vector.tensor_tensor_scan(flat(sums), flat(carry), flat(totals), 0.0, ALU.mult, ALU.add))
                chained(nc.vector.tensor_tensor(totals[:, :, :], totals[:, :, :], sums[:, :, :], ALU.subtract))
                chained(nc.vector.tensor_tensor(sh["neg_c"][:, :, :], totals[:, :, :], p_within[:, :, :], ALU.subtract))

            @block.scalar
            def _(act):
                act.wait_ge(dve_step, 12)
                nc.scalar.activation(near[:, :], near[:, :], ACT.Ln).then_inc(act_step, 1)


def prompt_attention(nc, d, sh, kind):
    NK = 1 if kind == "A" else 2
    KW = NK * HEAD
    PAIRS = 4
    UNITS = 2 * NPT
    col0 = 0 if kind == "A" else CH
    with ExitStack() as ctx:
        n_ = kind.lower() + "_"
        sb = lambda n, s, t=F32: ctx.enter_context(nc.sbuf_tensor(n_ + n, s, t))
        pb = lambda n, s, t=F32: ctx.enter_context(nc.psum_tensor(n_ + n, s, t))
        sem = lambda n: nc.alloc_semaphore(n_ + n)
        q_raw = sb("q_raw", [P, NPT, 2, HEAD])
        k_raw = sb("k_raw", [P, NPT, NK, HEAD])
        v_raw = sb("v_raw", [P, 2, NPT, KW])
        q_parts = sb("q_parts", [P, NPT, 2, 2, HEAD])
        k_high = sb("k_high", [P, NPT, NK, 2, HEAD])
        k_low = sb("k_low", [P, NPT, NK, 2, HEAD])
        diag = sb("diag", [P, 2, NPT, P])
        q_t = sb("q_t", [P, 2, SEQ], F32R)
        kh_t = sb("kh_t", [P, NK, SEQ], F32R)
        kl_t = sb("kl_t", [P, NK, SEQ], F32R)
        bias = sb("bias", [P, 2, SEQ])
        probs = sb("probs", [P, 4, SEQ])
        probs_t = sb("probs_t", [P, 4, CH])
        neg_max = sb("neg_max", [P, 4])
        denom = sb("denom", [P, 4])
        recip = sb("recip", [P, 4])
        mixed = sb("mixed", [P, 2, NPT, 2, HEAD])
        p_scores = pb("p_scores", [P, 2, SEQ])
        p_turn = pb("p_turn", [P, 2, CH])
        p_out = pb("p_out", [P, 2, CH])

        q_loaded, k_loaded = sem("q_loaded"), sem("k_loaded")
        v_loaded = sem("v_loaded")
        mixed_stored = sem("mixed_stored")
        high_ready, low_ready, diag_ready = sem("high_ready"), sem("low_ready"), sem("diag_ready")
        turned = sem("turned")
        turn_act, turn_dve = sem("turn_act"), sem("turn_dve")
        scored = sem("scored")
        biased = sem("biased")
        exped = sem("exped")
        summed = sem("summed")
        probs_t_used = sem("probs_t_used")
        out_read = sem("out_read")
        bias_ready = sem("bias_ready")
        spare = sem("spare")

        stack_events = [("q", h, half) for h in range(2) for half in range(2)]
        stack_events += [(part, h, half) for part in ("kh", "kl") for h in range(NK) for half in range(2)]
        if kind == "A":
            stack_events += [("bias", h, half) for h in range(2) for half in range(2)]
        units = [(h, qb) for h in range(2) for qb in range(NPT)]
        groups = []
        for u, (h, qb) in enumerate(units):
            for b0 in range(0, qb + 1, 4):
                groups.append((u, b0, min(4, qb + 1 - b0)))
        NS, NG = len(stack_events), len(groups)
        NE = NS + NG
        assert NS % 2 == 0 and NE % 2 == 0 and NG % 4 == 0
        groups_of = lambda u: [g for g, x in enumerate(groups) if x[0] == u]

        def wait_turned(eng, i, e):
            eng.wait_ge(turned, NE * i + e + 1)

        def stack_evacuate(eng, i, e, copy):
            what, h, half = stack_events[e]
            to = {"q": q_t, "kh": kh_t, "kl": kl_t, "bias": bias}[what]
            wait_turned(eng, i, e)
            copy(to[:, h, half * CH:(half + 1) * CH], p_turn[:, e % 2, :])\
                .then_inc(turn_act if e % 2 == 0 else turn_dve, 1)

        def probs_evacuate(eng, i, g, copy):
            e = NS + g
            n = groups[g][2] * P
            wait_turned(eng, i, e)
            eng.wait_ge(probs_t_used, NG * i + g + 1)
            copy(probs_t[:, g % 4, 0:n], p_turn[:, e % 2, 0:n])\
                .then_inc(turn_act if e % 2 == 0 else turn_dve, 1)

        with nc.Block() as block:
            def store(sp, i):
                sp.wait_ge(out_read, 2 + UNITS * (i + 1))
                sp.wait_ge(mixed_stored, 32 + 16 * i)
                sp.dma_start(d["mix_scratch"][0:SEQ, col0 + i * P:col0 + (i + 1) * P]
                             .rearrange("(t p) e -> p t e", p=P),
                             mixed[:, i % 2].rearrange("p t h e -> p t (h e)")).then_inc(mixed_stored, 16)

            @block.sync
            def _(sp):
                kv = ("fk_p", "fv_p") if kind == "A" else ("wk_p", "wv_p")
                for i in range(PAIRS):
                    if i >= 1:
                        sp.wait_ge(high_ready, 2 * i)
                        sp.wait_ge(low_ready, 2 * i)
                    sp.dma_start(q_raw[:, :, :, :].rearrange("p t h e -> p t (h e)"),
                                 d["q_scratch"][0:SEQ, col0 + i * P:col0 + (i + 1) * P]
                                 .rearrange("(t p) e -> p t e", p=P)).then_inc(q_loaded, 16)
                    sp.dma_start(k_raw[:, :, :, :].rearrange("p t h e -> p t (h e)"),
                                 d[kv[0]][:, i * KW:(i + 1) * KW].rearrange("(t p) e -> p t e", p=P))\
                        .then_inc(k_loaded, 16)
                    if i >= 1:
                        sp.wait_ge(v_loaded, 16 * i)
                    if i >= 2:
                        sp.wait_ge(probs_t_used, 4 + NG * (i - 1))
                    sp.dma_start(v_raw[:, i % 2], d[kv[1]][:, i * KW:(i + 1) * KW].rearrange("(t p) e -> p t e", p=P))\
                        .then_inc(v_loaded, 16)
                    if i >= 1:
                        store(sp, i - 1)
                store(sp, PAIRS - 1)
                sp.wait_ge(mixed_stored, 32 + 16 * PAIRS)

            @block.scalar
            def _(act):
                act.sem_inc(turn_act, 1)
                act.sem_inc(out_read, 2)
                act.sem_inc(mixed_stored, 32)
                with act.Fori(0, PAIRS) as i:
                    act.wait_ge(q_loaded, 16 * i + 16)
                    act.wait_ge(scored, UNITS * i + 1)
                    nc.scalar.activation(q_parts[:, :, :, 0, :].bitcast(F32R), q_raw[:, :, :, :], ACT.Copy, scale=SCALE)\
                        .then_inc(high_ready, 1)
                    act.wait_ge(k_loaded, 16 * i + 16)
                    for t in range(2):
                        ins = nc.scalar.activation(k_high[:, :, :, t, :].bitcast(F32R), k_raw[:, :, :, :], ACT.Copy)
                    ins.then_inc(high_ready, 1)
                    for e in range(0, NS, 2):
                        stack_evacuate(act, i, e, nc.scalar.copy)

                    def exp_unit(u):
                        n = (units[u][1] + 1) * P
                        act.wait_ge(biased, 2 + UNITS * i + u + 1)
                        nc.scalar.activation(probs[:, u % 4, 0:n], probs[:, u % 4, 0:n], ACT.Exp,
                                             bias=neg_max[:, u % 4:u % 4 + 1], scale=-1.0,
                                             accum_out=denom[:, u % 4:u % 4 + 1]).then_inc(exped, 1)

                    def scale_unit(u):
                        h, qb = units[u]
                        if u == 0:
                            act.wait_ge(mixed_stored, 16 * i + 16)
                        act.wait_ge(summed, UNITS * i + u + 1)
                        act.wait_ge(probs_t_used, 4 + NG * i + groups_of(u)[-1] + 1)
                        nc.scalar.activation(mixed[:, ds(i % 2, 1), qb, h, :], p_out[:, u % 2, 0:HEAD], ACT.Copy,
                                             scale=recip[:, u % 4:u % 4 + 1]).then_inc(out_read, 1)

                    for u in range(UNITS + 3):
                        if u < UNITS:
                            exp_unit(u)
                        if 1 <= u <= UNITS:
                            for g in groups_of(u - 1):
                                if (NS + g) % 2 == 0:
                                    probs_evacuate(act, i, g, nc.scalar.copy)
                        if u >= 3:
                            scale_unit(u - 3)

            @block.vector
            def _(dve):
                dve.sem_inc(turn_dve, 1)
                dve.sem_inc(biased, 2)
                with dve.Fori(0, PAIRS) as i:
                    dve.wait_ge(high_ready, 2 * i + 1)
                    nc.vector.scalar_tensor_tensor(out=q_parts[:, :, :, 1, :].bitcast(F32R), in0=q_raw[:, :, :, :],
                                                   scalar=SCALE, in1=q_parts[:, :, :, 0, :], op0=ALU.mult,
                                                   op1=ALU.subtract).then_inc(low_ready, 1)
                    dve.wait_ge(high_ready, 2 * i + 2)
                    for t in range(2):
                        ins = nc.vector.tensor_tensor(k_low[:, :, :, t, :].bitcast(F32R), k_raw[:, :, :, :],
                                                      k_high[:, :, :, t, :], ALU.subtract)
                    ins.then_inc(low_ready, 1)
                    for h in range(2):
                        if kind == "A":
                            ins = nc.vector.tensor_tensor(
                                diag[:, h], sh["ident"][:, None, :].broadcast_to([P, NPT, P]),
                                sh["neg_c"][:, ds(2 * i + h, 1), :].rearrange("p o t -> p (o t)")[:, :, None]
                                .broadcast_to([P, NPT, P]), ALU.mult)
                        else:
                            ins = nc.vector.scalar_tensor_tensor(
                                out=bias[:, h, :], in0=sh["dist"][:, :], scalar=sh["neg_slope"][:, ds(2 * i + h, 1)],
                                in1=sh["log_count"][:, :], op0=ALU.mult, op1=ALU.add)
                    ins.then_inc(diag_ready, 1)
                    for e in range(1, NS, 2):
                        stack_evacuate(dve, i, e, nc.vector.tensor_copy)

                    def bias_unit(u):
                        h, qb = units[u]
                        n = (qb + 1) * P
                        b0 = 0 if kind == "A" else SEQ - n
                        if u >= 4:
                            dve.wait_ge(turned, NE * i + NS + groups_of(u - 4)[-1] + 1)
                        dve.wait_ge(scored, UNITS * i + u + 2)
                        dve.sem_inc(spare, 1)
                        nc.vector.tensor_tensor_reduce(out=probs[:, u % 4, 0:n], in0=p_scores[:, u % 2, 0:n],
                                                       in1=bias[:, h, b0:b0 + n], scale=-1.0, scalar=3e38,
                                                       op0=ALU.add, op1=ALU.min,
                                                       accum_out=neg_max[:, u % 4:u % 4 + 1]).then_inc(biased, 1)

                    dve.wait_ge(turn_act, 1 + NE // 2 * i + NS // 2)
                    dve.wait_ge(turn_dve, 1 + NE // 2 * i + NS // 2)
                    dve.wait_ge(diag_ready, i + 1)
                    dve.sem_inc(spare, 1)
                    for u in range(UNITS + 1):
                        if u < UNITS:
                            bias_unit(u)
                        if u >= 1:
                            dve.wait_ge(exped, UNITS * i + u)
                            nc.vector.reciprocal(recip[:, (u - 1) % 4:(u - 1) % 4 + 1],
                                                 denom[:, (u - 1) % 4:(u - 1) % 4 + 1]).then_inc(summed, 1)
                            for g in groups_of(u - 1):
                                if (NS + g) % 2 == 1:
                                    probs_evacuate(dve, i, g, nc.vector.tensor_copy)

            @block.tensor
            def _(pe):
                pe.sem_inc(scored, 1)
                pe.sem_inc(probs_t_used, 4)

                def wait_bank(i, e):
                    pe.wait_ge(turn_act if e % 2 == 0 else turn_dve, NE // 2 * i + e // 2 + 1)

                with pe.Fori(0, PAIRS) as i:
                    for e, (what, h, half) in enumerate(stack_events):
                        wait_bank(i, e)
                        if what == "bias":
                            pe.wait_ge(diag_ready, i + 1)
                            nc.tensor.matmul(p_turn[:, e % 2, :], sh["ones"][:, :],
                                             diag[:, h, half * 4:(half + 1) * 4, :].rearrange("p t m -> p (t m)"),
                                             start=True, stop=True).then_inc(turned, 1)
                            continue
                        pe.wait_ge(low_ready, 2 * i + (1 if what == "q" else 2))
                        src = {"q": q_parts, "kh": k_high, "kl": k_low}[what]
                        for j in range(4):
                            last = nc.tensor.transpose(p_turn[:, e % 2, j * P:(j + 1) * P],
                                                       src[:, half * 4 + j, h].rearrange("p s e -> p (s e)"),
                                                       sh["ident"][:, :])
                        last.then_inc(turned, 1)
                    pe.wait_ge(turn_act, 1 + NE // 2 * i + NS // 2)
                    pe.wait_ge(turn_dve, 1 + NE // 2 * i + NS // 2)
                    pe.wait_ge(v_loaded, 16 * i + 16)

                    def score(u):
                        h, qb = units[u]
                        n = (qb + 1) * P
                        pe.wait_ge(biased, UNITS * i + u + 1)
                        for c0 in range(0, n, CH):
                            c1 = min(n, c0 + CH)
                            masked = kind == "A" and c1 == n
                            for part, k_t in enumerate((kh_t, kl_t)):
                                last = nc.tensor.matmul(p_scores[:, u % 2, c0:c1], q_t[:, h, qb * P:(qb + 1) * P],
                                                        k_t[:, h % NK, c0:c1], start=(part == 0),
                                                        stop=(part == 1 and not masked))
                            if masked:
                                last = nc.tensor.matmul(p_scores[:, u % 2, n - P:n], sh["ident_bf"][:, :],
                                                        sh["mask_bf"][:, :], start=False, stop=True)
                        last.then_inc(scored, 1)

                    def turn(u):
                        pe.wait_ge(exped, UNITS * i + u + 1)
                        for g in groups_of(u):
                            _, b0, nb = groups[g]
                            wait_bank(i, NS + g)
                            for j in range(nb):
                                last = nc.tensor.transpose(p_turn[:, (NS + g) % 2, j * P:(j + 1) * P],
                                                           probs[:, u % 4, (b0 + j) * P:(b0 + j + 1) * P],
                                                           sh["ident"][:, :])
                            last.then_inc(turned, 1)

                    def weigh(u):
                        h, qb = units[u]
                        pe.wait_ge(out_read, UNITS * i + u + 1)
                        for g in groups_of(u):
                            _, b0, nb = groups[g]
                            e = NS + g
                            pe.wait_ge(turn_act if e % 2 == 0 else turn_dve, NE // 2 * i + e // 2 + 2)
                            for j in range(nb):
                                b = b0 + j
                                last = nc.tensor.matmul(p_out[:, u % 2, 0:HEAD], probs_t[:, g % 4, j * P:(j + 1) * P],
                                                        v_raw[:, ds(i % 2, 1), b, (h % NK) * HEAD:(h % NK + 1) * HEAD],
                                                        start=(b == 0), stop=(b == qb))
                            last.then_inc(probs_t_used, 1)

                    score(0)
                    score(1)
                    for u in range(UNITS):
                        turn(u)
                        if u + 2 < UNITS:
                            score(u + 2)
                        if u >= 1:
                            weigh(u - 1)
                    weigh(UNITS - 1)


def sample_tables(nc, d, sh):
    POOL_ROWS = d["cache_fox_logf"].shape[1]
    GROUPS = DEC_BATCH * N_PAGES // P
    SEQS = DEC_BATCH // GROUPS
    RUNS = GROUPS * HEADS_A * SEQS
    with ExitStack() as ctx:
        sb = lambda n, s, t=F32: ctx.enter_context(nc.sbuf_tensor("c_" + n, s, t))
        pb = lambda n, s, t=F32: ctx.enter_context(nc.psum_tensor("c_" + n, s, t))
        sem = lambda n: nc.alloc_semaphore("c_" + n)
        page_ids = sb("page_ids", [P, GROUPS], I32)
        pages = sb("pages", [P, GROUPS, PAGE * HEADS_A])
        by_pos = sb("by_pos", [P, GROUPS, HEADS_A, P])
        totals = sb("totals", [P, RUNS, N_PAGES])
        sums = sb("sums", [P, RUNS, N_PAGES])
        carry = sb("carry", [P, RUNS, N_PAGES])
        same = sb("same", [N_NEW, N_NEW])
        own = sb("own", [N_NEW, DEC_BATCH])
        past = sb("past", [N_NEW, HEADS_A, DEC_BATCH])
        past_sum = sb("past_sum", [N_NEW, HEADS_A])
        neg_new = sb("neg_new", [N_NEW, HEADS_A])
        dist_i = sb("dist_i", [P, WIN_ROWS, HEADS_B, DEC_SEQ], I32)
        bits_i = sb("bits_i", [P, WIN_ROWS, HEADS_B, DEC_SEQ], I32)
        res_i = sb("res_i", [P, WIN_ROWS, HEADS_B, DEC_SEQ], I32)
        dist = sb("dist", [P, WIN_ROWS, HEADS_B, DEC_SEQ])
        near = sb("near", [P, WIN_ROWS, HEADS_B, DEC_SEQ])
        term = sb("term", [P, WIN_ROWS, HEADS_B, DEC_SEQ])
        count = sb("count", [P, WIN_ROWS, HEADS_B, DEC_SEQ])
        new_dist_i = sb("new_dist_i", [N_NEW, DEC_BATCH, HEADS_B, DEC_SEQ], I32)
        new_dist = sb("new_dist", [N_NEW, DEC_BATCH, HEADS_B, DEC_SEQ])
        p_big = pb("p_big", [P, 4 * CH])
        p_sum = pb("p_sum", [P, 4 * CH])
        ids_loaded = sem("ids_loaded")
        pages_loaded = [sem(f"pages_loaded{g}") for g in range(GROUPS)]
        clamped = sem("clamped")
        pool_step, dve_step, act_step, pe_step = sem("pool_step"), sem("dve_step"), sem("act_step"), sem("pe_step")

        with nc.Block() as block:
            @block.sync
            def _(sp):
                for g in range(GROUPS):
                    sp.dma_start(page_ids[:, g:g + 1], d["page_table"][g * SEQS:(g + 1) * SEQS, :]
                                 .rearrange("b (j o) -> (b j) o", o=1)).then_inc(ids_loaded, 16)

            @block.gpsimd
            def _(pool):
                pool.wait_ge(ids_loaded, 16 * GROUPS)
                rows = d["cache_fox_logf"][0].rearrange("n s h -> n (s h)")
                for g in range(GROUPS):
                    nc.gpsimd.indirect_dma_start(
                        out=pages[:, g, :], out_offset=None, in_=rows,
                        in_offset=bass.IndirectOffsetOnAxis(ap=page_ids[:, g:g + 1], axis=0),
                        bounds_check=POOL_ROWS - 1).then_inc(pages_loaded[g], 16)
                g_ = nc.gpsimd
                new, win = sh["new_mask"], [[0, HEADS_B], [1, DEC_SEQ]]
                g_.memset(new[:, :, :, :], 0.0).then_inc(pool_step, 1)
                g_.memset(same[:, :], 1.0).then_inc(pool_step, 1)
                g_.memset(own[:, :], 1.0).then_inc(pool_step, 1)
                g_.iota(dist_i[:, 0:DENSE_ROWS], pattern=[[-P, DENSE_ROWS]] + win, base=DENSE_ROWS * P,
                        channel_multiplier=-1).then_inc(pool_step, 1)
                g_.iota(dist_i[:, DENSE_ROWS:], pattern=[[-CH, WIN_ROWS - DENSE_ROWS], [0, HEADS_B], [DEC_SEQ, DEC_SEQ]],
                        base=WINDOW, channel_multiplier=-DEC_SEQ).then_inc(pool_step, 1)
                g_.iota(res_i[:, :], pattern=[[0, WIN_ROWS], [0, HEADS_B], [-1, DEC_SEQ]], base=P,
                        channel_multiplier=1).then_inc(pool_step, 1)
                g_.iota(new_dist_i[:, :], pattern=[[DEC_SEQ, DEC_BATCH]] + win, base=0,
                        channel_multiplier=-1).then_inc(pool_step, 1)
                pool.wait_ge(pool_step, 7)
                g_.affine_select(out=new[:, :, :, :], in_=new[:, :, :, :], compare_op=ALU.is_ge, fill=NEG, base=0,
                                 pattern=[[DEC_SEQ, DEC_BATCH]] + win, channel_multiplier=-1).then_inc(pool_step, 1)
                pool.wait_ge(pool_step, 8)
                g_.affine_select(out=new[:, :, :, :], in_=new[:, :, :, :], compare_op=ALU.is_ge, fill=NEG, base=0,
                                 pattern=[[-DEC_SEQ, DEC_BATCH], [0, HEADS_B], [0, DEC_SEQ]], channel_multiplier=1)\
                    .then_inc(pool_step, 1)
                g_.affine_select(out=same[:, :], in_=same[:, :], compare_op=ALU.is_ge, fill=0.0, base=0,
                                 pattern=[[1, N_NEW]], channel_multiplier=-1).then_inc(pool_step, 1)
                g_.affine_select(out=own[:, :], in_=own[:, :], compare_op=ALU.is_ge, fill=0.0, base=0,
                                 pattern=[[-DEC_SEQ, DEC_BATCH]], channel_multiplier=1).then_inc(pool_step, 1)
                pool.wait_ge(pool_step, 11)
                g_.affine_select(out=same[:, :], in_=same[:, :], compare_op=ALU.is_ge, fill=0.0, base=0,
                                 pattern=[[-DEC_SEQ, DEC_BATCH], [0, DEC_SEQ]], channel_multiplier=1).then_inc(pool_step, 1)
                g_.affine_select(out=own[:, :], in_=own[:, :], compare_op=ALU.is_ge, fill=0.0, base=DEC_SEQ - 1,
                                 pattern=[[DEC_SEQ, DEC_BATCH]], channel_multiplier=-1).then_inc(pool_step, 1)
                g_.affine_select(out=sh["new_count"][:, :, :, :], in_=new[:, :, :, :], compare_op=ALU.not_equal,
                                 fill=float(np.log(3.0)), base=0, pattern=[[DEC_SEQ, DEC_BATCH]] + win,
                                 channel_multiplier=-1).then_inc(pool_step, 1)

            @block.tensor
            def _(pe):
                for g in range(GROUPS):
                    pe.wait_ge(pages_loaded[g], 16)
                    for h in range(HEADS_A):
                        e = g * HEADS_A + h
                        last = nc.tensor.transpose(p_big[:, e * P:(e + 1) * P], pages[:, g, h::HEADS_A],
                                                   sh["ident"][:, :])
                last.then_inc(pe_step, 1)
                pe.wait_ge(act_step, 1)
                for m, out in ((sh["ones"], p_sum), (sh["tri"], p_big)):
                    for j in range(4):
                        last = nc.tensor.matmul(out[:, j * CH:(j + 1) * CH], m[:, :],
                                                by_pos[:, :, :, :].rearrange("p g h n -> p (g h n)")[:, j * CH:(j + 1) * CH],
                                                start=True, stop=True)
                    last.then_inc(pe_step, 1)
                pe.wait_ge(dve_step, 2)
                pe.wait_ge(pool_step, 13)
                nc.tensor.matmul(p_sum[:N_NEW, 0:HEADS_A], same[:, :], sh["logf"][:N_NEW, NPT, :],
                                 start=True, stop=True).then_inc(pe_step, 1)

            @block.scalar
            def _(act):
                act.wait_ge(pe_step, 1)
                nc.scalar.copy(by_pos[:, :, :, :].rearrange("p g h n -> p (g h n)"),
                               p_big[:, :]).then_inc(act_step, 1)
                act.wait_ge(clamped, 1)
                nc.scalar.activation(near[:, :], near[:, :], ACT.Ln).then_inc(act_step, 1)

            @block.vector
            def _(dve):
                steps = [0]

                def chained(ins):
                    steps[0] += 1
                    ins.then_inc(dve_step, 1)
                    dve.wait_ge(dve_step, steps[0])

                chained(nc.vector.memset(carry[:, :, :], 1.0))
                dve.wait_ge(pe_step, 2)
                chained(nc.vector.tensor_copy(totals[:, :, :].rearrange("p r n -> p (r n)"),
                                              p_sum[:, :]))
                chained(nc.vector.memset(carry[:, :, 0:1], 0.0))
                flat = lambda a: a[:, :, :].rearrange("p r n -> p (r n)")
                chained(nc.vector.tensor_tensor_scan(flat(sums), flat(carry), flat(totals), 0.0, ALU.mult, ALU.add))
                chained(nc.vector.tensor_tensor(totals[:, :, :], totals[:, :, :], sums[:, :, :], ALU.subtract))
                dve.wait_ge(pe_step, 3)
                view = "p (g h b) n -> p g h b n"
                tot_v = totals[:, :, :].rearrange(view, g=GROUPS, h=HEADS_A)
                sum_v = sums[:, :, :].rearrange(view, g=GROUPS, h=HEADS_A)
                in_v = p_big[:, :].rearrange("p (g h b n) -> p g h b n", g=GROUPS, h=HEADS_A, n=N_PAGES)
                for g in range(GROUPS):
                    for b in range(SEQS):
                        last = nc.vector.tensor_tensor(
                            sh["neg_c_past"][:, g * SEQS + b, :, :].rearrange("p n h -> p h n"),
                            tot_v[:, g, :, b, :], in_v[:, g, :, b, :], ALU.subtract)
                chained(last)
                dve.wait_ge(pool_step, 13)
                for g in range(GROUPS):
                    last = nc.vector.tensor_tensor(
                        past[:, :, g * SEQS:(g + 1) * SEQS], sum_v[:N_NEW, g, :, :, N_PAGES - 1],
                        own[:, None, g * SEQS:(g + 1) * SEQS].broadcast_to([N_NEW, HEADS_A, SEQS]), ALU.mult)
                chained(last)
                chained(nc.vector.tensor_reduce(past_sum[:, :], past[:, :, :], AX.X, ALU.add))
                dve.wait_ge(pe_step, 4)
                chained(nc.vector.scalar_tensor_tensor(out=neg_new[:, :], in0=p_sum[:N_NEW, 0:HEADS_A], scalar=-1.0,
                                                       in1=past_sum[:, :], op0=ALU.mult, op1=ALU.subtract))
                dve.wait_ge(pool_step, 14)
                for b in range(DEC_BATCH):
                    last = nc.vector.tensor_tensor(sh["new_bias_a"][:, b], sh["new_mask"][:, b],
                                                   neg_new[:, :, None].broadcast_to([N_NEW, HEADS_A, DEC_SEQ]), ALU.add)
                chained(last)
                chained(nc.vector.tensor_copy(dist[:, :], dist_i[:, :]))
                chained(nc.vector.tensor_scalar(count[:, :], dist[:, :], 128.0, None, ALU.is_le))
                flat = lambda a: a[:, :, :, :].rearrange("p r h j -> p (r h j)")
                for n, reach in ((3, 512.0), (15, 2048.0)):
                    chained(nc.vector.tensor_scalar(bits_i[:, :], dist_i[:, :], n, None, ALU.bitwise_and))
                    chained(nc.vector.tensor_scalar(term[:, :], bits_i[:, :], 0.0, None, ALU.is_equal))
                    chained(nc.vector.scalar_tensor_tensor(out=flat(near), in0=flat(dist), scalar=reach,
                                                           in1=flat(term), op0=ALU.is_le, op1=ALU.mult))
                    chained(nc.vector.tensor_tensor(count[:, :], count[:, :], near[:, :], ALU.add))
                chained(nc.vector.tensor_scalar(bits_i[:, :], res_i[:, :], 3, None, ALU.bitwise_and))
                chained(nc.vector.tensor_scalar(term[:, :], bits_i[:, :], 0.0, None, ALU.is_equal))
                chained(nc.vector.tensor_tensor(count[:, DENSE_ROWS:], count[:, DENSE_ROWS:], term[:, DENSE_ROWS:],
                                                ALU.mult))
                nc.vector.tensor_scalar(near[:, :], count[:, :], 1.0, None, ALU.max).then_inc(clamped, 1)
                chained(nc.vector.tensor_scalar(term[:, :], count[:, :], 0.0, NEG, ALU.is_equal, ALU.mult))
                dve.wait_ge(act_step, 2)
                chained(nc.vector.tensor_tensor(count[:, :], near[:, :], term[:, :], ALU.add))
                chained(nc.vector.tensor_copy(new_dist[:, :], new_dist_i[:, :]))
                for h in range(HEADS_B):
                    nc.vector.scalar_tensor_tensor(out=sh["win_bias"][:, :, h, :], in0=dist[:, :, h, :],
                                                   scalar=sh["neg_slope"][:, h:h + 1], in1=count[:, :, h, :],
                                                   op0=ALU.mult, op1=ALU.add)
                    last = nc.vector.scalar_tensor_tensor(out=sh["new_bias_b"][:, :, h, :], in0=new_dist[:, :, h, :],
                                                          scalar=sh["neg_slope"][:N_NEW, h:h + 1],
                                                          in1=sh["new_count"][:, :, h, :], op0=ALU.mult, op1=ALU.add)
                chained(last)


def sample_attention(nc, d, sh, kind):
    A = kind == "A"
    ROWS = N_PAGES // 2 if A else WIN_ROWS
    KEYSETS = N_PAGES if A else WIN_ROWS
    PAIRS = KV_A // 2 if A else HEADS_B // 2
    G = GROUP_A if A else 1
    QC = 2 * G * DEC_SEQ
    QN = PAIRS * QC
    KW = PAIRS * P
    col0 = 0 if A else CH
    TURNS = DEC_BATCH // 2
    with ExitStack() as ctx:
        n_ = "d" + kind.lower() + "_"
        sb = lambda n, s, t=F32: ctx.enter_context(nc.sbuf_tensor(n_ + n, s, t))
        pb = lambda n, s, t=F32: ctx.enter_context(nc.psum_tensor(n_ + n, s, t))
        sem = lambda n: nc.alloc_semaphore(n_ + n)
        KR = 4 if A else 2 * ROWS
        k_in = sb("k_in", [P, KR, CH])
        v_in = sb("v_in", [P, 2, ROWS, CH])
        k_t = sb("k_t", [P, 2, CH])
        table = sb("table", [1, DEC_BATCH * N_PAGES], I32)
        q_in = sb("q_in", [N_NEW, CH])
        k_new = sb("k_new", [N_NEW, KW])
        v_new = sb("v_new", [N_NEW, KW])
        k_new_t = sb("k_new_t", [P, PAIRS, N_NEW])
        q_blocks = sb("q_blocks", [P, DEC_BATCH, PAIRS, QC])
        logits = sb("logits", [P, 2, KEYSETS + 1, QN])
        probs = sb("probs", [P, 2, KEYSETS + 1, QN])
        part_max = sb("part_max", [P, 2, QN])
        all_max = sb("all_max", [P, 2, QN])
        part_sum = sb("part_sum", [P, 2, QN])
        all_sum = sb("all_sum", [P, 2, QN])
        recip = sb("recip", [P, 2, QN])
        out_t = sb("out_t", [P, PAIRS, G, DEC_BATCH, DEC_SEQ])
        mixed = sb("mixed", [N_NEW, CH])
        p_scores = pb("p_scores", [P, 2, 1024])
        p_turn = pb("p_turn", [P, 2, CH])
        p_side = pb("p_side", [P, 2, CH])

        setup_loaded, table_loaded = sem("setup_loaded"), sem("table_loaded")
        k_loaded = [sem(f"k_loaded{s}") for s in range(4 if A else 2)]
        v_loaded = [sem(f"v_loaded{s}") for s in range(2)]
        set_pe, set_dve = sem("set_pe"), sem("set_dve")
        turned = sem("turned")
        turn_act, turn_dve = sem("turn_act"), sem("turn_dve")
        scored = sem("scored")
        biased = sem("biased")
        maxed = sem("maxed")
        max_spread = sem("max_spread")
        shifted = sem("shifted")
        exped = sem("exped")
        summed = sem("summed")
        sum_spread = sem("sum_spread")
        weighed = sem("weighed")
        recip_ready = sem("recip_ready")
        out_ready = sem("out_ready")
        spare = sem("spare")
        stored = sem("stored")
        L = 16 * (4 if A else 4)

        def block_of(r, i):
            return (i % PAIRS, 2 * r + i // PAIRS) if A else (i, r)

        with nc.Block() as block:
            @block.sync
            def _(sp):
                if A:
                    sp.dma_start(table[:, :], d["page_table"].rearrange("(o b) j -> o (b j)", o=1)).then_inc(table_loaded, 16)
                sp.dma_start(q_in[:, :], d["q_scratch"][SEQ:TOK, col0:col0 + CH]).then_inc(setup_loaded, 16)
                sp.dma_start(k_new[:, :], d["fk_s" if A else "wk_s"]).then_inc(setup_loaded, 16)
                sp.dma_start(v_new[:, :], d["fv_s" if A else "wv_s"]).then_inc(setup_loaded, 16)
                if A:
                    sp.wait_ge(table_loaded, 16)
                with sp.Fori(0, TURNS) as i:
                    for b in range(2):
                        if A:
                            for r in range(ROWS):
                                n = b * ROWS + r
                                sp.wait_ge(turned, 2 * ROWS * i + n + 1)
                                sp.sem_inc(spare, 1)
                                if r == 0:
                                    sp.wait_ge(weighed, 2 * i + b + 1)
                                    sp.sem_inc(spare, 1)
                                for j in range(2):
                                    page = sp.value_load(table[0:1, ds(2 * N_PAGES * i + 2 * n + j, 1)],
                                                         min_val=0, max_val=d["cache_fox_k"].shape[1] - 1)
                                    for cache, dst, done in (("cache_fox_k", k_in[:, n % 4], k_loaded[n % 4]),
                                                             ("cache_fox_v", v_in[:, b, r], v_loaded[b])):
                                        src = d[cache][0].rearrange("n s h e -> n s (h e)")[ds(page, 1)]
                                        sp.dma_start(dst[:, j * KW:(j + 1) * KW],
                                                     src.rearrange("o s e -> (o s) e")).then_inc(done, 16)
                        else:
                            sp.wait_ge(scored, 2 * i + b + 1)
                            sp.sem_inc(spare, 1)
                            for cache, dst, done in (("cache_win_k", k_in[:, b * ROWS:(b + 1) * ROWS], k_loaded[b]),
                                                     ("cache_win_v", v_in[:, b], v_loaded[b])):
                                if cache == "cache_win_v":
                                    sp.wait_ge(weighed, 2 * i + b + 1)
                                sp.sem_inc(spare, 1)
                                src = d[cache][0].rearrange("b s h e -> b s (h e)")[ds(2 * i + b, 1)]\
                                    .rearrange("o s e -> (o s) e")
                                dense = src[WINDOW - DENSE_ROWS * P:WINDOW, :].rearrange("(c p) e -> p c e", p=P)
                                sp.dma_start(dst[:, 0:DENSE_ROWS], dense).then_inc(done, 16)
                                for c in range(DENSE_ROWS, ROWS):
                                    r0 = (c - DENSE_ROWS) * CH
                                    rows = src[r0:r0 + CH, :].rearrange("(m r) e -> m r e", r=16)[:, 0:DEC_SEQ, :]
                                    sp.dma_start(dst[:, c], rows).then_inc(done, 16)
                sp.wait_ge(set_dve, (4 + 2 * PAIRS * G))
                sp.dma_start(d["mix_scratch"][SEQ:TOK, col0:col0 + CH], mixed[:, :]).then_inc(stored, 16)
                sp.wait_ge(stored, 16)

            @block.gpsimd
            def _(pool):
                with pool.Fori(0, TURNS) as i:
                    def spread(ready, src, dst, op, done, b):
                        pool.wait_ge(ready, 2 * i + b + 1)
                        pool.sem_inc(spare, 1)
                        nc.gpsimd.partition_all_reduce(dst[:, b], src[:, b], P, op).then_inc(done, 1)

                    for b in range(2):
                        spread(maxed, part_max, all_max, RMAX, max_spread, b)
                        spread(summed, part_sum, all_sum, RADD, sum_spread, b)

            @block.tensor
            def _(pe):
                pe.sem_inc(turned, 4)
                pe.sem_inc(scored, 2)
                pe.sem_inc(weighed, 2)
                pe.wait_ge(setup_loaded, 48)
                for j in range(4):
                    nc.tensor.transpose(p_turn[:, 0, j * N_NEW:(j + 1) * N_NEW], q_in[:, j * P:(j + 1) * P],
                                        sh["ident"][:N_NEW, :N_NEW])
                for j in range(PAIRS):
                    last = nc.tensor.transpose(p_turn[:, 1, j * N_NEW:(j + 1) * N_NEW], k_new[:, j * P:(j + 1) * P],
                                               sh["ident"][:N_NEW, :N_NEW])
                last.then_inc(set_pe, 1)
                pe.wait_ge(set_dve, 3 + 2 * PAIRS * G)
                with pe.Fori(0, TURNS) as i:
                    def turn(n):
                        b, r = divmod(n, ROWS)
                        if A:
                            pe.wait_ge(k_loaded[n % 4], 32 * (2 * ROWS // 4 * i + n // 4 + 1))
                        elif r == 0:
                            pe.wait_ge(k_loaded[b], L * (i + 1))
                        pe.wait_ge(turn_act if n % 2 == 0 else turn_dve, ROWS * i + n // 2 + 1)
                        for j in range(4):
                            last = nc.tensor.transpose(p_turn[:, n % 2, j * P:(j + 1) * P],
                                                       k_in[:, n % KR, j * P:(j + 1) * P], sh["ident"][:, :])
                        last.then_inc(turned, 1)

                    def score(n):
                        b, r = divmod(n, ROWS)
                        pe.wait_ge(turn_act if n % 2 == 0 else turn_dve, ROWS * i + n // 2 + 2)
                        for j in range(4):
                            pair, keys = block_of(r, j)
                            c0 = keys * QN + pair * QC
                            nc.tensor.matmul(p_scores[:, b, c0:c0 + QC], k_t[:, n % 2, j * P:(j + 1) * P],
                                             q_blocks[:, ds(2 * i + b, 1), pair, :], start=True, stop=True)

                    for b in range(2):
                        pe.wait_ge(biased, 2 * i + b + 1)
                        turn(b * ROWS)
                        for r in range(ROWS):
                            if r + 1 < ROWS:
                                turn(b * ROWS + r + 1)
                            score(b * ROWS + r)
                        pe.wait_ge(out_ready, 2 * i + b + 1)
                        pe.sem_inc(spare, 1)
                        for pair in range(PAIRS):
                            last = nc.tensor.matmul(p_side[:N_NEW, b, pair * QC:(pair + 1) * QC],
                                                    k_new_t[:, pair, :], q_blocks[:, ds(2 * i + b, 1), pair, :],
                                                    start=True, stop=True)
                        last.then_inc(scored, 1)
                    for b in range(2):
                        pe.wait_ge(exped, 2 * i + b + 1)
                        pe.wait_ge(v_loaded[b], (16 * 2 * ROWS if A else L) * (i + 1))
                        for pair in range(PAIRS):
                            out = p_side[:, b, 64 + pair * QC:64 + (pair + 1) * QC]
                            for keys in range(KEYSETS):
                                r, c0 = (keys // 2, keys % 2 * KW + pair * P) if A else (keys, pair * P)
                                nc.tensor.matmul(out, v_in[:, b, r, c0:c0 + P],
                                                 probs[:, b, keys, pair * QC:(pair + 1) * QC],
                                                 start=(keys == 0), stop=False)
                            last = nc.tensor.matmul(out, v_new[:, pair * P:(pair + 1) * P],
                                                    probs[:N_NEW, b, KEYSETS, pair * QC:(pair + 1) * QC],
                                                    start=False, stop=True)
                        last.then_inc(weighed, 1)
                pe.wait_ge(out_ready, 2 + DEC_BATCH)
                for pair in range(PAIRS):
                    for g in range(G):
                        c0 = (pair * G + g) * P
                        last = nc.tensor.transpose(p_turn[:N_NEW, 0, c0:c0 + P],
                                                   out_t[:, pair, g].rearrange("p b t -> p (b t)"), sh["ident"][:, :])
                last.then_inc(set_pe, 1)

            @block.scalar
            def _(act):
                act.sem_inc(turn_act, 1)
                with act.Fori(0, TURNS) as i:
                    def evacuate(n):
                        act.wait_ge(turned, 4 + 2 * ROWS * i + n + 1)
                        nc.scalar.copy(k_t[:, n % 2, :], p_turn[:, n % 2, :]).then_inc(turn_act, 1)

                    def exp(b):
                        act.wait_ge(shifted, 2 * i + b + 1)
                        act.wait_ge(weighed, 2 * i + b + 1)
                        nc.scalar.activation(probs[:, b], logits[:, b], ACT.Exp).then_inc(exped, 1)

                    for n in range(2 * ROWS):
                        if n == ROWS + ROWS // 2 + 1:
                            exp(0)
                        if n % 2 == 0:
                            evacuate(n)
                    exp(1)

            @block.vector
            def _(dve):
                dve.sem_inc(turn_dve, 1)
                dve.sem_inc(biased, 2)
                dve.sem_inc(out_ready, 2)
                nc.vector.memset(q_blocks[:, :, :, :], 0.0).then_inc(set_dve, 1)
                nc.vector.memset(logits[:, :, KEYSETS, :], NEG).then_inc(set_dve, 1)
                dve.wait_ge(set_pe, 1)
                dve.wait_ge(set_dve, 2)
                copies = 0
                for kv in range(2 * PAIRS):
                    pair, kh = divmod(kv, 2)
                    for g in range(G):
                        tile, row = (kv, g * HEAD) if A else (pair, kh * HEAD)
                        src = p_turn[row:row + HEAD, 0, tile * N_NEW:(tile + 1) * N_NEW]\
                            .rearrange("p (b t) -> p b t", b=DEC_BATCH)
                        c0 = (kh * G + g) * DEC_SEQ
                        nc.vector.tensor_scalar(q_blocks[kh * HEAD:(kh + 1) * HEAD, :, pair, c0:c0 + DEC_SEQ], src,
                                                SCALE, None, ALU.mult).then_inc(set_dve, 1)
                        copies += 1
                nc.vector.tensor_copy(k_new_t[:, :, :].rearrange("p a n -> p (a n)"),
                                      p_turn[:, 1, 0:PAIRS * N_NEW]).then_inc(set_dve, 1)
                assert 3 + copies == 3 + 2 * PAIRS * G
                with dve.Fori(0, TURNS) as i:
                    def evacuate(n):
                        dve.wait_ge(turned, 4 + 2 * ROWS * i + n + 1)
                        nc.vector.tensor_copy(k_t[:, n % 2, :], p_turn[:, n % 2, :]).then_inc(turn_dve, 1)

                    def add_bias(b):
                        dve.wait_ge(scored, 2 + 2 * i + b + 1)
                        scores = p_scores[:, b, 0:KEYSETS * QN]
                        if A:
                            nc.vector.tensor_tensor(
                                logits[:, b, 0:KEYSETS, :].rearrange("p n (h t) -> p (n h) t", t=DEC_SEQ),
                                scores.rearrange("p (n t) -> p n t", t=DEC_SEQ),
                                sh["neg_c_past"][:, ds(2 * i + b, 1), :, :].rearrange("p o n h -> p (o n h)")[:, :, None]
                                .broadcast_to([P, KEYSETS * HEADS_A, DEC_SEQ]), ALU.add)
                        else:
                            nc.vector.tensor_tensor(
                                logits[:, b, 0:KEYSETS, :].rearrange("p n q -> p (n q)"), scores,
                                sh["win_bias"][:, :, :, :].rearrange("p n h t -> p (n h t)"), ALU.add)
                        new_bias = sh["new_bias_a" if A else "new_bias_b"]
                        nc.vector.tensor_tensor(logits[:N_NEW, b, KEYSETS, :], p_side[:N_NEW, b, 0:QN],
                                                new_bias[:, ds(2 * i + b, 1)].rearrange("p o h t -> p (o h t)"),
                                                ALU.add).then_inc(biased, 1)
                        dve.wait_ge(biased, 2 + 2 * i + b + 1)
                        nc.vector.tensor_reduce(part_max[:, b], logits[:, b].rearrange("p n q -> p q n"), AX.X, ALU.max)\
                            .then_inc(maxed, 1)

                    def shift(b):
                        dve.wait_ge(max_spread, 2 * i + b + 1)
                        nc.vector.tensor_tensor(logits[:, b], logits[:, b],
                                                all_max[:, b, None, :].broadcast_to([P, KEYSETS + 1, QN]),
                                                ALU.subtract).then_inc(shifted, 1)

                    def row_sums(b):
                        dve.wait_ge(exped, 2 * i + b + 1)
                        nc.vector.tensor_reduce(part_sum[:, b], probs[:, b].rearrange("p n q -> p q n"), AX.X, ALU.add)\
                            .then_inc(summed, 1)

                    def normalise(b):
                        dve.wait_ge(sum_spread, 2 * i + b + 1)
                        nc.vector.reciprocal(recip[:, b], all_sum[:, b]).then_inc(recip_ready, 1)
                        dve.wait_ge(recip_ready, 2 * i + b + 1)
                        dve.wait_ge(weighed, 2 + 2 * i + b + 1)
                        for kh in range(2):
                            part = slice(kh * HEAD, (kh + 1) * HEAD)
                            pick = lambda a: a.rearrange("p (a k g t) -> p a k g t", a=PAIRS, k=2, g=G)[:, :, kh]
                            last = nc.vector.tensor_tensor(
                                out_t[part, :, :, ds(2 * i + b, 1), :].rearrange("p a g o t -> p a (g o) t"),
                                pick(p_side[part, b, 64:64 + QN]), pick(recip[part, b, :]), ALU.mult)
                        last.then_inc(out_ready, 1)

                    for n in range(2 * ROWS):
                        if n == ROWS:
                            add_bias(0)
                        if n == ROWS + ROWS // 2:
                            shift(0)
                        if n % 2 == 1:
                            evacuate(n)
                    add_bias(1)
                    row_sums(0)
                    shift(1)
                    row_sums(1)
                    normalise(0)
                    normalise(1)
                dve.wait_ge(set_pe, 2)
                src = p_turn[:N_NEW, 0, :].rearrange("p (a g k e) -> p a g k e", a=PAIRS, g=G, k=2)
                dst = mixed[:, :].rearrange("p (a k g e) -> p a g k e", a=PAIRS, k=2, g=G)
                for a in range(PAIRS):
                    last = nc.vector.tensor_copy(dst[:, a], src[:, a])
                last.then_inc(set_dve, 1)


PIECE = TOK // 3
NP = TOK // PIECE
LAST_P = SEQ - (NP - 1) * PIECE
FT = D_FF // P
UT = 2 * FT
SLOTS = 4
ADDS = KT + 1
AHEAD = SLOTS - 1


def project_out(nc, d, sh):
    with ExitStack() as ctx:
        sb = lambda n, s, t=F32: ctx.enter_context(nc.sbuf_tensor("o_" + n, s, t))
        pb = lambda n, s, t=F32: ctx.enter_context(nc.psum_tensor("o_" + n, s, t))
        sem = lambda n: nc.alloc_semaphore("o_" + n)
        rows_in = sb("rows_in", [P, 2, D_MODEL])
        mix_hi = sb("mix_hi", [P, KT, TOK], F32R)
        mix_lo = sb("mix_lo", [P, KT, TOK], F32R)
        y = sb("y", [P, KT, NP, PIECE])
        w_raw = sb("w_raw", [P, SLOTS, KT, P])
        w_hi = sb("w_hi", [P, SLOTS, KT, P], F32R)
        w_lo = sb("w_lo", [P, SLOTS, KT, P], F32R)
        square = sb("square", [P, 2, PIECE])
        sum_sq = sb("sum_sq", [P, NP, PIECE])
        gains_in = sb("gains_in", [4 * KT, P])
        taps_in = sb("taps_in", [UT, 4, P])
        p_turn = pb("p_turn", [P, 2, D_MODEL])
        p_y = pb("p_y", [P, NP, CH])
        p_sum = pb("p_sum", [P, CH])
        x_t, gains, taps = sh["x_t"], sh["gains"], sh["taps"]

        rows_loaded = [sem("rows_loaded0"), sem("rows_loaded1")]
        consts_loaded = sem("consts_loaded")
        w_loaded = [sem(f"w_loaded{s}") for s in range(SLOTS)]
        turned, turn_hi, turn_read = sem("turned"), sem("turn_hi"), sem("turn_read")
        w_hi_ready = sem("w_hi_ready")
        w_lo_ready = sem("w_lo_ready")
        y_done = sem("y_done")
        y_read = sem("y_read")
        squared = sem("squared")
        added = sem("added")
        sum_done, rms_ready, rstd_ready = sem("sum_done"), sem("rms_ready"), sem("rstd_ready")
        gained, scaled = sem("gained"), sem("scaled")
        const_pe, const_act, eps_ready = sem("const_pe"), sem("const_act"), sem("eps_ready")

        with nc.Block() as block:
            @block.sync
            def _(sp):
                def load_rows(n):
                    t = n // 2
                    t0, rows = TILES[t]
                    if n >= 2:
                        sp.wait_ge(turned, n - 1)
                    sp.dma_start(rows_in[:rows, n % 2, :], d["mix_scratch"][t0:t0 + rows, :] if n % 2 == 0 else d["x"](t))\
                        .then_inc(rows_loaded[n % 2], 16)

                load_rows(0)
                load_rows(1)
                for j, name in enumerate(("g_attn_post", "g_ffn_pre", "g_ffn_post", "g_ple")):
                    sp.dma_start(gains_in[j * KT:(j + 1) * KT, :], d[name].rearrange("o (k p) -> (o k) p", p=P))\
                        .then_inc(consts_loaded, 16)
                sp.dma_start(taps_in[:, 0:3, :], d["conv_w"][0].rearrange("j (t p) -> t j p", p=P))\
                    .then_inc(consts_loaded, 16)
                sp.dma_start(taps_in[:, 3, :], d["conv_b"][0].rearrange("(t p) -> t p", p=P)).then_inc(consts_loaded, 16)

                def load_w(m):
                    if m >= SLOTS:
                        sp.wait_ge(w_lo_ready, m - SLOTS + 1)
                    sp.dma_start(w_raw[:, m % SLOTS],
                                 d["w_out"][0].rearrange("(k p) n -> p k n", p=P)[:, :, m * P:(m + 1) * P])\
                        .then_inc(w_loaded[m % SLOTS], 16)

                for n in range(2, 2 * NT):
                    load_rows(n)
                    if n < 2 + SLOTS:
                        load_w(n - 2)
                for m in range(SLOTS, KT):
                    load_w(m)

            @block.gpsimd
            def _(pool):
                nc.gpsimd.memset(sum_sq[:, :, :], 0.0).then_inc(added, 1)
                for n in range(NP * KT):
                    q = n % NP
                    pool.wait_ge(squared, n + 1)
                    pool.wait_ge(added, n + 1)
                    nc.gpsimd.tensor_tensor(sum_sq[:, q, :], sum_sq[:, q, :], square[:, n % 2, :], ALU.add)\
                        .then_inc(added, 1)

            @block.tensor
            def _(pe):
                for n in range(2 * NT):
                    t0, rows = TILES[n // 2]
                    pe.wait_ge(rows_loaded[n % 2], 16 * (n // 2 + 1))
                    if n >= 2:
                        pe.wait_ge(turn_read, n - 1)
                    for k in range(KT):
                        last = nc.tensor.transpose(p_turn[:, n % 2, k * P:k * P + rows],
                                                   rows_in[:rows, n % 2, k * P:(k + 1) * P], sh["ident"][:rows, :rows])
                    last.then_inc(turned, 1)
                pe.wait_ge(consts_loaded, 96)
                nc.tensor.transpose(p_sum[:, 0:4 * KT], gains_in[:, :], sh["ident"][:4 * KT, :4 * KT])
                for j in range(4):
                    last = nc.tensor.transpose(p_sum[:, 64 + j * UT:64 + (j + 1) * UT], taps_in[:, j, :],
                                               sh["ident"][:UT, :UT])
                last.then_inc(const_pe, 1)
                pe.wait_ge(turn_read, 2 * NT)
                for m in range(KT):
                    pe.wait_ge(w_lo_ready, m + 1)
                    for q in range(NP):
                        c0 = q * PIECE
                        if m > 0:
                            pe.wait_ge(y_read, NP * (m - 1) + q + 1)
                        for k in range(KT):
                            for part, (w, a) in enumerate(((w_hi, mix_hi), (w_hi, mix_lo), (w_lo, mix_hi))):
                                last = nc.tensor.matmul(p_y[:, q, 0:PIECE], w[:, m % SLOTS, k, :], a[:, k, c0:c0 + PIECE],
                                                        start=(k == 0 and part == 0), stop=(k == KT - 1 and part == 2))
                        last.then_inc(y_done, 1)
                pe.wait_ge(const_act, 1)
                for q in range(NP):
                    pe.wait_ge(added, 1 + NP * (KT - 1) + q + 1)
                    if q > 0:
                        pe.wait_ge(rms_ready, q)
                    nc.tensor.matmul(p_sum[:, 0:PIECE], sh["ones"][:, :], sum_sq[:, q, :],
                                     start=True, stop=True).then_inc(sum_done, 1)

            @block.scalar
            def _(act):
                def split_w(m):
                    act.wait_ge(w_loaded[m % SLOTS], 16 * (m // SLOTS + 1))
                    if m >= SLOTS:
                        act.wait_ge(y_done, NP * (m - SLOTS + 1))
                    nc.scalar.activation(w_hi[:, m % SLOTS], w_raw[:, m % SLOTS], ACT.Copy).then_inc(w_hi_ready, 1)

                for t in range(NT):
                    t0, rows = TILES[t]
                    act.wait_ge(turned, 2 * t + 1)
                    nc.scalar.activation(mix_hi[:, :, t0:t0 + rows],
                                         p_turn[:, 0, :].rearrange("p (k m) -> p k m", k=KT)[:, :, 0:rows],
                                         ACT.Copy).then_inc(turn_hi, 1)
                    act.wait_ge(turned, 2 * t + 2)
                    act.wait_ge(turn_read, 2 * t + 1)
                    nc.scalar.activation(x_t[:, :, t0:t0 + rows],
                                         p_turn[:, 1, :].rearrange("p (k m) -> p k m", k=KT)[:, :, 0:rows],
                                         ACT.Copy).then_inc(turn_read, 1)
                    if 2 <= t < 2 + SLOTS:
                        split_w(t - 2)
                act.wait_ge(const_pe, 1)
                nc.scalar.copy(gains[:, :, :].rearrange("p a k -> p (a k)"), p_sum[:, 0:4 * KT])
                nc.scalar.copy(taps[:, :, :].rearrange("p a k -> p (a k)"), p_sum[:, 64:64 + 4 * UT]).then_inc(const_act, 1)
                for m in range(KT):
                    for q in range(NP):
                        n = NP * m + q
                        act.wait_ge(y_done, n + 1)
                        if n >= 2:
                            act.wait_ge(added, n)
                        nc.scalar.activation(square[:, n % 2, :], p_y[:, q, 0:PIECE], ACT.Square).then_inc(squared, 1)
                        nc.scalar.activation(y[:, m, q, :], p_y[:, q, 0:PIECE], ACT.Copy).then_inc(y_read, 1)
                    if m + SLOTS < KT:
                        split_w(m + SLOTS)
                act.wait_ge(eps_ready, 1)
                for q in range(NP):
                    act.wait_ge(sum_done, q + 1)
                    nc.scalar.activation(sum_sq[:, q, :], p_sum[:, 0:PIECE], ACT.Sqrt, scale=1.0 / D_MODEL,
                                         bias=sh["eps"][:, :]).then_inc(rms_ready, 1)

            @block.vector
            def _(dve):
                nc.vector.memset(sh["eps"][:, :], EPS).then_inc(eps_ready, 1)

                def split_w(m):
                    dve.wait_ge(w_hi_ready, m + 1)
                    nc.vector.tensor_tensor(w_lo[:, m % SLOTS], w_raw[:, m % SLOTS], w_hi[:, m % SLOTS].bitcast(F32),
                                            ALU.subtract).then_inc(w_lo_ready, 1)

                for t in range(NT):
                    t0, rows = TILES[t]
                    dve.wait_ge(turn_hi, t + 1)
                    if t > 0:
                        dve.wait_ge(turn_read, 2 * t)
                    nc.vector.tensor_tensor(mix_lo[:, :, t0:t0 + rows],
                                            p_turn[:, 0, :].rearrange("p (k m) -> p k m", k=KT)[:, :, 0:rows],
                                            mix_hi[:, :, t0:t0 + rows].bitcast(F32), ALU.subtract).then_inc(turn_read, 1)
                    if 2 <= t < 2 + SLOTS:
                        split_w(t - 2)
                for m in range(SLOTS, KT):
                    split_w(m)
                dve.wait_ge(const_act, 1)
                for q in range(NP):
                    dve.wait_ge(rms_ready, q + 1)
                    nc.vector.reciprocal(sum_sq[:, q, :], sum_sq[:, q, :]).then_inc(rstd_ready, 1)
                    dve.wait_ge(rstd_ready, q + 1)
                    for k in range(KT):
                        nc.vector.scalar_tensor_tensor(out=y[:, k, q, :], in0=y[:, k, q, :], scalar=gains[:, 0, k:k + 1],
                                                       in1=sum_sq[:, q, :], op0=ALU.mult, op1=ALU.mult).then_inc(gained, 1)
                    for k in range(KT):
                        dve.wait_ge(gained, q * KT + k + 1)
                        ins = nc.vector.tensor_tensor(x_t[:, k, q * PIECE:(q + 1) * PIECE],
                                                      x_t[:, k, q * PIECE:(q + 1) * PIECE], y[:, k, q, :], ALU.add)
                    ins.then_inc(scaled, 1)


def conv_ffn(nc, d, sh):
    N_TILES = UT + 3 * KT
    BLOCKS = [(0, 8), (8, 8), (16, 6)]
    PRE = [0] + [2 * p - 1 for p in range(1, NP)]
    POST = [2 * p + 2 if p < NP - 1 else 2 * p + 1 for p in range(NP)]
    ROUNDS = 4
    QT = UT // ROUNDS
    STATE = 2 * DEC_BATCH
    with ExitStack() as ctx:
        sb = lambda n, s, t=F32: ctx.enter_context(nc.sbuf_tensor("f_" + n, s, t))
        pb = lambda n, s, t=F32: ctx.enter_context(nc.psum_tensor("f_" + n, s, t))
        sem = lambda n: nc.alloc_semaphore("f_" + n)
        xn_hi = sb("xn_hi", [P, KT, PIECE], F32R)
        xn_lo = sb("xn_lo", [P, KT, PIECE], F32R)
        xn = sb("xn", [P, 2, PIECE])
        h_hi = sb("h_hi", [P, FT, PIECE], F32R)
        h_lo = sb("h_lo", [P, FT, PIECE], F32R)
        w_raw = sb("w_raw", [P, SLOTS, KT, P])
        w_hi = sb("w_hi", [P, SLOTS, KT, P], F32R)
        w_lo = sb("w_lo", [P, SLOTS, KT, P], F32R)
        work = sb("work", [P, KT, 2 + PIECE])
        new_up = sb("new_up", [P, SLOTS, DEC_BATCH, 2 + DEC_SEQ])
        square = sb("square", [P, 2, PIECE])
        sum_sq = sb("sum_sq", [P, PIECE])
        rstd = sb("rstd", [P, PIECE])
        before = sb("before", [P, UT, 2 + STATE])
        rows_io = sb("rows_io", [2 + STATE, QT, P])
        p_up = pb("p_up", [P, SLOTS, CH])
        p_y = pb("p_y", [P, 2, CH])
        p_sum = pb("p_sum", [P, CH])
        p_turn = pb("p_turn", [P, CH])
        x_t, gains, taps = sh["x_t"], sh["gains"], sh["taps"]
        up = lambda j, c0, c1: work[:, j, c0:c1]
        conv = lambda j: work[:, SLOTS + j, 0:PIECE]

        w_loaded = [sem(f"w_loaded{s}") for s in range(SLOTS)]
        w_hi_ready = sem("w_hi_ready")
        w_lo_ready = sem("w_lo_ready")
        w_used = sem("w_used")
        up_read = sem("up_read")
        haloed = sem("haloed")
        carried = sem("carried")
        convolved = sem("convolved")
        tap_added = sem("tap_added")
        gelued, hid_ready, hid_hi = sem("gelued"), sem("hid_ready"), sem("hid_hi")
        hid_lo = sem("hid_lo")
        y_read = sem("y_read")
        squared, added = sem("squared"), sem("added")
        sum_done, rms_ready, rstd_ready = sem("sum_done"), sem("rms_ready"), sem("rstd_ready")
        xn_ready, xn_hi_ready, xn_lo_ready = sem("xn_ready"), sem("xn_hi_ready"), sem("xn_lo_ready")
        gained, residual = sem("gained"), sem("residual")
        rows_loaded, rows_stored, rows_out = sem("rows_loaded"), sem("rows_stored"), sem("rows_out")
        turned, turn_read, cleared = sem("turned"), sem("turn_read"), sem("cleared")
        spare = sem("spare")

        def wait_loaded(eng, p, base, per, i, j):
            n = N_TILES * p + base + j
            eng.wait_ge(w_loaded[j % SLOTS], 16 * (n // SLOTS + 1) + 16 * (per // SLOTS) * i)

        with nc.Block() as block:
            @block.sync
            def _(sp):
                w_up = d["w_up"][0].rearrange("(k p) n -> p k n", p=P)
                w_down = d["w_down"][0].rearrange("(k p) n -> p k n", p=P)
                for p in range(NP + 1):
                    with sp.Fori(0, FT // 2 if p < NP else 1) as i:
                        for j in range(SLOTS if p < NP else AHEAD):
                            s, half = divmod(j, 2)
                            sp.wait_ge(w_lo_ready, N_TILES * p + SLOTS * i + j + 1)
                            sp.sem_inc(spare, 1)
                            sp.dma_start(w_raw[:, j], w_up[:, :, ds((2 * i + s + half * FT) * P, P)])\
                                .then_inc(w_loaded[j], 16)
                    if p == NP:
                        break
                    with sp.Fori(0, KT // 4) as i:
                        for j in range(12):
                            m, b = divmod(j, 3)
                            f0, fn = BLOCKS[b]
                            sp.wait_ge(w_lo_ready, N_TILES * p + UT + 12 * i + j + 1)
                            sp.sem_inc(spare, 1)
                            sp.dma_start(w_raw[:, j % SLOTS, 0:fn], w_down[:, f0:f0 + fn, ds((4 * i + m) * P, P)])\
                                .then_inc(w_loaded[j % SLOTS], 16)
                for s in range(SLOTS):
                    sp.wait_ge(w_loaded[s], 16 * (NP * N_TILES // SLOTS + (s < AHEAD)))

            @block.gpsimd
            def _(pool):
                def load_state(r):
                    pool.dma_start(rows_io[:STATE], d["state_conv"][0].rearrange("b j (t p) -> (b j) t p", p=P)
                                   [:, r * QT:(r + 1) * QT]).then_inc(rows_loaded, 16)

                def next_state(r):
                    if r + 1 < ROUNDS:
                        pool.wait_ge(turned, r + 1)
                        load_state(r + 1)

                def clear_sum(q):
                    if q > 0:
                        pool.wait_ge(sum_done, q)
                    nc.gpsimd.memset(sum_sq[:, :], 0.0).then_inc(added, 1)

                def add_square(q, k, slot):
                    pool.wait_ge(squared, KT * q + k + 1)
                    pool.wait_ge(added, ADDS * q + k + 1)
                    nc.gpsimd.tensor_tensor(sum_sq[:, :], sum_sq[:, :], square[:, slot, :], ALU.add).then_inc(added, 1)

                def add_squares(q):
                    clear_sum(q)
                    for k in range(KT):
                        add_square(q, k, k % 2)

                pool.sem_inc(carried, 4)
                load_state(0)
                nc.gpsimd.memset(before[:, :, 0:2], 0.0).then_inc(cleared, 1)
                pool.wait_ge(cleared, 1)
                add_squares(PRE[0])
                for p in range(NP):
                    last_piece = p == NP - 1
                    if not last_piece:
                        add_squares(PRE[p + 1])
                    else:
                        pool.wait_ge(turn_read, ROUNDS)
                    if p > 0:
                        pool.wait_ge(residual, p)
                        pool.wait_ge(carried, 4 + UT * p)
                    with pool.Fori(0, FT // 2) as i:
                        for j in range(SLOTS):
                            s, half = divmod(j, 2)
                            u = UT * p + SLOTS * i + j
                            tile = 2 * i + s + half * FT
                            pool.wait_ge(convolved, u + 1)
                            pool.sem_inc(spare, 1)
                            ins = nc.gpsimd.tensor_copy(up(j, 0, 2), before[:, ds(tile, 1), 0:2].rearrange("p o c -> p (o c)"))
                            if last_piece:
                                ins = nc.gpsimd.tensor_copy(
                                    new_up[:, j, :, 0:2],
                                    before[:, ds(tile, 1), 2:].rearrange("p o (b c) -> p (o b) c", c=2))
                            ins.then_inc(haloed, 1)
                            pool.wait_ge(up_read, 4 + u + 1)
                            pool.wait_ge(haloed, u + 1)
                            pool.sem_inc(spare, 1)
                            last = LAST_P if last_piece else PIECE
                            ins = nc.gpsimd.tensor_copy(before[:, ds(tile, 1), 0:2].rearrange("p o c -> p (o c)"),
                                                        up(j, last, last + 2))
                            if last_piece:
                                ins = nc.gpsimd.tensor_copy(
                                    before[:, ds(tile, 1), 2:].rearrange("p o (b c) -> p (o b) c", c=2),
                                    new_up[:, j, :, DEC_SEQ:DEC_SEQ + 2])
                            ins.then_inc(carried, 1)
                    next_state(2 * p)
                    clear_sum(POST[p])
                    with pool.Fori(0, KT // 4) as i:
                        for m in range(4):
                            add_square(POST[p], 4 * i + m, m % 2)
                    next_state(2 * p + 1)
                for r in range(ROUNDS):
                    pool.wait_ge(rows_out, r + 1)
                    pool.dma_start(d["cv_p"][0, 0].rearrange("j (t p) -> j t p", p=P)[:, r * QT:(r + 1) * QT],
                                   rows_io[0:2]).then_inc(rows_stored, 16)
                    pool.dma_start(d["cv_s"][0].rearrange("b j (t p) -> (b j) t p", p=P)[:, r * QT:(r + 1) * QT],
                                   rows_io[2:2 + STATE]).then_inc(rows_stored, 16)
                pool.wait_ge(rows_stored, 32 * ROUNDS)

            @block.tensor
            def _(pe):
                pe.sem_inc(w_used, 4)

                def turn_state(r):
                    if r < ROUNDS:
                        pe.wait_ge(rows_loaded, 16 * (r + 1))
                        if r > 0:
                            pe.wait_ge(turn_read, r)
                        for t in range(QT):
                            last = nc.tensor.transpose(p_turn[:, t * STATE:(t + 1) * STATE], rows_io[:STATE, t, :],
                                                       sh["ident"][:STATE, :STATE])
                        last.then_inc(turned, 1)

                def sum_squares(q):
                    pe.wait_ge(added, ADDS * (q + 1))
                    if q > 0:
                        pe.wait_ge(rms_ready, q)
                    nc.tensor.matmul(p_sum[:, 0:PIECE], sh["ones"][:, :], sum_sq[:, :], start=True, stop=True)\
                        .then_inc(sum_done, 1)

                sum_squares(PRE[0])
                for p in range(NP):
                    pe.wait_ge(xn_lo_ready, KT * (p + 1))
                    with pe.Fori(0, FT // 2) as i:
                        for j in range(SLOTS):
                            pe.wait_ge(w_lo_ready, 4 + N_TILES * p + SLOTS * i + j + 1)
                            pe.wait_ge(up_read, UT * p + SLOTS * i + j + 1)
                            for k in range(KT):
                                for part, (w, a) in enumerate(((w_hi, xn_hi), (w_hi, xn_lo), (w_lo, xn_hi))):
                                    last = nc.tensor.matmul(p_up[:, j, 0:PIECE], w[:, j, k, :], a[:, k, :],
                                                            start=(k == 0 and part == 0), stop=(k == KT - 1 and part == 2))
                            last.then_inc(w_used, 1)
                    turn_state(2 * p)
                    if p < NP - 1:
                        sum_squares(PRE[p + 1])
                    with pe.Fori(0, KT // 4) as i:
                        for j in range(12):
                            m, b = divmod(j, 3)
                            f0, fn = BLOCKS[b]
                            pe.wait_ge(w_lo_ready, 4 + N_TILES * p + UT + 12 * i + j + 1)
                            if j < 3:
                                pe.wait_ge(hid_lo, 2 + FT * p + f0 + fn)
                            if b == 0:
                                pe.wait_ge(y_read, KT * p + 4 * i + m + 1)
                            for f in range(fn):
                                for part, (w, a) in enumerate(((w_hi, h_hi), (w_hi, h_lo), (w_lo, h_hi))):
                                    last = nc.tensor.matmul(
                                        p_y[:, m % 2, 0:PIECE], w[:, j % SLOTS, f, :], a[:, f0 + f, :],
                                        start=(b == 0 and f == 0 and part == 0), stop=(b == 2 and f == fn - 1 and part == 2))
                            last.then_inc(w_used, 1)
                    turn_state(2 * p + 1)
                    sum_squares(POST[p])
                pe.wait_ge(carried, 4 + NP * UT)
                for r in range(ROUNDS):
                    if r > 0:
                        pe.wait_ge(rows_out, r)
                    for t in range(QT):
                        last = nc.tensor.transpose(p_up[:2 + STATE, t // 4, t % 4 * P:(t % 4 + 1) * P],
                                                   before[:, r * QT + t, :], sh["ident"][:, :])
                    last.then_inc(turned, 1)

            @block.scalar
            def _(act):
                def split_w(p, base, per, i, j):
                    wait_loaded(act, p, base, per, i, j)
                    act.wait_ge(w_used, N_TILES * p + base + per * i + j + 1)
                    nc.scalar.activation(w_hi[:, j % SLOTS], w_raw[:, j % SLOTS], ACT.Copy).then_inc(w_hi_ready, 1)

                def state_read(r):
                    if r < ROUNDS:
                        act.wait_ge(turned, r + 1)
                        nc.scalar.activation(before[:, r * QT:(r + 1) * QT, 2:],
                                             p_turn[:, 0:QT * STATE].rearrange("p (t c) -> p t c", t=QT),
                                             ACT.Copy).then_inc(turn_read, 1)

                def squares(p, q):
                    for k in range(KT):
                        n = ADDS * q + k
                        if n > 0:
                            act.wait_ge(added, n)
                        nc.scalar.activation(square[:, k % 2, :], x_t[:, k, p * PIECE:(p + 1) * PIECE],
                                             ACT.Square).then_inc(squared, 1)

                def root(q):
                    act.wait_ge(sum_done, q + 1)
                    nc.scalar.activation(rstd[:, :], p_sum[:, 0:PIECE], ACT.Sqrt, scale=1.0 / D_MODEL,
                                         bias=sh["eps"][:, :]).then_inc(rms_ready, 1)

                def normed_hi(p):
                    for k in range(KT):
                        act.wait_ge(xn_ready, KT * p + k + 1)
                        nc.scalar.activation(xn_hi[:, k, :], xn[:, k % 2, :], ACT.Copy).then_inc(xn_hi_ready, 1)

                act.sem_inc(up_read, 4)
                act.sem_inc(y_read, 2)
                squares(0, PRE[0])
                for j in range(AHEAD):
                    split_w(0, 0, SLOTS, 0, j)
                root(PRE[0])
                normed_hi(0)
                for p in range(NP):
                    last_piece = p == NP - 1
                    if not last_piece:
                        squares(p + 1, PRE[p + 1])
                    if p > 0:
                        act.wait_ge(residual, p)
                    with act.Fori(0, FT // 2) as i:
                        def read_up(j):
                            s, half = divmod(j, 2)
                            n, u = N_TILES * p + SLOTS * i + j, UT * p + SLOTS * i + j
                            tile = 2 * i + s + half * FT
                            split_w(p, 0, SLOTS, i, j + AHEAD)
                            act.wait_ge(w_used, 4 + n + 1)
                            act.wait_ge(convolved, u + 1)
                            act.wait_ge(carried, u + 1)
                            act.wait_ge(hid_lo, FT * p + 2 * i + s + 1)
                            if last_piece:
                                nc.scalar.activation(up(j, 2, 2 + LAST_P), p_up[:, j, 0:LAST_P], ACT.Copy)
                                nc.scalar.activation(new_up[:, j, :, 2:],
                                                     p_up[:, j, LAST_P:PIECE].rearrange("p (b t) -> p b t", b=DEC_BATCH),
                                                     ACT.Copy)
                            else:
                                nc.scalar.activation(up(j, 2, 2 + PIECE), p_up[:, j, 0:PIECE], ACT.Copy)
                            nc.scalar.activation(conv(j), p_up[:, j, 0:PIECE], ACT.Identity,
                                                 scale=taps[:, 2, ds(tile, 1)], bias=taps[:, 3, ds(tile, 1)])\
                                .then_inc(up_read, 1)

                        def gelu(s):
                            act.wait_ge(convolved, 4 + UT * p + SLOTS * i + 2 * s + 1)
                            nc.scalar.activation(conv(2 * s), conv(2 * s), ACT.Gelu_apprx_tanh).then_inc(gelued, 1)

                        def hidden_hi(s):
                            act.wait_ge(hid_ready, FT * p + 2 * i + s + 1)
                            nc.scalar.activation(h_hi[:, ds(2 * i + s, 1), :].rearrange("p o c -> p (o c)"),
                                                 conv(2 * s + 1), ACT.Copy).then_inc(hid_hi, 1)

                        read_up(0)
                        read_up(1)
                        read_up(2)
                        gelu(0)
                        read_up(3)
                        hidden_hi(0)
                        gelu(1)
                        hidden_hi(1)
                    state_read(2 * p)
                    if not last_piece:
                        root(PRE[p + 1])
                        normed_hi(p + 1)
                    act.wait_ge(carried, 4 + UT * (p + 1))
                    with act.Fori(0, KT // 4) as i:
                        for j in range(12):
                            m, b = divmod(j, 3)
                            split_w(p, UT, 12, i, j + AHEAD)
                            if b == 2:
                                act.wait_ge(w_used, 4 + N_TILES * p + UT + 12 * i + j + 1)
                                act.wait_ge(added, ADDS * POST[p] + 4 * i + m)
                                nc.scalar.activation(square[:, m % 2, :], p_y[:, m % 2, 0:PIECE], ACT.Square)\
                                    .then_inc(squared, 1)
                                nc.scalar.activation(work[:, ds(4 * i + m, 1), 0:PIECE].rearrange("p o c -> p (o c)"),
                                                     p_y[:, m % 2, 0:PIECE], ACT.Copy).then_inc(y_read, 1)
                    state_read(2 * p + 1)
                    root(POST[p])
                for r in range(ROUNDS):
                    act.wait_ge(turned, ROUNDS + r + 1)
                    if r > 0:
                        act.wait_ge(rows_stored, 32 * r)
                    nc.scalar.activation(rows_io[:, :, :], p_up[:2 + STATE, 0:3, :].rearrange("p a (t c) -> p (a t) c", c=P)
                                         [:, 0:QT, :], ACT.Copy).then_inc(rows_out, 1)

            @block.vector
            def _(dve):
                def split_w(p, base, per, i, j):
                    dve.wait_ge(w_hi_ready, N_TILES * p + base + per * i + j + 1)
                    nc.vector.tensor_tensor(w_lo[:, j % SLOTS], w_raw[:, j % SLOTS], w_hi[:, j % SLOTS].bitcast(F32),
                                            ALU.subtract).then_inc(w_lo_ready, 1)

                def invert(q):
                    dve.wait_ge(rms_ready, q + 1)
                    nc.vector.reciprocal(rstd[:, :], rstd[:, :]).then_inc(rstd_ready, 1)
                    dve.wait_ge(rstd_ready, q + 1)

                def normalise(p):
                    def low(k):
                        dve.wait_ge(xn_hi_ready, KT * p + k + 1)
                        nc.vector.tensor_tensor(xn_lo[:, k, :], xn[:, k % 2, :], xn_hi[:, k, :].bitcast(F32),
                                                ALU.subtract).then_inc(xn_lo_ready, 1)

                    for k in range(KT):
                        if k >= 2:
                            dve.wait_ge(xn_lo_ready, KT * p + k - 1)
                        nc.vector.scalar_tensor_tensor(out=xn[:, k % 2, :], in0=x_t[:, k, p * PIECE:(p + 1) * PIECE],
                                                       scalar=gains[:, 1, k:k + 1], in1=rstd[:, :],
                                                       op0=ALU.mult, op1=ALU.mult).then_inc(xn_ready, 1)
                        if k >= 1:
                            low(k - 1)
                    low(KT - 1)

                dve.sem_inc(w_lo_ready, 4)
                dve.sem_inc(convolved, 4)
                dve.sem_inc(hid_lo, 2)
                for j in range(AHEAD):
                    split_w(0, 0, SLOTS, 0, j)
                invert(PRE[0])
                normalise(0)
                for p in range(NP):
                    last_piece = p == NP - 1
                    with dve.Fori(0, FT // 2) as i:
                        def add_tap(j, tap, done):
                            s, half = divmod(j, 2)
                            tile = 2 * i + s + half * FT
                            rows = LAST_P if last_piece else PIECE
                            ins = nc.vector.scalar_tensor_tensor(
                                out=conv(j)[:, 0:rows], in0=up(j, tap, tap + rows), scalar=taps[:, tap, ds(tile, 1)],
                                in1=conv(j)[:, 0:rows], op0=ALU.mult, op1=ALU.add)
                            if last_piece:
                                new = conv(j)[:, rows:PIECE].rearrange("p (b t) -> p b t", b=DEC_BATCH)
                                ins = nc.vector.scalar_tensor_tensor(
                                    out=new, in0=new_up[:, j, :, tap:tap + DEC_SEQ], scalar=taps[:, tap, ds(tile, 1)],
                                    in1=new, op0=ALU.mult, op1=ALU.add)
                            ins.then_inc(done, 1)

                        def convolve(j):
                            u = UT * p + SLOTS * i + j
                            split_w(p, 0, SLOTS, i, j + AHEAD)
                            dve.wait_ge(haloed, u + 1)
                            dve.wait_ge(up_read, 4 + u + 1)
                            add_tap(j, 1, tap_added)
                            dve.wait_ge(tap_added, u + 1)
                            add_tap(j, 0, convolved)

                        def gate(s):
                            h = FT * p + 2 * i + s
                            dve.wait_ge(gelued, h + 1)
                            dve.wait_ge(convolved, 4 + UT * p + SLOTS * i + 2 * s + 2)
                            nc.vector.tensor_tensor(conv(2 * s + 1), conv(2 * s), conv(2 * s + 1), ALU.mult)\
                                .then_inc(hid_ready, 1)

                        def hidden_lo(s):
                            dve.wait_ge(hid_hi, FT * p + 2 * i + s + 1)
                            nc.vector.tensor_tensor(h_lo[:, ds(2 * i + s, 1), :].rearrange("p o c -> p (o c)"),
                                                    conv(2 * s + 1),
                                                    h_hi[:, ds(2 * i + s, 1), :].rearrange("p o c -> p (o c)").bitcast(F32),
                                                    ALU.subtract).then_inc(hid_lo, 1)

                        convolve(0)
                        convolve(1)
                        convolve(2)
                        gate(0)
                        convolve(3)
                        hidden_lo(0)
                        gate(1)
                        hidden_lo(1)
                    if not last_piece:
                        invert(PRE[p + 1])
                        normalise(p + 1)
                    with dve.Fori(0, KT // 4) as i:
                        for j in range(12):
                            split_w(p, UT, 12, i, j + AHEAD)
                    invert(POST[p])
                    for k in range(KT):
                        if k == 0:
                            dve.wait_ge(y_read, 2 + KT * (p + 1))
                        nc.vector.scalar_tensor_tensor(out=work[:, k, 0:PIECE], in0=work[:, k, 0:PIECE],
                                                       scalar=gains[:, 2, k:k + 1], in1=rstd[:, :],
                                                       op0=ALU.mult, op1=ALU.mult).then_inc(gained, 1)
                    for k in range(KT):
                        dve.wait_ge(gained, KT * p + k + 1)
                        ins = nc.vector.tensor_tensor(x_t[:, k, p * PIECE:(p + 1) * PIECE],
                                                      x_t[:, k, p * PIECE:(p + 1) * PIECE], work[:, k, 0:PIECE], ALU.add)
                    ins.then_inc(residual, 1)


def embed_and_store(nc, d, sh):
    IT = PLE // P
    with ExitStack() as ctx:
        sb = lambda n, s, t=F32: ctx.enter_context(nc.sbuf_tensor("g_" + n, s, t))
        pb = lambda n, s, t=F32: ctx.enter_context(nc.psum_tensor("g_" + n, s, t))
        sem = lambda n: nc.alloc_semaphore("g_" + n)
        xn_hi = sb("xn_hi", [P, KT, TOK], F32R)
        xn_lo = sb("xn_lo", [P, KT, TOK], F32R)
        e_hi = sb("e_hi", [P, IT, TOK], F32R)
        e_lo = sb("e_lo", [P, IT, TOK], F32R)
        xn = sb("xn", [P, 2, PIECE])
        w_raw = sb("w_raw", [P, SLOTS, KT + IT, P])
        w_hi = sb("w_hi", [P, SLOTS, KT + IT, P], F32R)
        w_lo = sb("w_lo", [P, SLOTS, KT + IT, P], F32R)
        square = sb("square", [P, 2, PIECE])
        sum_sq = sb("sum_sq", [P, NP, PIECE])
        gate = sb("gate", [P, 2, PIECE])
        rows_io = sb("rows_io", [P, 2, D_MODEL])
        p_gate = pb("p_gate", [P, NP, CH])
        p_emb = pb("p_emb", [P, NP, CH])
        p_sum = pb("p_sum", [P, CH])
        x_t, gains = sh["x_t"], sh["gains"]

        e_loaded = [sem("e_loaded0"), sem("e_loaded1")]
        w_loaded = [sem(f"w_loaded{s}") for s in range(SLOTS)]
        e_turned, e_hi_ready, e_lo_ready = sem("e_turned"), sem("e_hi_ready"), sem("e_lo_ready")
        w_hi_ready, w_lo_ready = sem("w_hi_ready"), sem("w_lo_ready")
        squared, added = sem("squared"), sem("added")
        sum_done, rms_ready, rstd_ready = sem("sum_done"), sem("rms_ready"), sem("rstd_ready")
        xn_ready, xn_hi_ready, xn_lo_ready = sem("xn_ready"), sem("xn_hi_ready"), sem("xn_lo_ready")
        products, gated, embedded, residual = sem("products"), sem("gated"), sem("embedded"), sem("residual")
        turned, out_act, out_dve = sem("turned"), sem("out_act"), sem("out_dve")
        stored = [sem("stored0"), sem("stored1")]

        def piece(a, k, q):
            return a[:, k, q * PIECE:(q + 1) * PIECE]

        with nc.Block() as block:
            @block.sync
            def _(sp):
                def load_e(t):
                    t0, rows = TILES[t]
                    src = d["p_prompt"][0, 0][t0:t0 + rows, :] if t < NPT else d["p_sample"][0].rearrange("b s e -> (b s) e")
                    if t >= 2:
                        sp.wait_ge(e_turned, t - 1)
                    sp.dma_start(rows_io[:rows, t % 2, 0:PLE], src).then_inc(e_loaded[t % 2], 16)

                def load_w(m):
                    if m >= SLOTS:
                        sp.wait_ge(w_lo_ready, m - SLOTS + 1)
                    for k0, kn, name in ((0, KT, "w_ple_gate"), (KT, IT, "w_ple")):
                        sp.dma_start(w_raw[:, m % SLOTS, k0:k0 + kn],
                                     d[name][0].rearrange("(k p) n -> p k n", p=P)[:, :, m * P:(m + 1) * P])\
                            .then_inc(w_loaded[m % SLOTS], 16)

                load_e(0)
                load_e(1)
                for m in range(SLOTS):
                    load_w(m)
                for t in range(2, NT):
                    load_e(t)
                for m in range(SLOTS, KT):
                    load_w(m)
                for t in range(NT):
                    t0, rows = TILES[t]
                    sp.wait_ge(out_act, t + 1)
                    sp.wait_ge(out_dve, t + 1)
                    sp.dma_start(d["y_p"][t0:t0 + rows, :] if t < NPT else d["y_s"], rows_io[:rows, t % 2, :])\
                        .then_inc(stored[t % 2], 16)
                for s in range(2):
                    sp.wait_ge(stored[s], 16 * len(range(s, NT, 2)))

            @block.gpsimd
            def _(pool):
                nc.gpsimd.memset(sum_sq[:, :, :], 0.0).then_inc(added, 1)
                for n in range(NP * KT):
                    pool.wait_ge(squared, n + 1)
                    pool.wait_ge(added, n + 1)
                    nc.gpsimd.tensor_tensor(sum_sq[:, n // KT, :], sum_sq[:, n // KT, :], square[:, n % 2, :], ALU.add)\
                        .then_inc(added, 1)

            @block.tensor
            def _(pe):
                for t in range(NT):
                    t0, rows = TILES[t]
                    pe.wait_ge(e_loaded[t % 2], 16 * (t // 2 + 1))
                    if t >= NP:
                        pe.wait_ge(e_lo_ready, t - NP + 1)
                    for k in range(IT):
                        last = nc.tensor.transpose(p_gate[:, t % NP, k * P:k * P + rows],
                                                   rows_io[:rows, t % 2, k * P:(k + 1) * P], sh["ident"][:rows, :rows])
                    last.then_inc(e_turned, 1)
                for q in range(NP):
                    pe.wait_ge(added, 1 + KT * (q + 1))
                    if q > 0:
                        pe.wait_ge(rms_ready, q)
                    nc.tensor.matmul(p_sum[:, 0:PIECE], sh["ones"][:, :], sum_sq[:, q, :], start=True, stop=True)\
                        .then_inc(sum_done, 1)
                pe.wait_ge(e_lo_ready, NT)
                for m in range(KT):
                    pe.wait_ge(w_lo_ready, m + 1)
                    for q in range(NP):
                        if m == 0:
                            pe.wait_ge(xn_lo_ready, KT * (q + 1))
                        else:
                            pe.wait_ge(embedded, NP * (m - 1) + q + 1)
                        for out, w0, kn, hi, lo in ((p_gate, 0, KT, xn_hi, xn_lo), (p_emb, KT, IT, e_hi, e_lo)):
                            for k in range(kn):
                                for part, (w, a) in enumerate(((w_hi, hi), (w_hi, lo), (w_lo, hi))):
                                    last = nc.tensor.matmul(out[:, q, 0:PIECE], w[:, m % SLOTS, w0 + k, :], piece(a, k, q),
                                                            start=(k == 0 and part == 0), stop=(k == kn - 1 and part == 2))
                        last.then_inc(products, 1)
                pe.wait_ge(residual, NP * KT)
                for t in range(NT):
                    t0, rows = TILES[t]
                    bank = p_gate if t % 2 == 0 else p_emb
                    if t >= 2:
                        pe.wait_ge(out_act, t - 1)
                        pe.wait_ge(out_dve, t - 1)
                    for k in range(KT):
                        last = nc.tensor.transpose(bank[:rows, k // 4, k % 4 * P:(k % 4 + 1) * P],
                                                   x_t[:, k, t0:t0 + rows], sh["ident"][:, :])
                    last.then_inc(turned, 1)

            @block.scalar
            def _(act):
                def split_w(m):
                    act.wait_ge(w_loaded[m % SLOTS], 32 * (m // SLOTS + 1))
                    if m >= SLOTS:
                        act.wait_ge(products, NP * (m - SLOTS + 1))
                    nc.scalar.activation(w_hi[:, m % SLOTS], w_raw[:, m % SLOTS], ACT.Copy).then_inc(w_hi_ready, 1)

                def e_split(t):
                    t0, rows = TILES[t]
                    act.wait_ge(e_turned, t + 1)
                    nc.scalar.activation(e_hi[:, :, t0:t0 + rows],
                                         p_gate[:, t % NP, 0:PLE].rearrange("p (k m) -> p k m", k=IT)[:, :, 0:rows],
                                         ACT.Copy).then_inc(e_hi_ready, 1)

                for n in range(NP * KT):
                    if n >= 2:
                        act.wait_ge(added, n)
                    nc.scalar.activation(square[:, n % 2, :], piece(x_t, n % KT, n // KT), ACT.Square).then_inc(squared, 1)
                for t in range(NT):
                    e_split(t)
                for q in range(NP):
                    act.wait_ge(sum_done, q + 1)
                    nc.scalar.activation(sum_sq[:, q, :], p_sum[:, 0:PIECE], ACT.Sqrt, scale=1.0 / D_MODEL,
                                         bias=sh["eps"][:, :]).then_inc(rms_ready, 1)
                for m in range(SLOTS):
                    split_w(m)
                for n in range(NP * KT):
                    act.wait_ge(xn_ready, n + 1)
                    nc.scalar.activation(piece(xn_hi, n % KT, n // KT), xn[:, n % 2, :], ACT.Copy).then_inc(xn_hi_ready, 1)
                for m in range(KT):
                    for q in range(NP):
                        n = NP * m + q
                        act.wait_ge(products, n + 1)
                        if n >= 2:
                            act.wait_ge(residual, n - 1)
                        nc.scalar.activation(gate[:, n % 2, :], p_gate[:, q, 0:PIECE], ACT.Sigmoid).then_inc(gated, 1)
                    if m + SLOTS < KT:
                        split_w(m + SLOTS)
                for t in range(NT):
                    rows = TILES[t][1]
                    bank = p_gate if t % 2 == 0 else p_emb
                    act.wait_ge(turned, t + 1)
                    if t >= 2:
                        act.wait_ge(stored[t % 2], 16 * (t // 2))
                    nc.scalar.copy(rows_io[:rows, t % 2, 0:CH], bank[:rows, 0, :]).then_inc(out_act, 1)

            @block.vector
            def _(dve):
                def split_w(m):
                    dve.wait_ge(w_hi_ready, m + 1)
                    nc.vector.tensor_tensor(w_lo[:, m % SLOTS], w_raw[:, m % SLOTS], w_hi[:, m % SLOTS].bitcast(F32),
                                            ALU.subtract).then_inc(w_lo_ready, 1)

                for t in range(NT):
                    t0, rows = TILES[t]
                    dve.wait_ge(e_hi_ready, t + 1)
                    nc.vector.tensor_tensor(e_lo[:, :, t0:t0 + rows],
                                            p_gate[:, t % NP, 0:PLE].rearrange("p (k m) -> p k m", k=IT)[:, :, 0:rows],
                                            e_hi[:, :, t0:t0 + rows].bitcast(F32), ALU.subtract).then_inc(e_lo_ready, 1)

                def low(n):
                    dve.wait_ge(xn_hi_ready, n + 1)
                    nc.vector.tensor_tensor(piece(xn_lo, n % KT, n // KT), xn[:, n % 2, :],
                                            piece(xn_hi, n % KT, n // KT).bitcast(F32), ALU.subtract).then_inc(xn_lo_ready, 1)

                for n in range(NP * KT):
                    q, k = divmod(n, KT)
                    if k == 0:
                        dve.wait_ge(rms_ready, q + 1)
                        nc.vector.reciprocal(sum_sq[:, q, :], sum_sq[:, q, :]).then_inc(rstd_ready, 1)
                        dve.wait_ge(rstd_ready, q + 1)
                    if n == 2:
                        for m in range(SLOTS):
                            split_w(m)
                    if n >= 2:
                        dve.wait_ge(xn_lo_ready, n - 1)
                    nc.vector.scalar_tensor_tensor(out=xn[:, n % 2, :], in0=piece(x_t, k, q), scalar=gains[:, 3, k:k + 1],
                                                   in1=sum_sq[:, q, :], op0=ALU.mult, op1=ALU.mult).then_inc(xn_ready, 1)
                    if n >= 1:
                        low(n - 1)
                low(NP * KT - 1)
                for m in range(KT):
                    for q in range(NP):
                        n = NP * m + q
                        dve.wait_ge(gated, n + 1)
                        nc.vector.tensor_tensor(gate[:, n % 2, :], gate[:, n % 2, :], p_emb[:, q, 0:PIECE], ALU.mult)\
                            .then_inc(embedded, 1)
                        dve.wait_ge(embedded, n + 1)
                        nc.vector.tensor_tensor(piece(x_t, m, q), piece(x_t, m, q), gate[:, n % 2, :], ALU.add)\
                            .then_inc(residual, 1)
                    if m + SLOTS < KT:
                        split_w(m + SLOTS)
                for t in range(NT):
                    rows = TILES[t][1]
                    bank = p_gate if t % 2 == 0 else p_emb
                    dve.wait_ge(turned, t + 1)
                    if t >= 2:
                        dve.wait_ge(stored[t % 2], 16 * (t // 2))
                    nc.vector.tensor_copy(rows_io[:rows, t % 2, CH:2 * CH], bank[:rows, 1, :]).then_inc(out_dve, 1)


def hymba_step(nc, d, stages=9):
    with ExitStack() as ctx:
        def tensors(stack, shapes):
            return {n: stack.enter_context(nc.sbuf_tensor(n, s, (t or [F32])[0])) for n, (s, *t) in shapes.items()}

        sh = tensors(ctx, {"ident": ([P, P],), "ones": ([P, P],), "logf": ([P, NT, HEADS_A],)})
        with nc.cleanup_on_exit():
            norm_and_project(nc, d, sh)
            with ExitStack() as attention:
                sh |= tensors(attention, {
                    "tri": ([P, P],), "ident_bf": ([P, P], BF16), "mask_bf": ([P, P], BF16),
                    "neg_slope": ([P, HEADS_B],)})
                with ExitStack() as prompt:
                    sh |= tensors(prompt, {"dist": ([P, SEQ],), "log_count": ([P, SEQ],), "neg_c": ([P, HEADS_A, NPT],)})
                    if stages >= 2:
                        build_tables(nc, d, sh)
                        prompt_attention(nc, d, sh, "A")
                        prompt_attention(nc, d, sh, "B")
                with ExitStack() as sample:
                    rows = [N_NEW, DEC_BATCH, HEADS_A, DEC_SEQ]
                    sh |= tensors(sample, {
                        "neg_c_past": ([P, DEC_BATCH, N_PAGES, HEADS_A],), "win_bias": ([P, WIN_ROWS, HEADS_B, DEC_SEQ],),
                        "new_mask": (rows,), "new_count": (rows,), "new_bias_a": (rows,), "new_bias_b": (rows,)})
                    if stages >= 3:
                        sample_tables(nc, d, sh)
                        sample_attention(nc, d, sh, "A")
                        sample_attention(nc, d, sh, "B")
        if stages >= 4:
            sh |= tensors(ctx, {"x_t": ([P, KT, TOK],), "gains": ([P, 4, KT],), "taps": ([P, 4, UT],), "eps": ([P, 1],)})
            project_out(nc, d, sh)
            conv_ffn(nc, d, sh)
            embed_and_store(nc, d, sh)


_INS = ['x_prompt', 'x_sample', 'p_prompt', 'p_sample', 'cache_fox_k', 'cache_fox_v', 'cache_fox_logf',
        'cache_win_k', 'cache_win_v', 'state_conv', 'page_table', 'g_attn_pre', 'w_in', 'b_forget', 'w_out',
        'g_attn_post', 'g_ffn_pre', 'w_up', 'conv_w', 'conv_b', 'w_down', 'g_ffn_post', 'g_ple', 'w_ple_gate',
        'w_ple']
_OUTS = [('y_p', (1, SEQ, D_MODEL)), ('y_s', (DEC_BATCH, DEC_SEQ, D_MODEL)),
         ('fk_p', (1, 1, SEQ, KV_A, HEAD)), ('fv_p', (1, 1, SEQ, KV_A, HEAD)), ('fl_p', (1, 1, SEQ, HEADS_A)),
         ('wk_p', (1, 1, SEQ, HEADS_B, HEAD)), ('wv_p', (1, 1, SEQ, HEADS_B, HEAD)), ('cv_p', (1, 1, 2, 2 * D_FF)),
         ('fk_s', (1, DEC_BATCH, DEC_SEQ, KV_A, HEAD)), ('fv_s', (1, DEC_BATCH, DEC_SEQ, KV_A, HEAD)),
         ('fl_s', (1, DEC_BATCH, DEC_SEQ, HEADS_A)),
         ('wk_s', (1, DEC_BATCH, DEC_SEQ, HEADS_B, HEAD)), ('wv_s', (1, DEC_BATCH, DEC_SEQ, HEADS_B, HEAD)),
         ('cv_s', (1, DEC_BATCH, 2, 2 * D_FF))]


def build(nc, args, outs, stages=9):
    d = dict(args)
    for name, shape in _OUTS:
        a = outs[name]
        if name in ('y_p',):
            d[name] = a.rearrange("b s d -> (b s) d")
        elif name == 'y_s':
            d[name] = a.rearrange("b s d -> (b s) d")
        elif name[:2] in ('fk', 'fv', 'wk', 'wv'):
            d[name] = a.rearrange("l b s h e -> (l b s) (h e)")
        elif name[:2] == 'fl':
            d[name] = a.rearrange("l b s h -> (l b s) h")
        else:
            d[name] = a.rearrange("l b s f -> l b s f")
    x_p = args['x_prompt'].rearrange("b s d -> (b s) d")
    x_s = args['x_sample'].rearrange("b s d -> (b s) d")
    d["x"] = lambda t: x_p[t * P:(t + 1) * P, :] if t < NPT else x_s
    d["q_scratch"] = nc.dram_tensor("q_scratch", (TOK, 2 * CH), F32, kind="Internal").ap()
    d["mix_scratch"] = nc.dram_tensor("mix_scratch", (TOK, 2 * CH), F32, kind="Internal").ap()
    hymba_step(nc, d, stages)


def kernel(**inputs):
    import numpy as _np
    import concourse.bacc as _bacc
    from concourse import mybir as _mybir
    from concourse.bass_utils import run_bass_kernel_spmd as _run

    nc = _bacc.Bacc("TRN2", target_bir_lowering=False, num_devices=1)
    arrays, args, outs = {}, {}, {}
    for name in _INS:
        a = _np.ascontiguousarray(inputs[name])
        arrays[f"in_{name}"] = a
        args[name] = nc.dram_tensor(f"in_{name}", a.shape, _mybir.dt.from_np(a.dtype), kind="ExternalInput").ap()
    for name, shape in _OUTS:
        outs[name] = nc.dram_tensor(f"out_{name}", shape, F32, kind="ExternalOutput").ap()
    build(nc, args, outs)
    r = _run(nc, [arrays], core_ids=[0])
    return tuple(r.results[0][f"out_{name}"] for name, _ in _OUTS)
```

```python
import numpy as np
import concourse.bass as bass
from concourse import mybir
from contextlib import ExitStack

F32 = mybir.dt.float32
F32R = mybir.dt.float32r
BF16 = mybir.dt.bfloat16
I32 = mybir.dt.int32
ALU = mybir.AluOpType
ACT = mybir.ActivationFunctionType
AX = mybir.AxisListType
ds = bass.ds

D_MODEL = 1024
SEQ = 1024
DEC_BATCH = 8
DEC_SEQ = 4
PAST_LEN = 4096
PAGE = 128
HEAD = 64
HEADS_A = 8
KV_A = 4
GROUP_A = HEADS_A // KV_A
HEADS_B = 8
WINDOW = 2048
D_FF = 2816
PLE = 256
EPS = 1e-6
SCALE = HEAD ** -0.5
NEG = -1e30
N_PAGES = PAST_LEN // PAGE

P = 128
N_NEW = DEC_BATCH * DEC_SEQ
TOK = SEQ + N_NEW
KT = D_MODEL // P
TILES = [(t * P, P) for t in range(SEQ // P)] + [(SEQ, N_NEW)]
NT = len(TILES)
NPT = SEQ // P
CH = 512
LOGF_COL = 2 * CH
CHUNK_COLS = [0, CH, LOGF_COL + HEADS_A, LOGF_COL + HEADS_A + CH, LOGF_COL + HEADS_A + 2 * CH]
NC = len(CHUNK_COLS)
DENSE_ROWS = 4
WIN_ROWS = DENSE_ROWS + (WINDOW - DENSE_ROWS * P) // (P * 16 // DEC_SEQ)
HALF = 2 * P
QB_ORDER = [4, 0, 5, 1, 6, 2, 7, 3]
RMAX = bass.bass_isa.ReduceOp.max
RADD = bass.bass_isa.ReduceOp.add


def norm_and_project(nc, d, sh):
    with ExitStack() as ctx:
        sb = lambda n, s, t=F32: ctx.enter_context(nc.sbuf_tensor(n, s, t))
        pb = lambda n, s, t=F32: ctx.enter_context(nc.psum_tensor(n, s, t))
        sem = lambda n: nc.alloc_semaphore(n)
        x_in = sb("p_x_in", [P, 2, D_MODEL])
        gain = sb("p_gain", [P, D_MODEL])
        x_norm = sb("p_x_norm", [P, 2, D_MODEL])
        square = sb("p_square", [P, D_MODEL])
        mean_sq = sb("p_mean_sq", [P, NT])
        rms = sb("p_rms", [P, NT])
        rstd = sb("p_rstd", [P, NT])
        xt_hi = sb("p_xt_hi", [P, KT, TOK], F32R)
        xt_lo = sb("p_xt_lo", [P, KT, TOK], F32R)
        w_raw = sb("p_w_raw", [P, 2, KT, CH])
        w_hi = sb("p_w_hi", [P, 2, KT, CH], F32R)
        w_lo = sb("p_w_lo", [P, 2, KT, CH], F32R)
        wf_raw = sb("p_wf_raw", [P, KT, HEADS_A])
        wf_hi = sb("p_wf_hi", [P, KT, HEADS_A], F32R)
        wf_lo = sb("p_wf_lo", [P, KT, HEADS_A], F32R)
        z_out = sb("p_z_out", [P, 3, CH])
        b_f = sb("p_b_f", [P, HEADS_A])
        lf_pre = sb("p_lf_pre", [P, NT, HEADS_A])
        lf_tmp = sb("p_lf_tmp", [P, NT, HEADS_A])
        lf_min = sb("p_lf_min", [P, NT, HEADS_A])
        pt = pb("p_pt", [P, 2, D_MODEL])
        pz = pb("p_pz", [P, 3, CH])
        pf = pb("p_pf", [P, NT, HEADS_A])

        x_loaded = [sem(f"p_x_loaded{i}") for i in range(2)]
        gain_loaded = sem("p_gain_loaded")
        w_loaded = [sem(f"p_w_loaded{i}") for i in range(2)]
        wf_loaded = sem("p_wf_loaded")
        bf_loaded = sem("p_bf_loaded")
        stored = [sem(f"p_stored{i}") for i in range(3)]
        lf_stored = sem("p_lf_stored")
        squared = sem("p_squared")
        mean_ready = sem("p_mean_ready")
        rooted = sem("p_rooted")
        rstd_ready = sem("p_rstd_ready")
        normed = sem("p_normed")
        transposed = sem("p_transposed")
        hi_ready = sem("p_hi_ready")
        lo_ready = sem("p_lo_ready")
        w_hi_ready = sem("p_w_hi_ready")
        w_lo_ready = sem("p_w_lo_ready")
        wf_hi_ready = sem("p_wf_hi_ready")
        wf_lo_ready = sem("p_wf_lo_ready")
        z_done = sem("p_z_done")
        z_act = sem("p_z_act")
        z_dve = sem("p_z_dve")
        pf_done = sem("p_pf_done")
        lf_step = sem("p_lf_step")
        lf_act = sem("p_lf_act")
        ident_ready = sem("p_ident_ready")

        w_in = d["w_in"][0].rearrange("(k p) n -> p k n", p=P)
        act_tiles = [t for t in range(NT) if t % 2 == 0]
        dve_tiles = [t for t in range(NT) if t % 2 == 1]

        def evacuated(eng, c, t):
            if t % 2 == 0:
                eng.wait_ge(z_act, len(act_tiles) * c + t // 2 + 1)
            else:
                eng.wait_ge(z_dve, len(dve_tiles) * c + t // 2 + 1)

        def rows_of(name_p, name_s, t, c0, cols):
            t0, n = TILES[t]
            return d[name_p][t0:t0 + n, c0:c0 + cols] if t < NPT else d[name_s][0:n, c0:c0 + cols]

        def destinations(c, t):
            if c == 0 or c == 2:
                t0, n = TILES[t]
                return [(0, CH, d["q_scratch"][t0:t0 + n, (c // 2) * CH:(c // 2 + 1) * CH])]
            if c == 1:
                return [(0, CH // 2, rows_of("fk_p", "fk_s", t, 0, CH // 2)),
                        (CH // 2, CH // 2, rows_of("fv_p", "fv_s", t, 0, CH // 2))]
            pair = ("wk_p", "wk_s") if c == 3 else ("wv_p", "wv_s")
            return [(0, CH, rows_of(*pair, t, 0, CH))]

        def store_count(c, t, through):
            n = 0
            for cc in range(c + 1):
                for tt in range(t % 3, NT, 3):
                    if (cc, tt) < (c, t) or (through and (cc, tt) == (c, t)):
                        n += 16 * len(destinations(cc, tt))
            return n

        with nc.Block() as block:
            @block.sync
            def _(sp):
                def load_x(t):
                    t0, n = TILES[t]
                    if t >= 2:
                        sp.wait_ge(normed, t - 1)
                    sp.dma_start(x_in[:n, t % 2, :], d["x"](t)).then_inc(x_loaded[t % 2], 16)

                def load_w(c):
                    if c >= 2:
                        sp.wait_ge(w_hi_ready, c - 1)
                        sp.wait_ge(w_lo_ready, c - 1)
                    sp.dma_start(w_raw[:, c % 2], w_in[:, :, CHUNK_COLS[c]:CHUNK_COLS[c] + CH])\
                        .then_inc(w_loaded[c % 2], 16)

                load_x(0)
                sp.dma_start(gain[:, :], d["g_attn_pre"][0].partition_broadcast(P)).then_inc(gain_loaded, 16)
                load_x(1)
                load_w(0)
                load_x(2)
                load_w(1)
                load_x(3)
                sp.dma_start(wf_raw[:, :, :], w_in[:, :, LOGF_COL:LOGF_COL + HEADS_A]).then_inc(wf_loaded, 16)
                sp.dma_start(b_f[:, :], d["b_forget"][0].partition_broadcast(P)).then_inc(bf_loaded, 16)
                for c in range(NC):
                    for t in range(NT):
                        if t == 4 and c + 2 < NC:
                            load_w(c + 2)
                        evacuated(sp, c, t)
                        for c0, cols, rows in destinations(c, t):
                            sp.dma_start(rows, z_out[:TILES[t][1], t % 3, c0:c0 + cols]).then_inc(stored[t % 3], 16)
                        if c == 0 and t + 4 < NT:
                            load_x(t + 4)
                sp.wait_ge(lf_step, 4)
                sp.dma_start(d["fl_p"].rearrange("(t p) h -> p t h", p=P), sh["logf"][:, 0:NPT, :])\
                    .then_inc(lf_stored, 16)
                sp.dma_start(d["fl_s"], sh["logf"][:N_NEW, NPT, :]).then_inc(lf_stored, 16)
                for s in range(3):
                    sp.wait_ge(stored[s], store_count(NC - 1, NT - 3 + s, True))
                sp.wait_ge(lf_stored, 32)

            @block.gpsimd
            def _(pool):
                nc.gpsimd.memset(sh["ident"][:, :], 0.0).then_inc(ident_ready, 1)
                pool.wait_ge(ident_ready, 1)
                nc.gpsimd.affine_select(out=sh["ident"][:, :], in_=sh["ident"][:, :], compare_op=ALU.not_equal,
                                        fill=1.0, base=0, pattern=[[-1, P]], channel_multiplier=1)\
                    .then_inc(ident_ready, 1)

            @block.scalar
            def _(act):
                def split_w(c):
                    act.wait_ge(w_loaded[c % 2], 16 * (c // 2 + 1))
                    if c >= 2:
                        act.wait_ge(z_done, NT * (c - 1))
                    nc.scalar.activation(w_hi[:, c % 2], w_raw[:, c % 2], ACT.Copy).then_inc(w_hi_ready, 1)

                def evacuate_z(c, t):
                    n = TILES[t][1]
                    act.wait_ge(z_done, NT * c + t + 1)
                    if store_count(c, t, False):
                        act.wait_ge(stored[t % 3], store_count(c, t, False))
                    nc.scalar.copy(z_out[:n, t % 3, :], pz[:n, t % 3, :]).then_inc(z_act, 1)

                def square_tile(t):
                    n = TILES[t][1]
                    act.wait_ge(x_loaded[t % 2], 16 * (t // 2 + 1))
                    nc.scalar.activation(square[:n, :], x_in[:n, t % 2, :], ACT.Square,
                                         accum_out=mean_sq[:n, t:t + 1]).then_inc(squared, 1)
                    act.wait_ge(mean_ready, t + 1)
                    nc.scalar.activation(rstd[:n, t:t + 1], rms[:n, t:t + 1], ACT.Sqrt).then_inc(rooted, 1)

                def split_hi(t):
                    t0, n = TILES[t]
                    act.wait_ge(transposed, t + 1)
                    nc.scalar.activation(xt_hi[:, :, t0:t0 + n],
                                         pt[:, t % 2, :].rearrange("p (k m) -> p k m", k=KT)[:, :, 0:n],
                                         ACT.Copy).then_inc(hi_ready, 1)

                square_tile(0)
                split_w(0)
                square_tile(1)
                split_hi(0)
                for c in range(NC):
                    for t in range(NT):
                        if c == 0 and t + 2 < NT:
                            square_tile(t + 2)
                        if c == 0 and t + 1 < NT:
                            split_hi(t + 1)
                        if c == 1 and t == 0:
                            act.wait_ge(wf_loaded, 16)
                            nc.scalar.activation(wf_hi[:, :, :], wf_raw[:, :, :], ACT.Copy).then_inc(wf_hi_ready, 1)
                        if t == 2 and c + 1 < NC:
                            split_w(c + 1)
                        if t % 2 == 0:
                            evacuate_z(c, t)
                act.wait_ge(lf_step, 2)
                nc.scalar.activation(lf_tmp[:, :, :], lf_pre[:, :, :], ACT.Abs).then_inc(lf_act, 1)
                act.wait_ge(lf_act, 1)
                nc.scalar.activation(lf_tmp[:, :, :], lf_tmp[:, :, :], ACT.Exp, scale=-1.0).then_inc(lf_act, 1)
                act.wait_ge(lf_act, 2)
                nc.scalar.activation(lf_tmp[:, :, :], lf_tmp[:, :, :], ACT.Ln, bias=1.0).then_inc(lf_act, 1)

            @block.vector
            def _(dve):
                def split_w(c):
                    dve.wait_ge(w_hi_ready, c + 1)
                    if c >= 2:
                        dve.wait_ge(z_done, NT * (c - 1))
                    nc.vector.tensor_tensor(w_lo[:, c % 2], w_raw[:, c % 2], w_hi[:, c % 2].bitcast(F32),
                                            ALU.subtract).then_inc(w_lo_ready, 1)

                def norm_tile(t):
                    n = TILES[t][1]
                    dve.wait_ge(squared, t + 1)
                    nc.vector.tensor_scalar(rms[:n, t:t + 1], mean_sq[:n, t:t + 1], 1.0 / D_MODEL, EPS,
                                            ALU.mult, ALU.add).then_inc(mean_ready, 1)
                    dve.wait_ge(rooted, t + 1)
                    nc.vector.reciprocal(rstd[:n, t:t + 1], rstd[:n, t:t + 1]).then_inc(rstd_ready, 1)
                    dve.wait_ge(rstd_ready, t + 1)
                    if t == 0:
                        dve.wait_ge(gain_loaded, 16)
                    if t >= 2:
                        dve.wait_ge(transposed, t - 1)
                    nc.vector.scalar_tensor_tensor(out=x_norm[:n, t % 2, :], in0=x_in[:n, t % 2, :],
                                                   scalar=rstd[:n, t:t + 1], in1=gain[:n, :],
                                                   op0=ALU.mult, op1=ALU.mult).then_inc(normed, 1)

                def split_lo(t):
                    t0, n = TILES[t]
                    dve.wait_ge(hi_ready, t + 1)
                    nc.vector.tensor_tensor(xt_lo[:, :, t0:t0 + n],
                                            pt[:, t % 2, :].rearrange("p (k m) -> p k m", k=KT)[:, :, 0:n],
                                            xt_hi[:, :, t0:t0 + n].bitcast(F32), ALU.subtract).then_inc(lo_ready, 1)

                def evacuate_z(c, t):
                    n = TILES[t][1]
                    dve.wait_ge(z_done, NT * c + t + 1)
                    if store_count(c, t, False):
                        dve.wait_ge(stored[t % 3], store_count(c, t, False))
                    nc.vector.tensor_copy(z_out[:n, t % 3, :], pz[:n, t % 3, :]).then_inc(z_dve, 1)

                nc.vector.memset(lf_pre[:, :, :], 0.0).then_inc(lf_step, 1)
                norm_tile(0)
                split_w(0)
                norm_tile(1)
                split_lo(0)
                for c in range(NC):
                    for t in range(NT):
                        if c == 0 and t + 2 < NT:
                            norm_tile(t + 2)
                        if c == 0 and t + 1 < NT:
                            split_lo(t + 1)
                        if c == 1 and t == 0:
                            dve.wait_ge(wf_hi_ready, 1)
                            nc.vector.tensor_tensor(wf_lo[:, :, :], wf_raw[:, :, :], wf_hi[:, :, :].bitcast(F32),
                                                    ALU.subtract).then_inc(wf_lo_ready, 1)
                        if t == 3 and c + 1 < NC:
                            split_w(c + 1)
                        if t % 2 == 1:
                            evacuate_z(c, t)
                dve.wait_ge(pf_done, 1)
                dve.wait_ge(bf_loaded, 16)
                dve.wait_ge(lf_step, 1)
                bias = b_f[:, None, :].broadcast_to([P, NT, HEADS_A])
                nc.vector.tensor_tensor(lf_pre[:, 0:NPT, :], pf[:, 0:NPT, :], bias[:, 0:NPT, :], ALU.add)
                nc.vector.tensor_tensor(lf_pre[:N_NEW, NPT, :], pf[:N_NEW, NPT, :], bias[:N_NEW, NPT, :], ALU.add)\
                    .then_inc(lf_step, 1)
                dve.wait_ge(lf_step, 2)
                nc.vector.tensor_scalar(lf_min[:, :, :], lf_pre[:, :, :], 0.0, None, ALU.min).then_inc(lf_step, 1)
                dve.wait_ge(lf_step, 3)
                dve.wait_ge(lf_act, 3)
                nc.vector.tensor_tensor(sh["logf"][:, :, :], lf_min[:, :, :], lf_tmp[:, :, :], ALU.subtract)\
                    .then_inc(lf_step, 1)

            @block.tensor
            def _(pe):
                def transpose_tile(t):
                    n = TILES[t][1]
                    pe.wait_ge(normed, t + 1)
                    if t >= 2:
                        pe.wait_ge(lo_ready, t - 1)
                    for k in range(KT):
                        last = nc.tensor.transpose(pt[:, t % 2, k * P:k * P + n], x_norm[:n, t % 2, k * P:(k + 1) * P],
                                                   sh["ident"][:n, :n])
                    last.then_inc(transposed, 1)

                def project(c, t, hi, lo, out):
                    t0, n = TILES[t]
                    for k in range(KT):
                        for a, b, part in ((xt_hi, hi, 0), (xt_hi, lo, 1), (xt_lo, hi, 2)):
                            last = nc.tensor.matmul(out, a[:, k, t0:t0 + n], b[:, k, :],
                                                    start=(k == 0 and part == 0), stop=(k == KT - 1 and part == 2))
                    return last

                pe.wait_ge(ident_ready, 2)
                transpose_tile(0)
                for c in range(NC):
                    pe.wait_ge(w_lo_ready, c + 1)
                    for t in range(NT):
                        if c == 0:
                            if t + 1 < NT:
                                transpose_tile(t + 1)
                            pe.wait_ge(lo_ready, t + 1)
                        if (c, t) >= (0, 3):
                            evacuated(pe, c if t >= 3 else c - 1, t - 3 if t >= 3 else NT - 3 + t)
                        project(c, t, w_hi[:, c % 2], w_lo[:, c % 2], pz[:TILES[t][1], t % 3, :]).then_inc(z_done, 1)
                pe.wait_ge(wf_lo_ready, 1)
                for t in range(NT):
                    last = project(NC, t, wf_hi, wf_lo, pf[:TILES[t][1], t, :])
                last.then_inc(pf_done, 1)


def build_tables(nc, d, sh):
    with ExitStack() as ctx:
        sb = lambda n, s, t=F32: ctx.enter_context(nc.sbuf_tensor(n, s, t))
        sem = lambda n: nc.alloc_semaphore(n)
        dist_i = sb("t_dist_i", [P, SEQ], I32)
        bits_i = sb("t_bits_i", [P, SEQ], I32)
        near = sb("t_near", [P, SEQ])
        count = sb("t_count", [P, SEQ])
        term = sb("t_term", [P, SEQ])
        carry = sb("t_carry", [P, HEADS_A, NPT])
        totals = sb("t_totals", [P, HEADS_A, NPT])
        sums = sb("t_sums", [P, HEADS_A, NPT])
        p_within = ctx.enter_context(nc.psum_tensor("t_p_within", [P, HEADS_A, NPT], F32))
        p_totals = ctx.enter_context(nc.psum_tensor("t_p_totals", [P, HEADS_A, NPT], F32))
        pool_step = sem("t_pool_step")
        dve_step = sem("t_dve_step")
        act_step = sem("t_act_step")
        sums_ready = sem("t_sums_ready")

        with nc.Block() as block:
            @block.gpsimd
            def _(pool):
                nc.gpsimd.iota(dist_i[:, :], pattern=[[-1, SEQ]], base=SEQ - P, channel_multiplier=1).then_inc(pool_step, 1)
                nc.gpsimd.memset(sh["ones"][:, :], 1.0).then_inc(pool_step, 1)
                nc.gpsimd.memset(sh["ident_bf"][:, :], 0.0).then_inc(pool_step, 1)
                nc.gpsimd.memset(sh["mask_bf"][:, :], 0.0).then_inc(pool_step, 1)
                pool.wait_ge(pool_step, 4)
                nc.gpsimd.affine_select(out=sh["ident_bf"][:, :], in_=sh["ident_bf"][:, :], compare_op=ALU.not_equal,
                                        fill=1.0, base=0, pattern=[[-1, P]], channel_multiplier=1).then_inc(pool_step, 1)
                nc.gpsimd.affine_select(out=sh["tri"][:, :], in_=sh["ones"][:, :], compare_op=ALU.is_ge,
                                        fill=0.0, base=0, pattern=[[1, P]], channel_multiplier=-1).then_inc(pool_step, 1)
                nc.gpsimd.affine_select(out=sh["mask_bf"][:, :], in_=sh["mask_bf"][:, :], compare_op=ALU.is_ge,
                                        fill=NEG, base=0, pattern=[[-1, P]], channel_multiplier=1).then_inc(pool_step, 1)

            @block.tensor
            def _(pe):
                pe.wait_ge(pool_step, 6)
                lf = sh["logf"][:, 0:NPT, :].rearrange("p t h -> p h t")
                nc.tensor.matmul(p_within[:, :, :], sh["tri"][:, :], lf, start=True, stop=True)
                nc.tensor.matmul(p_totals[:, :, :], sh["ones"][:, :], lf, start=True, stop=True).then_inc(sums_ready, 1)

            @block.vector
            def _(dve):
                steps = [0]

                def chained(ins):
                    steps[0] += 1
                    ins.then_inc(dve_step, 1)
                    dve.wait_ge(dve_step, steps[0])

                dve.wait_ge(pool_step, 1)
                chained(nc.vector.tensor_copy(sh["dist"][:, :], dist_i[:, :]))
                chained(nc.vector.tensor_scalar(count[:, :], sh["dist"][:, :], 128.0, None, ALU.is_le))
                for n, reach in ((3, 512.0), (15, 2048.0)):
                    chained(nc.vector.tensor_scalar(bits_i[:, :], dist_i[:, :], n, None, ALU.bitwise_and))
                    chained(nc.vector.tensor_scalar(near[:, :], bits_i[:, :], 0.0, None, ALU.is_equal))
                    chained(nc.vector.scalar_tensor_tensor(out=term[:, :], in0=sh["dist"][:, :], scalar=reach,
                                                           in1=near[:, :], op0=ALU.is_le, op1=ALU.mult))
                    chained(nc.vector.tensor_tensor(count[:, :], count[:, :], term[:, :], ALU.add))
                chained(nc.vector.scalar_tensor_tensor(out=count[:, :], in0=sh["dist"][:, :], scalar=0.0,
                                                       in1=count[:, :], op0=ALU.is_ge, op1=ALU.mult))
                chained(nc.vector.tensor_scalar(near[:, :], count[:, :], 1.0, None, ALU.max))
                dve.wait_ge(act_step, 1)
                chained(nc.vector.tensor_scalar(term[:, :], count[:, :], 0.0, NEG, ALU.is_equal, ALU.mult))
                chained(nc.vector.tensor_tensor(sh["log_count"][:, :], near[:, :], term[:, :], ALU.add))
                for h in range(HEADS_B):
                    last = nc.vector.memset(sh["neg_slope"][:, h:h + 1], -2.0 ** (-8.0 * (h + 1) / HEADS_B))
                chained(last)
                chained(nc.vector.memset(carry[:, :, :], 1.0))
                chained(nc.vector.memset(carry[:, :, 0:1], 0.0))
                dve.wait_ge(sums_ready, 1)
                chained(nc.vector.tensor_copy(totals[:, :, :], p_totals[:, :, :]))
                flat = lambda a: a[:, :, :].rearrange("p h t -> p (h t)")
                chained(nc.vector.tensor_tensor_scan(flat(sums), flat(carry), flat(totals), 0.0, ALU.mult, ALU.add))
                chained(nc.vector.tensor_tensor(totals[:, :, :], totals[:, :, :], sums[:, :, :], ALU.subtract))
                chained(nc.vector.tensor_tensor(sh["neg_c"][:, :, :], totals[:, :, :], p_within[:, :, :], ALU.subtract))

            @block.scalar
            def _(act):
                act.wait_ge(dve_step, 12)
                nc.scalar.activation(near[:, :], near[:, :], ACT.Ln).then_inc(act_step, 1)


def prompt_attention(nc, d, sh, kind):
    NK = 1 if kind == "A" else 2
    KW = NK * HEAD
    PAIRS = 4
    UNITS = 2 * NPT
    ALL = PAIRS * UNITS
    ORDER = QB_ORDER
    COPIES = 2 // NK
    TILE0 = 0 if kind == "A" else CH // P
    col0 = 0 if kind == "A" else CH
    with ExitStack() as ctx:
        n_ = kind.lower() + "_"
        sb = lambda n, s, t=F32: ctx.enter_context(nc.sbuf_tensor(n_ + n, s, t))
        pb = lambda n, s, t=F32: ctx.enter_context(nc.psum_tensor(n_ + n, s, t))
        sem = lambda n: nc.alloc_semaphore(n_ + n)
        q_raw = sb("q_raw", [P, NPT, 2, HEAD])
        k_raw = sb("k_raw", [P, NPT, NK, HEAD])
        v_raw = sb("v_raw", [P, 2, NPT, 2 * HEAD])
        q_parts = sb("q_parts", [P, NPT, 2, 2, HEAD])
        k_high = sb("k_high", [P, NPT, NK, 2, HEAD])
        k_low = sb("k_low", [P, NPT, NK, 2, HEAD])
        diag = sb("diag", [P, 2, NPT, P]) if kind == "A" else None
        q_t = sb("q_t", [P, 2, 2, SEQ], F32R)
        kh_t = sb("kh_t", [P, 2, NK, SEQ], F32R)
        kl_t = sb("kl_t", [P, 2, NK, SEQ], F32R)
        bias = sb("bias", [P, 2, 2, SEQ])
        probs = sb("probs", [P, 4, SEQ])
        probs_t = sb("probs_t", [P, 2, NPT, 2, P])
        neg_max = sb("neg_max", [P, 4])
        denom = sb("denom", [P, 4])
        recip = sb("recip", [P, 4])
        p_scores = pb("p_scores", [P, 2, SEQ])
        p_turn = pb("p_turn", [P, 2, CH])
        p_out = pb("p_out", [P, 2, CH])

        q_loaded, k_loaded, v_loaded = sem("q_loaded"), sem("k_loaded"), sem("v_loaded")
        high_ready, low_ready = sem("high_ready"), sem("low_ready")
        diag_ready = sem("diag_ready")
        turned = sem("turned")
        turn_act, turn_dve = sem("turn_act"), sem("turn_dve")
        scored, biased, exped = sem("scored"), sem("biased"), sem("exped")
        summed = sem("summed")
        normed = sem("normed")
        weighed = sem("weighed")
        out_read = sem("out_read")

        stack_events = [("q", h, half) for h in range(2) for half in range(2)]
        stack_events += [(part, h, half) for part in ("kh", "kl") for h in range(NK) for half in range(2)]
        if kind == "A":
            stack_events += [("bias", h, half) for h in range(2) for half in range(2)]
        NS = len(stack_events)

        def unit(u):
            i, v = divmod(u, UNITS)
            return i, v % 2, ORDER[v // 2], u // 2

        events, step_events, stack_end = [], [], {}
        STACK_STEPS = (3, 3, 4, 5, 5, 6, 7, 7, 8, 9, 10, 11)
        for s in stack_events:
            events.append((0,) + s)
        stack_end[0] = len(events) - 1
        for u in range(ALL):
            i, h, qb, _ = unit(u)
            mine = []
            for b0 in range(0, qb + 1, 4):
                mine.append(len(events))
                events.append((u, b0, min(4, qb + 1 - b0)))
            for s, step in enumerate(STACK_STEPS):
                if i + 1 < PAIRS and step == u % UNITS:
                    mine.append(len(events))
                    events.append((i + 1,) + stack_events[s])
                    stack_end[i + 1] = len(events) - 1
            step_events.append(mine)
        assert NS == len(STACK_STEPS)
        groups_of = lambda u: [e for e in step_events[u] if len(events[e]) == 3]

        def wait_read(eng, e):
            eng.wait_ge(turn_act if e % 2 == 0 else turn_dve, e // 2 + 1)

        def wait_stacks(eng, i):
            wait_read(eng, stack_end[i])
            wait_read(eng, stack_end[i] - 1)

        def evacuate(eng, e, copy):
            eng.wait_ge(turned, e + 1)
            if len(events[e]) == 3:
                u, b0, nb = events[e]
                _, h, _, block = unit(u)
                if block >= 2:
                    eng.wait_ge(weighed, block - 1)
                ins = copy(probs_t[:, block % 2, b0:b0 + nb, h, :],
                           p_turn[:, e % 2, 0:nb * P].rearrange("p (b q) -> p b q", q=P))
            else:
                i, what, h, half = events[e]
                to = {"q": q_t, "kh": kh_t, "kl": kl_t, "bias": bias}[what]
                ins = copy(to[:, i % 2, h, half * CH:(half + 1) * CH], p_turn[:, e % 2, :])
            ins.then_inc(turn_act if e % 2 == 0 else turn_dve, 1)

        with nc.Block() as block:
            @block.sync
            def _(sp):
                kv = ("fk_p", "fv_p") if kind == "A" else ("wk_p", "wv_p")
                for i in range(PAIRS):
                    if i >= 1:
                        sp.wait_ge(high_ready, 2 * i)
                        sp.wait_ge(low_ready, 2 * i)
                    sp.dma_start(q_raw[:, :, :, :].rearrange("p t h e -> p t (h e)"),
                                 d["q_scratch"][0:SEQ, col0 + i * P:col0 + (i + 1) * P]
                                 .rearrange("(t p) e -> p t e", p=P)).then_inc(q_loaded, 16)
                    sp.dma_start(k_raw[:, :, :, :].rearrange("p t h e -> p t (h e)"),
                                 d[kv[0]][:, i * KW:(i + 1) * KW].rearrange("(t p) e -> p t e", p=P))\
                        .then_inc(k_loaded, 16)
                    if i >= 1:
                        sp.wait_ge(v_loaded, 16 * COPIES * i)
                    if i >= 2:
                        sp.wait_ge(weighed, NPT * (i - 1))
                    for c in range(COPIES):
                        sp.dma_start(v_raw[:, i % 2, :, c * KW:(c + 1) * KW],
                                     d[kv[1]][:, i * KW:(i + 1) * KW].rearrange("(t p) e -> p t e", p=P))\
                            .then_inc(v_loaded, 16)

            @block.scalar
            def _(act):
                def split_q(i):
                    act.wait_ge(q_loaded, 16 * (i + 1))
                    if i >= 1:
                        act.wait_ge(turned, stack_end[i - 1] + 1)
                    nc.scalar.activation(q_parts[:, :, :, 0, :].bitcast(F32R), q_raw[:, :, :, :], ACT.Copy, scale=SCALE)\
                        .then_inc(high_ready, 1)

                def split_k(i):
                    act.wait_ge(k_loaded, 16 * (i + 1))
                    for t in range(2):
                        ins = nc.scalar.activation(k_high[:, :, :, t, :].bitcast(F32R), k_raw[:, :, :, :], ACT.Copy)
                    ins.then_inc(high_ready, 1)

                def exp(u):
                    n = (unit(u)[2] + 1) * P
                    act.wait_ge(biased, u + 1)
                    nc.scalar.activation(probs[:, u % 4, 0:n], probs[:, u % 4, 0:n], ACT.Exp,
                                         bias=neg_max[:, u % 4:u % 4 + 1], scale=-1.0,
                                         accum_out=denom[:, u % 4:u % 4 + 1]).then_inc(exped, 1)

                def read_out(n):
                    i, _, qb, _ = unit(2 * n)
                    act.wait_ge(weighed, n + 1)
                    for h in range(2):
                        part = slice(h * HEAD, (h + 1) * HEAD)
                        ins = nc.scalar.activation(sh["rows_t"][part, TILE0 + i, qb * P:(qb + 1) * P],
                                                   p_out[part, n % 2, h * P:(h + 1) * P], ACT.Copy)
                    ins.then_inc(out_read, 1)

                split_q(0)
                split_k(0)
                for e in range(0, NS, 2):
                    evacuate(act, e, nc.scalar.copy)
                for u in range(ALL + 2):
                    if u < ALL:
                        exp(u)
                        i, v = divmod(u, UNITS)
                        if v == 0 and i + 1 < PAIRS:
                            split_q(i + 1)
                        if v == 1 and i + 1 < PAIRS:
                            split_k(i + 1)
                    if u >= 2:
                        for e in step_events[u - 2]:
                            if e % 2 == 0:
                                evacuate(act, e, nc.scalar.copy)
                    if u >= 5 and u % 2 == 1:
                        read_out((u - 5) // 2)
                for n in range((ALL + 1 - 5) // 2 + 1, ALL // 2):
                    read_out(n)

            @block.vector
            def _(dve):
                def split_q(i):
                    dve.wait_ge(high_ready, 2 * i + 1)
                    nc.vector.scalar_tensor_tensor(out=q_parts[:, :, :, 1, :].bitcast(F32R), in0=q_raw[:, :, :, :],
                                                   scalar=SCALE, in1=q_parts[:, :, :, 0, :], op0=ALU.mult,
                                                   op1=ALU.subtract).then_inc(low_ready, 1)

                def split_k(i):
                    dve.wait_ge(high_ready, 2 * i + 2)
                    for t in range(2):
                        ins = nc.vector.tensor_tensor(k_low[:, :, :, t, :].bitcast(F32R), k_raw[:, :, :, :],
                                                      k_high[:, :, :, t, :], ALU.subtract)
                    ins.then_inc(low_ready, 1)

                def make_bias(i, h):
                    if kind == "A":
                        ins = nc.vector.tensor_tensor(
                            diag[:, h], sh["ident"][:, None, :].broadcast_to([P, NPT, P]),
                            sh["neg_c"][:, 2 * i + h, :][:, :, None].broadcast_to([P, NPT, P]), ALU.mult)
                    else:
                        ins = nc.vector.scalar_tensor_tensor(
                            out=bias[:, i % 2, h, :], in0=sh["dist"][:, :],
                            scalar=sh["neg_slope"][:, 2 * i + h:2 * i + h + 1],
                            in1=sh["log_count"][:, :], op0=ALU.mult, op1=ALU.add)
                    ins.then_inc(diag_ready, 1)

                def bias_unit(u):
                    i, h, qb, _ = unit(u)
                    n = (qb + 1) * P
                    b0 = 0 if kind == "A" else SEQ - n
                    if u % UNITS == 0:
                        wait_stacks(dve, i)
                        dve.wait_ge(diag_ready, 2 * (i + 1))
                    if u >= 4:
                        dve.wait_ge(turned, groups_of(u - 4)[-1] + 1)
                    dve.wait_ge(scored, u + 1)
                    nc.vector.tensor_tensor_reduce(out=probs[:, u % 4, 0:n], in0=p_scores[:, u % 2, 0:n],
                                                   in1=bias[:, i % 2, h, b0:b0 + n], scale=-1.0, scalar=3e38,
                                                   op0=ALU.add, op1=ALU.min,
                                                   accum_out=neg_max[:, u % 4:u % 4 + 1]).then_inc(biased, 1)

                def normalise(u):
                    n = (unit(u)[2] + 1) * P
                    dve.wait_ge(exped, u + 1)
                    nc.vector.reciprocal(recip[:, u % 4:u % 4 + 1], denom[:, u % 4:u % 4 + 1]).then_inc(summed, 1)
                    dve.wait_ge(summed, u + 1)
                    nc.vector.tensor_scalar(probs[:, u % 4, 0:n], probs[:, u % 4, 0:n], recip[:, u % 4:u % 4 + 1],
                                            None, ALU.mult).then_inc(normed, 1)

                split_q(0)
                split_k(0)
                make_bias(0, 0)
                make_bias(0, 1)
                for e in range(1, NS, 2):
                    evacuate(dve, e, nc.vector.tensor_copy)
                for u in range(ALL + 2):
                    i, v = divmod(u, UNITS)
                    if u < ALL:
                        bias_unit(u)
                    if 1 <= u <= ALL:
                        normalise(u - 1)
                    if i + 1 < PAIRS:
                        if v == 1:
                            split_q(i + 1)
                        if v == 2:
                            split_k(i + 1)
                        if v in (4, 6):
                            if v == 4 and kind == "A":
                                dve.wait_ge(turned, stack_end[i] + 1)
                            make_bias(i + 1, (v - 4) // 2)
                    if u >= 2:
                        for e in step_events[u - 2]:
                            if e % 2 == 1:
                                evacuate(dve, e, nc.vector.tensor_copy)

            @block.tensor
            def _(pe):
                def stack(e):
                    i, what, h, half = events[e]
                    if e >= 2:
                        wait_read(pe, e - 2)
                    if what == "bias":
                        pe.wait_ge(diag_ready, 2 * i + h + 1)
                        nc.tensor.matmul(p_turn[:, e % 2, :], sh["ones"][:, :],
                                         diag[:, h, half * 4:(half + 1) * 4, :].rearrange("p t m -> p (t m)"),
                                         start=True, stop=True).then_inc(turned, 1)
                        return
                    pe.wait_ge(low_ready, 2 * i + (1 if what == "q" else 2))
                    src = {"q": q_parts, "kh": k_high, "kl": k_low}[what]
                    for j in range(4):
                        last = nc.tensor.transpose(p_turn[:, e % 2, j * P:(j + 1) * P],
                                                   src[:, half * 4 + j, h].rearrange("p s e -> p (s e)"),
                                                   sh["ident"][:, :])
                    last.then_inc(turned, 1)

                def score(u):
                    i, h, qb, _ = unit(u)
                    n = (qb + 1) * P
                    if u % UNITS == 0:
                        wait_stacks(pe, i)
                    if u >= 2:
                        pe.wait_ge(biased, u - 1)
                    for c0 in range(0, n, CH):
                        c1 = min(n, c0 + CH)
                        masked = kind == "A" and c1 == n
                        for part, k_t in enumerate((kh_t, kl_t)):
                            last = nc.tensor.matmul(p_scores[:, u % 2, c0:c1], q_t[:, i % 2, h, qb * P:(qb + 1) * P],
                                                    k_t[:, i % 2, h % NK, c0:c1], start=(part == 0),
                                                    stop=(part == 1 and not masked))
                        if masked:
                            last = nc.tensor.matmul(p_scores[:, u % 2, n - P:n], sh["ident_bf"][:, :],
                                                    sh["mask_bf"][:, :], start=False, stop=True)
                    last.then_inc(scored, 1)

                def turn(u):
                    pe.wait_ge(normed, u + 1)
                    for e in groups_of(u):
                        _, b0, nb = events[e]
                        if e >= 2:
                            wait_read(pe, e - 2)
                        for j in range(nb):
                            last = nc.tensor.transpose(p_turn[:, e % 2, j * P:(j + 1) * P],
                                                       probs[:, u % 4, (b0 + j) * P:(b0 + j + 1) * P],
                                                       sh["ident"][:, :])
                        last.then_inc(turned, 1)

                def weigh(n, half):
                    i, _, qb, _ = unit(2 * n)
                    blocks = range(qb + 1)
                    if half == 0:
                        if n % NPT == 0:
                            pe.wait_ge(v_loaded, 16 * COPIES * (i + 1))
                        if n >= 2:
                            pe.wait_ge(out_read, n - 1)
                        for e in groups_of(2 * n) + groups_of(2 * n + 1):
                            wait_read(pe, e)
                    for b in blocks[:qb // 2 + 1] if half == 0 else blocks[qb // 2 + 1:]:
                        last = nc.tensor.matmul(p_out[:, n % 2, 0:2 * P], v_raw[:, i % 2, b, :],
                                                probs_t[:, n % 2, b, :, :], start=(b == 0), stop=(b == qb))
                        if b == qb:
                            last.then_inc(weighed, 1)

                for e in range(NS):
                    stack(e)
                score(0)
                score(1)
                for u in range(ALL):
                    if u + 2 < ALL:
                        score(u + 2)
                    if u >= 3:
                        weigh((u - 3) // 2, (u - 3) % 2)
                    turn(u)
                    for e in step_events[u]:
                        if len(events[e]) == 4:
                            stack(e)
                weigh(ALL // 2 - 2, 1)
                weigh(ALL // 2 - 1, 0)
                weigh(ALL // 2 - 1, 1)


def sample_tables(nc, d, sh):
    POOL_ROWS = d["cache_fox_logf"].shape[1]
    GROUPS = DEC_BATCH * N_PAGES // P
    SEQS = DEC_BATCH // GROUPS
    RUNS = GROUPS * HEADS_A * SEQS
    with ExitStack() as ctx:
        sb = lambda n, s, t=F32: ctx.enter_context(nc.sbuf_tensor("c_" + n, s, t))
        pb = lambda n, s, t=F32: ctx.enter_context(nc.psum_tensor("c_" + n, s, t))
        sem = lambda n: nc.alloc_semaphore("c_" + n)
        page_ids = sb("page_ids", [P, GROUPS], I32)
        pages = sb("pages", [P, GROUPS, PAGE * HEADS_A])
        by_pos = sb("by_pos", [P, GROUPS, HEADS_A, P])
        totals = sb("totals", [P, RUNS, N_PAGES])
        sums = sb("sums", [P, RUNS, N_PAGES])
        carry = sb("carry", [P, RUNS, N_PAGES])
        same = sb("same", [N_NEW, N_NEW])
        own = sb("own", [N_NEW, DEC_BATCH])
        past = sb("past", [N_NEW, HEADS_A, DEC_BATCH])
        past_sum = sb("past_sum", [N_NEW, HEADS_A])
        neg_new = sb("neg_new", [N_NEW, HEADS_A])
        dist_i = sb("dist_i", [P, WIN_ROWS, HEADS_B, DEC_SEQ], I32)
        bits_i = sb("bits_i", [P, WIN_ROWS, HEADS_B, DEC_SEQ], I32)
        res_i = sb("res_i", [P, WIN_ROWS, HEADS_B, DEC_SEQ], I32)
        dist = sb("dist", [P, WIN_ROWS, HEADS_B, DEC_SEQ])
        near = sb("near", [P, WIN_ROWS, HEADS_B, DEC_SEQ])
        term = sb("term", [P, WIN_ROWS, HEADS_B, DEC_SEQ])
        count = sb("count", [P, WIN_ROWS, HEADS_B, DEC_SEQ])
        new_dist_i = sb("new_dist_i", [N_NEW, DEC_BATCH, HEADS_B, DEC_SEQ], I32)
        new_dist = sb("new_dist", [N_NEW, DEC_BATCH, HEADS_B, DEC_SEQ])
        p_big = pb("p_big", [P, 4 * CH])
        p_sum = pb("p_sum", [P, 4 * CH])
        ids_loaded = sem("ids_loaded")
        pages_loaded = [sem(f"pages_loaded{g}") for g in range(GROUPS)]
        clamped = sem("clamped")
        pool_step, dve_step, act_step, pe_step = sem("pool_step"), sem("dve_step"), sem("act_step"), sem("pe_step")

        with nc.Block() as block:
            @block.sync
            def _(sp):
                for g in range(GROUPS):
                    sp.dma_start(page_ids[:, g:g + 1], d["page_table"][g * SEQS:(g + 1) * SEQS, :]
                                 .rearrange("b (j o) -> (b j) o", o=1)).then_inc(ids_loaded, 16)

            @block.gpsimd
            def _(pool):
                pool.wait_ge(ids_loaded, 16 * GROUPS)
                rows = d["cache_fox_logf"][0].rearrange("n s h -> n (s h)")
                for g in range(GROUPS):
                    nc.gpsimd.indirect_dma_start(
                        out=pages[:, g, :], out_offset=None, in_=rows,
                        in_offset=bass.IndirectOffsetOnAxis(ap=page_ids[:, g:g + 1], axis=0),
                        bounds_check=POOL_ROWS - 1).then_inc(pages_loaded[g], 16)
                g_ = nc.gpsimd
                new, win = sh["new_mask"], [[0, HEADS_B], [1, DEC_SEQ]]
                g_.memset(new[:, :, :, :], 0.0).then_inc(pool_step, 1)
                g_.memset(same[:, :], 1.0).then_inc(pool_step, 1)
                g_.memset(own[:, :], 1.0).then_inc(pool_step, 1)
                g_.iota(dist_i[:, 0:DENSE_ROWS], pattern=[[-P, DENSE_ROWS]] + win, base=DENSE_ROWS * P,
                        channel_multiplier=-1).then_inc(pool_step, 1)
                g_.iota(dist_i[:, DENSE_ROWS:], pattern=[[-CH, WIN_ROWS - DENSE_ROWS], [0, HEADS_B], [DEC_SEQ, DEC_SEQ]],
                        base=WINDOW, channel_multiplier=-DEC_SEQ).then_inc(pool_step, 1)
                g_.iota(res_i[:, :], pattern=[[0, WIN_ROWS], [0, HEADS_B], [-1, DEC_SEQ]], base=P,
                        channel_multiplier=1).then_inc(pool_step, 1)
                g_.iota(new_dist_i[:, :], pattern=[[DEC_SEQ, DEC_BATCH]] + win, base=0,
                        channel_multiplier=-1).then_inc(pool_step, 1)
                pool.wait_ge(pool_step, 7)
                g_.affine_select(out=new[:, :, :, :], in_=new[:, :, :, :], compare_op=ALU.is_ge, fill=NEG, base=0,
                                 pattern=[[DEC_SEQ, DEC_BATCH]] + win, channel_multiplier=-1).then_inc(pool_step, 1)
                pool.wait_ge(pool_step, 8)
                g_.affine_select(out=new[:, :, :, :], in_=new[:, :, :, :], compare_op=ALU.is_ge, fill=NEG, base=0,
                                 pattern=[[-DEC_SEQ, DEC_BATCH], [0, HEADS_B], [0, DEC_SEQ]], channel_multiplier=1)\
                    .then_inc(pool_step, 1)
                g_.affine_select(out=same[:, :], in_=same[:, :], compare_op=ALU.is_ge, fill=0.0, base=0,
                                 pattern=[[1, N_NEW]], channel_multiplier=-1).then_inc(pool_step, 1)
                g_.affine_select(out=own[:, :], in_=own[:, :], compare_op=ALU.is_ge, fill=0.0, base=0,
                                 pattern=[[-DEC_SEQ, DEC_BATCH]], channel_multiplier=1).then_inc(pool_step, 1)
                pool.wait_ge(pool_step, 11)
                g_.affine_select(out=same[:, :], in_=same[:, :], compare_op=ALU.is_ge, fill=0.0, base=0,
                                 pattern=[[-DEC_SEQ, DEC_BATCH], [0, DEC_SEQ]], channel_multiplier=1).then_inc(pool_step, 1)
                g_.affine_select(out=own[:, :], in_=own[:, :], compare_op=ALU.is_ge, fill=0.0, base=DEC_SEQ - 1,
                                 pattern=[[DEC_SEQ, DEC_BATCH]], channel_multiplier=-1).then_inc(pool_step, 1)
                g_.affine_select(out=sh["new_count"][:, :, :, :], in_=new[:, :, :, :], compare_op=ALU.not_equal,
                                 fill=float(np.log(3.0)), base=0, pattern=[[DEC_SEQ, DEC_BATCH]] + win,
                                 channel_multiplier=-1).then_inc(pool_step, 1)

            @block.tensor
            def _(pe):
                for g in range(GROUPS):
                    pe.wait_ge(pages_loaded[g], 16)
                    for h in range(HEADS_A):
                        e = g * HEADS_A + h
                        last = nc.tensor.transpose(p_big[:, e * P:(e + 1) * P], pages[:, g, h::HEADS_A],
                                                   sh["ident"][:, :])
                last.then_inc(pe_step, 1)
                pe.wait_ge(act_step, 1)
                for m, out in ((sh["ones"], p_sum), (sh["tri"], p_big)):
                    for j in range(4):
                        last = nc.tensor.matmul(out[:, j * CH:(j + 1) * CH], m[:, :],
                                                by_pos[:, :, :, :].rearrange("p g h n -> p (g h n)")[:, j * CH:(j + 1) * CH],
                                                start=True, stop=True)
                    last.then_inc(pe_step, 1)
                pe.wait_ge(dve_step, 2)
                pe.wait_ge(pool_step, 13)
                nc.tensor.matmul(p_sum[:N_NEW, 0:HEADS_A], same[:, :], sh["logf"][:N_NEW, NPT, :],
                                 start=True, stop=True).then_inc(pe_step, 1)

            @block.scalar
            def _(act):
                act.wait_ge(pe_step, 1)
                nc.scalar.copy(by_pos[:, :, :, :].rearrange("p g h n -> p (g h n)"),
                               p_big[:, :]).then_inc(act_step, 1)
                act.wait_ge(clamped, 1)
                nc.scalar.activation(near[:, :], near[:, :], ACT.Ln).then_inc(act_step, 1)

            @block.vector
            def _(dve):
                steps = [0]

                def chained(ins):
                    steps[0] += 1
                    ins.then_inc(dve_step, 1)
                    dve.wait_ge(dve_step, steps[0])

                chained(nc.vector.memset(carry[:, :, :], 1.0))
                dve.wait_ge(pe_step, 2)
                chained(nc.vector.tensor_copy(totals[:, :, :].rearrange("p r n -> p (r n)"),
                                              p_sum[:, :]))
                chained(nc.vector.memset(carry[:, :, 0:1], 0.0))
                flat = lambda a: a[:, :, :].rearrange("p r n -> p (r n)")
                chained(nc.vector.tensor_tensor_scan(flat(sums), flat(carry), flat(totals), 0.0, ALU.mult, ALU.add))
                chained(nc.vector.tensor_tensor(totals[:, :, :], totals[:, :, :], sums[:, :, :], ALU.subtract))
                dve.wait_ge(pe_step, 3)
                view = "p (g h b) n -> p g h b n"
                tot_v = totals[:, :, :].rearrange(view, g=GROUPS, h=HEADS_A)
                sum_v = sums[:, :, :].rearrange(view, g=GROUPS, h=HEADS_A)
                in_v = p_big[:, :].rearrange("p (g h b n) -> p g h b n", g=GROUPS, h=HEADS_A, n=N_PAGES)
                for g in range(GROUPS):
                    for b in range(SEQS):
                        last = nc.vector.tensor_tensor(
                            sh["neg_c_past"][:, g * SEQS + b, :, :].rearrange("p n h -> p h n"),
                            tot_v[:, g, :, b, :], in_v[:, g, :, b, :], ALU.subtract)
                chained(last)
                dve.wait_ge(pool_step, 13)
                for g in range(GROUPS):
                    last = nc.vector.tensor_tensor(
                        past[:, :, g * SEQS:(g + 1) * SEQS], sum_v[:N_NEW, g, :, :, N_PAGES - 1],
                        own[:, None, g * SEQS:(g + 1) * SEQS].broadcast_to([N_NEW, HEADS_A, SEQS]), ALU.mult)
                chained(last)
                chained(nc.vector.tensor_reduce(past_sum[:, :], past[:, :, :], AX.X, ALU.add))
                dve.wait_ge(pe_step, 4)
                chained(nc.vector.scalar_tensor_tensor(out=neg_new[:, :], in0=p_sum[:N_NEW, 0:HEADS_A], scalar=-1.0,
                                                       in1=past_sum[:, :], op0=ALU.mult, op1=ALU.subtract))
                dve.wait_ge(pool_step, 14)
                for b in range(DEC_BATCH):
                    last = nc.vector.tensor_tensor(sh["new_bias_a"][:, b], sh["new_mask"][:, b],
                                                   neg_new[:, :, None].broadcast_to([N_NEW, HEADS_A, DEC_SEQ]), ALU.add)
                chained(last)
                chained(nc.vector.tensor_copy(dist[:, :], dist_i[:, :]))
                chained(nc.vector.tensor_scalar(count[:, :], dist[:, :], 128.0, None, ALU.is_le))
                flat = lambda a: a[:, :, :, :].rearrange("p r h j -> p (r h j)")
                for n, reach in ((3, 512.0), (15, 2048.0)):
                    chained(nc.vector.tensor_scalar(bits_i[:, :], dist_i[:, :], n, None, ALU.bitwise_and))
                    chained(nc.vector.tensor_scalar(term[:, :], bits_i[:, :], 0.0, None, ALU.is_equal))
                    chained(nc.vector.scalar_tensor_tensor(out=flat(near), in0=flat(dist), scalar=reach,
                                                           in1=flat(term), op0=ALU.is_le, op1=ALU.mult))
                    chained(nc.vector.tensor_tensor(count[:, :], count[:, :], near[:, :], ALU.add))
                chained(nc.vector.tensor_scalar(bits_i[:, :], res_i[:, :], 3, None, ALU.bitwise_and))
                chained(nc.vector.tensor_scalar(term[:, :], bits_i[:, :], 0.0, None, ALU.is_equal))
                chained(nc.vector.tensor_tensor(count[:, DENSE_ROWS:], count[:, DENSE_ROWS:], term[:, DENSE_ROWS:],
                                                ALU.mult))
                nc.vector.tensor_scalar(near[:, :], count[:, :], 1.0, None, ALU.max).then_inc(clamped, 1)
                chained(nc.vector.tensor_scalar(term[:, :], count[:, :], 0.0, NEG, ALU.is_equal, ALU.mult))
                dve.wait_ge(act_step, 2)
                chained(nc.vector.tensor_tensor(count[:, :], near[:, :], term[:, :], ALU.add))
                chained(nc.vector.tensor_copy(new_dist[:, :], new_dist_i[:, :]))
                for h in range(HEADS_B):
                    nc.vector.scalar_tensor_tensor(out=sh["win_bias"][:, :, h, :], in0=dist[:, :, h, :],
                                                   scalar=sh["neg_slope"][:, h:h + 1], in1=count[:, :, h, :],
                                                   op0=ALU.mult, op1=ALU.add)
                    last = nc.vector.scalar_tensor_tensor(out=sh["new_bias_b"][:, :, h, :], in0=new_dist[:, :, h, :],
                                                          scalar=sh["neg_slope"][:N_NEW, h:h + 1],
                                                          in1=sh["new_count"][:, :, h, :], op0=ALU.mult, op1=ALU.add)
                chained(last)


def sample_attention(nc, d, sh, kind):
    A = kind == "A"
    ROWS = N_PAGES // 2 if A else WIN_ROWS
    KEYSETS = N_PAGES if A else WIN_ROWS
    PAIRS = KV_A // 2 if A else HEADS_B // 2
    G = GROUP_A if A else 1
    QC = 2 * G * DEC_SEQ
    QN = PAIRS * QC
    KW = PAIRS * P
    HALVES = KW // HALF
    col0 = 0 if A else CH
    TURNS = DEC_BATCH // 2
    with ExitStack() as ctx:
        n_ = "d" + kind.lower() + "_"
        sb = lambda n, s, t=F32: ctx.enter_context(nc.sbuf_tensor(n_ + n, s, t))
        pb = lambda n, s, t=F32: ctx.enter_context(nc.psum_tensor(n_ + n, s, t))
        sem = lambda n: nc.alloc_semaphore(n_ + n)
        K_RING = ROWS if A else 2 * ROWS
        k_in = sb("k_in", [P, K_RING, CH])
        v_in = sb("v_in", [P, 2, KEYSETS, HALVES, HALF + 1])
        k_t = sb("k_t", [P, 2, CH])
        table = sb("table", [1, DEC_BATCH * N_PAGES], I32)
        q_in = sb("q_in", [N_NEW, CH])
        k_new = sb("k_new", [N_NEW, KW])
        v_new = sb("v_new", [N_NEW, HALVES, HALF + 1])
        k_new_t = sb("k_new_t", [P, PAIRS, N_NEW])
        q_blocks = sb("q_blocks", [P, DEC_BATCH, PAIRS, QC])
        logits = sb("logits", [P, 2, KEYSETS + 1, QN])
        probs = sb("probs", [P, 2, KEYSETS + 1, QN])
        part_max = sb("part_max", [P, 2, QN])
        all_max = sb("all_max", [P, 2, QN])
        recip = sb("recip", [QN, 2, HALVES])
        out_all = sb("out_all", [QN, DEC_BATCH, HALVES, HALF])
        p_scores = pb("p_scores", [P, 2, KEYSETS * QN if A else CH])
        p_turn = pb("p_turn", [P, 2, CH])
        p_side = pb("p_side", [P, 2, CH])
        p_outs = [p_side] + [pb(f"p_out{f}", [P, 2, CH]) for f in range(1, HALVES)]

        setup_loaded, table_loaded = sem("setup_loaded"), sem("table_loaded")
        BATCH = ROWS // 4 if A else ROWS
        k_loaded = [sem(f"k_loaded{s}") for s in range(K_RING // BATCH)]
        v_loaded = [sem(f"v_loaded{s}") for s in range(2)]
        set_pe, set_dve = sem("set_pe"), sem("set_dve")
        turned = sem("turned")
        turn_act, turn_dve = sem("turn_act"), sem("turn_dve")
        scored = sem("scored")
        biased = sem("biased")
        maxed = sem("maxed")
        max_spread = sem("max_spread")
        shifted = sem("shifted")
        exped = sem("exped")
        ones_ready = sem("ones_ready")
        weighed = sem("weighed")
        recip_ready = sem("recip_ready")
        out_ready = sem("out_ready")
        spare = sem("spare")
        stored = sem("stored")
        K_LOADS = 16 * (2 * BATCH if A else ROWS)
        V_LOADS = 16 * (2 * ROWS if A else DENSE_ROWS + HALVES * (ROWS - DENSE_ROWS))

        def block_of(r, i):
            return (i % PAIRS, 2 * r + i // PAIRS) if A else (i, r)

        def load_pages(eng, i, b, cache):
            keys = cache == "cache_fox_k"
            for r0 in range(0, ROWS, BATCH):
                n = b * ROWS + r0
                if keys:
                    eng.wait_ge(turned, 2 * ROWS * i + n + BATCH)
                    eng.sem_inc(spare, 1)
                elif r0 == 0:
                    eng.wait_ge(weighed, 2 * i + b + 1)
                    eng.sem_inc(spare, 1)
                _, ids = nc.values_load_multi_w_load_instructions(
                    table[0:1, ds(2 * N_PAGES * i + 2 * n, 2 * BATCH)], engines=[eng.engine],
                    min_val=0, max_val=d[cache].shape[1] - 1)
                for e in range(2 * BATCH):
                    row, half = n + e // 2, e % 2
                    dst = k_in[:, row % K_RING, half * KW:(half + 1) * KW] if keys else v_in[:, b, row % ROWS * 2 + half, 0, 0:HALF]
                    done = k_loaded[n % K_RING // BATCH] if keys else v_loaded[b]
                    src = d[cache][0].rearrange("n s h e -> n s (h e)")[ds(ids[e], 1)].rearrange("o s e -> (o s) e")
                    eng.dma_start(dst, src).then_inc(done, 16)

        def load_window(eng, i, b, cache):
            keys = cache == "cache_win_k"
            if keys:
                eng.wait_ge(turned, 2 * ROWS * i + (b + 1) * ROWS)
            else:
                eng.wait_ge(weighed, 2 * i + b + 1)
            eng.sem_inc(spare, 1)
            src = d[cache][0].rearrange("b s h e -> b s (h e)")[ds(2 * i + b, 1)].rearrange("o s e -> (o s) e")
            for c in range(ROWS):
                if c < DENSE_ROWS:
                    r0 = WINDOW - (DENSE_ROWS - c) * P
                    rows = src[r0:r0 + P, :]
                else:
                    r0 = (c - DENSE_ROWS) * CH
                    rows = src[r0:r0 + CH, :].rearrange("(m r) e -> m r e", r=16)[:, 0:DEC_SEQ, :]
                if keys:
                    eng.dma_start(k_in[:, b * ROWS + c], rows).then_inc(k_loaded[b], 16)
                elif c < DENSE_ROWS:
                    eng.dma_start(v_in[:, b, c, :, 0:HALF], rows.rearrange("p (f e) -> p f e", f=HALVES))\
                        .then_inc(v_loaded[b], 16)
                else:
                    for f in range(HALVES):
                        eng.dma_start(v_in[:, b, c, f, 0:HALF], rows[:, :, f * HALF:(f + 1) * HALF])\
                            .then_inc(v_loaded[b], 16)

        with nc.Block() as block:
            @block.sync
            def _(sp):
                if A:
                    sp.dma_start(table[:, :], d["page_table"].rearrange("(o b) j -> o (b j)", o=1)).then_inc(table_loaded, 16)
                sp.dma_start(q_in[:, :], d["q_scratch"][SEQ:TOK, col0:col0 + CH]).then_inc(setup_loaded, 16)
                sp.dma_start(k_new[:, :], d["fk_s" if A else "wk_s"]).then_inc(setup_loaded, 16)
                sp.dma_start(v_new[:, :, 0:HALF], d["fv_s" if A else "wv_s"].rearrange("n (f e) -> n f e", e=HALF))\
                    .then_inc(setup_loaded, 16)
                if A:
                    sp.wait_ge(table_loaded, 16)
                with sp.Fori(0, TURNS) as i:
                    for b in range(2):
                        if A:
                            load_pages(sp, i, b, "cache_fox_k")
                        else:
                            load_window(sp, i, b, "cache_win_k")
                            load_window(sp, i, b, "cache_win_v")
                sp.wait_ge(out_ready, 2 + DEC_BATCH)
                for h in range(QN // DEC_SEQ):
                    f, c0 = divmod(h // G * HEAD, HALF)
                    sp.dma_start(d["mix_scratch"][SEQ:TOK, col0 + h * HEAD:col0 + (h + 1) * HEAD]
                                 .rearrange("(b t) e -> t b e", t=DEC_SEQ),
                                 out_all[h * DEC_SEQ:(h + 1) * DEC_SEQ, :, f, c0:c0 + HEAD]).then_inc(stored, 16)
                sp.wait_ge(stored, 16 * (QN // DEC_SEQ))

            @block.gpsimd
            def _(pool):
                nc.gpsimd.memset(v_in[:, :, :, :, HALF:], 1.0)
                nc.gpsimd.memset(v_new[:, :, HALF:], 1.0).then_inc(ones_ready, 1)
                if A:
                    pool.wait_ge(table_loaded, 16)
                with pool.Fori(0, TURNS) as i:
                    def spread(ready, src, dst, op, done, b):
                        pool.wait_ge(ready, 2 * i + b + 1)
                        pool.sem_inc(spare, 1)
                        nc.gpsimd.partition_all_reduce(dst[:, b], src[:, b], P, op).then_inc(done, 1)

                    if A:
                        load_pages(pool, i, 0, "cache_fox_v")
                    spread(maxed, part_max, all_max, RMAX, max_spread, 0)
                    if A:
                        load_pages(pool, i, 1, "cache_fox_v")
                    spread(maxed, part_max, all_max, RMAX, max_spread, 1)

            @block.tensor
            def _(pe):
                pe.sem_inc(turned, K_RING)
                pe.sem_inc(scored, 2)
                pe.sem_inc(weighed, 2)
                pe.wait_ge(setup_loaded, 48)
                for j in range(4):
                    nc.tensor.transpose(p_turn[:, 0, j * N_NEW:(j + 1) * N_NEW], q_in[:, j * P:(j + 1) * P],
                                        sh["ident"][:N_NEW, :N_NEW])
                for j in range(PAIRS):
                    last = nc.tensor.transpose(p_turn[:, 1, j * N_NEW:(j + 1) * N_NEW], k_new[:, j * P:(j + 1) * P],
                                               sh["ident"][:N_NEW, :N_NEW])
                last.then_inc(set_pe, 1)
                pe.wait_ge(ones_ready, 1)
                pe.wait_ge(set_dve, 3 + 2 * PAIRS * G)
                with pe.Fori(0, TURNS) as i:
                    def turn(n):
                        b, r = divmod(n, ROWS)
                        if r % BATCH == 0:
                            uses = 2 * ROWS // K_RING
                            pe.wait_ge(k_loaded[n % K_RING // BATCH], K_LOADS * (uses * i + n // K_RING + 1))
                        pe.wait_ge(turn_act if n % 2 == 0 else turn_dve, ROWS * i + n // 2 + 1)
                        for j in range(4):
                            last = nc.tensor.transpose(p_turn[:, n % 2, j * P:(j + 1) * P],
                                                       k_in[:, n % K_RING, j * P:(j + 1) * P], sh["ident"][:, :])
                        last.then_inc(turned, 1)

                    def score(n):
                        b, r = divmod(n, ROWS)
                        pe.wait_ge(turn_act if n % 2 == 0 else turn_dve, ROWS * i + n // 2 + 2)
                        for j in range(4):
                            pair, keys = block_of(r, j)
                            c0 = keys * QN + pair * QC
                            nc.tensor.matmul(p_scores[:, b, c0:c0 + QC], k_t[:, n % 2, j * P:(j + 1) * P],
                                             q_blocks[:, ds(2 * i + b, 1), pair, :], start=True, stop=True)

                    for b in range(2):
                        turn(b * ROWS)
                        pe.wait_ge(biased, 2 * i + b + 1)
                        for r in range(ROWS):
                            if r + 1 < ROWS:
                                turn(b * ROWS + r + 1)
                            score(b * ROWS + r)
                        pe.wait_ge(out_ready, 2 * i + b + 1)
                        pe.sem_inc(spare, 1)
                        for pair in range(PAIRS):
                            last = nc.tensor.matmul(p_side[:N_NEW, b, pair * QC:(pair + 1) * QC],
                                                    k_new_t[:, pair, :], q_blocks[:, ds(2 * i + b, 1), pair, :],
                                                    start=True, stop=True)
                        last.then_inc(scored, 1)
                    for b in range(2):
                        pe.wait_ge(exped, 2 * i + b + 1)
                        pe.wait_ge(v_loaded[b], V_LOADS * (i + 1))
                        for f, p_out in enumerate(p_outs):
                            out = p_out[:QN, b, 64:64 + HALF + 1]
                            for keys in range(KEYSETS):
                                nc.tensor.matmul(out, probs[:, b, keys, :], v_in[:, b, keys, f, :],
                                                 start=(keys == 0), stop=False)
                            last = nc.tensor.matmul(out, probs[:N_NEW, b, KEYSETS, :], v_new[:, f, :],
                                                    start=False, stop=True)
                        last.then_inc(weighed, 1)

            @block.scalar
            def _(act):
                act.sem_inc(turn_act, 1)
                with act.Fori(0, TURNS) as i:
                    def evacuate(n):
                        act.wait_ge(turned, K_RING + 2 * ROWS * i + n + 1)
                        nc.scalar.copy(k_t[:, n % 2, :], p_turn[:, n % 2, :]).then_inc(turn_act, 1)

                    def exp(b):
                        act.wait_ge(shifted, 2 * i + b + 1)
                        act.wait_ge(weighed, 2 * i + b + 1)
                        nc.scalar.activation(probs[:, b], logits[:, b], ACT.Exp).then_inc(exped, 1)

                    for n in range(2 * ROWS):
                        if n == ROWS + ROWS // 2 + 1:
                            exp(0)
                        if n % 2 == 0:
                            evacuate(n)
                    exp(1)

            @block.vector
            def _(dve):
                dve.sem_inc(turn_dve, 1)
                dve.sem_inc(biased, 2)
                dve.sem_inc(out_ready, 2)
                nc.vector.memset(q_blocks[:, :, :, :], 0.0).then_inc(set_dve, 1)
                nc.vector.memset(logits[:, :, KEYSETS, :], NEG).then_inc(set_dve, 1)
                dve.wait_ge(set_pe, 1)
                dve.wait_ge(set_dve, 2)
                copies = 0
                for kv in range(2 * PAIRS):
                    pair, kh = divmod(kv, 2)
                    for g in range(G):
                        tile, row = (kv, g * HEAD) if A else (pair, kh * HEAD)
                        src = p_turn[row:row + HEAD, 0, tile * N_NEW:(tile + 1) * N_NEW]\
                            .rearrange("p (b t) -> p b t", b=DEC_BATCH)
                        c0 = (kh * G + g) * DEC_SEQ
                        nc.vector.tensor_scalar(q_blocks[kh * HEAD:(kh + 1) * HEAD, :, pair, c0:c0 + DEC_SEQ], src,
                                                SCALE, None, ALU.mult).then_inc(set_dve, 1)
                        copies += 1
                nc.vector.tensor_copy(k_new_t[:, :, :].rearrange("p a n -> p (a n)"),
                                      p_turn[:, 1, 0:PAIRS * N_NEW]).then_inc(set_dve, 1)
                assert 3 + copies == 3 + 2 * PAIRS * G
                with dve.Fori(0, TURNS) as i:
                    def evacuate(n):
                        dve.wait_ge(turned, K_RING + 2 * ROWS * i + n + 1)
                        nc.vector.tensor_copy(k_t[:, n % 2, :], p_turn[:, n % 2, :]).then_inc(turn_dve, 1)

                    def add_bias(b):
                        dve.wait_ge(scored, 2 + 2 * i + b + 1)
                        scores = p_scores[:, b, 0:KEYSETS * QN]
                        if A:
                            nc.vector.tensor_tensor(
                                logits[:, b, 0:KEYSETS, :].rearrange("p n (h t) -> p (n h) t", t=DEC_SEQ),
                                scores.rearrange("p (n t) -> p n t", t=DEC_SEQ),
                                sh["neg_c_past"][:, ds(2 * i + b, 1), :, :].rearrange("p o n h -> p (o n h)")[:, :, None]
                                .broadcast_to([P, KEYSETS * HEADS_A, DEC_SEQ]), ALU.add)
                        else:
                            nc.vector.tensor_tensor(
                                logits[:, b, 0:KEYSETS, :].rearrange("p n q -> p (n q)"), scores,
                                sh["win_bias"][:, :, :, :].rearrange("p n h t -> p (n h t)"), ALU.add)
                        new_bias = sh["new_bias_a" if A else "new_bias_b"]
                        nc.vector.tensor_tensor(logits[:N_NEW, b, KEYSETS, :], p_side[:N_NEW, b, 0:QN],
                                                new_bias[:, ds(2 * i + b, 1)].rearrange("p o h t -> p (o h t)"),
                                                ALU.add).then_inc(biased, 1)
                        dve.wait_ge(biased, 2 + 2 * i + b + 1)
                        nc.vector.tensor_reduce(part_max[:, b], logits[:, b].rearrange("p n q -> p q n"), AX.X, ALU.max)\
                            .then_inc(maxed, 1)

                    def shift(b):
                        dve.wait_ge(max_spread, 2 * i + b + 1)
                        nc.vector.tensor_tensor(logits[:, b], logits[:, b],
                                                all_max[:, b, None, :].broadcast_to([P, KEYSETS + 1, QN]),
                                                ALU.subtract).then_inc(shifted, 1)

                    def normalise(b):
                        dve.wait_ge(weighed, 2 + 2 * i + b + 1)
                        for f, p_out in enumerate(p_outs):
                            last = nc.vector.reciprocal(recip[:, b, f:f + 1], p_out[:QN, b, 64 + HALF:64 + HALF + 1])
                        last.then_inc(recip_ready, 1)
                        dve.wait_ge(recip_ready, 2 * i + b + 1)
                        for f, p_out in enumerate(p_outs):
                            last = nc.vector.tensor_scalar(
                                out_all[:, ds(2 * i + b, 1), f, :].rearrange("p o e -> p (o e)"),
                                p_out[:QN, b, 64:64 + HALF], recip[:, b, f:f + 1], None, ALU.mult)
                        last.then_inc(out_ready, 1)

                    for n in range(2 * ROWS):
                        if n == ROWS:
                            add_bias(0)
                        if n == ROWS + ROWS // 2:
                            shift(0)
                        if n % 2 == 1:
                            evacuate(n)
                    add_bias(1)
                    shift(1)
                    normalise(0)
                    normalise(1)


PIECE = TOK // 3
NP = TOK // PIECE
LAST_P = SEQ - (NP - 1) * PIECE
FT = D_FF // P
UT = 2 * FT
SLOTS = 4
ADDS = KT + 1
AHEAD = SLOTS - 1


def piece(a, k, q):
    return a[:, k, q * PIECE:(q + 1) * PIECE]


def project_out(nc, d, sh):
    with ExitStack() as ctx:
        sb = lambda n, s, t=F32: ctx.enter_context(nc.sbuf_tensor("o_" + n, s, t))
        pb = lambda n, s, t=F32: ctx.enter_context(nc.psum_tensor("o_" + n, s, t))
        sem = lambda n: nc.alloc_semaphore("o_" + n)
        rows_in = sb("rows_in", [P, 2, D_MODEL])
        mix_hi = sb("mix_hi", [P, KT, TOK], F32R)
        mix_lo = sb("mix_lo", [P, KT, TOK], F32R)
        y = sb("y", [P, KT, TOK])
        w_raw = sb("w_raw", [P, SLOTS, KT, P])
        w_hi = sb("w_hi", [P, SLOTS, KT, P], F32R)
        w_lo = sb("w_lo", [P, SLOTS, KT, P], F32R)
        square = sb("square", [P, 2, PIECE])
        sum_sq = sb("sum_sq", [P, NP, PIECE])
        gains_in = sb("gains_in", [4 * KT, P])
        taps_in = sb("taps_in", [UT, 4, P])
        p_turn = pb("p_turn", [P, 2, D_MODEL])
        p_y = pb("p_y", [P, NP, CH])
        p_sum = pb("p_sum", [P, CH])
        x_t, gains, taps = sh["rows_t"], sh["gains"], sh["taps"]

        rows_loaded = [sem("rows_loaded0"), sem("rows_loaded1")]
        consts_loaded = sem("consts_loaded")
        w_loaded = [sem(f"w_loaded{s}") for s in range(SLOTS)]
        turned, turn_read = sem("turned"), sem("turn_read")
        mix_hi_ready, mix_lo_ready = sem("mix_hi_ready"), sem("mix_lo_ready")
        w_hi_ready = sem("w_hi_ready")
        w_lo_ready = sem("w_lo_ready")
        y_done = sem("y_done")
        y_read = sem("y_read")
        squared = sem("squared")
        added = sem("added")
        sum_done, rms_ready, rstd_ready = sem("sum_done"), sem("rms_ready"), sem("rstd_ready")
        gained, scaled = sem("gained"), sem("scaled")
        const_pe, const_act, eps_ready = sem("const_pe"), sem("const_act"), sem("eps_ready")

        with nc.Block() as block:
            @block.sync
            def _(sp):
                def load_rows(n):
                    t0, rows = TILES[NT - 1 if n == 0 else n - 1]
                    if n >= 2:
                        sp.wait_ge(turned, n - 1)
                    sp.dma_start(rows_in[:rows, n % 2, :], d["mix_scratch"][t0:t0 + rows, :] if n == 0 else d["x"](n - 1))\
                        .then_inc(rows_loaded[n % 2], 16)

                def load_w(m):
                    if m >= SLOTS:
                        sp.wait_ge(w_lo_ready, m - SLOTS + 1)
                    sp.dma_start(w_raw[:, m % SLOTS],
                                 d["w_out"][0].rearrange("(k p) n -> p k n", p=P)[:, :, m * P:(m + 1) * P])\
                        .then_inc(w_loaded[m % SLOTS], 16)

                load_rows(0)
                for m in range(SLOTS):
                    load_w(m)
                load_rows(1)
                for j, name in enumerate(("g_attn_post", "g_ffn_pre", "g_ffn_post", "g_ple")):
                    sp.dma_start(gains_in[j * KT:(j + 1) * KT, :], d[name].rearrange("o (k p) -> (o k) p", p=P))\
                        .then_inc(consts_loaded, 16)
                sp.dma_start(taps_in[:, 0:3, :], d["conv_w"][0].rearrange("j (t p) -> t j p", p=P))\
                    .then_inc(consts_loaded, 16)
                sp.dma_start(taps_in[:, 3, :], d["conv_b"][0].rearrange("(t p) -> t p", p=P)).then_inc(consts_loaded, 16)
                for n in range(2, NT + 1):
                    load_rows(n)
                    if SLOTS + n - 2 < KT:
                        load_w(SLOTS + n - 2)

            @block.gpsimd
            def _(pool):
                nc.gpsimd.memset(sum_sq[:, :, :], 0.0).then_inc(added, 1)
                for n in range(NP * KT):
                    q = n % NP
                    pool.wait_ge(squared, n + 1)
                    pool.wait_ge(added, n + 1)
                    nc.gpsimd.tensor_tensor(sum_sq[:, q, :], sum_sq[:, q, :], square[:, n % 2, :], ALU.add)\
                        .then_inc(added, 1)

            @block.tensor
            def _(pe):
                def turn_rows(n):
                    t0, rows = TILES[NT - 1 if n == 0 else n - 1]
                    pe.wait_ge(rows_loaded[n % 2], 16 * (n // 2 + 1))
                    if n >= 2:
                        pe.wait_ge(turn_read, n - 1)
                    for k in range(KT):
                        last = nc.tensor.transpose(p_turn[:, n % 2, k * P:k * P + rows],
                                                   rows_in[:rows, n % 2, k * P:(k + 1) * P], sh["ident"][:rows, :rows])
                    last.then_inc(turned, 1)

                turn_rows(0)
                pe.wait_ge(mix_lo_ready, KT)
                for m in range(KT):
                    pe.wait_ge(w_lo_ready, m + 1)
                    for q in range(NP):
                        c0 = q * PIECE
                        if m > 0:
                            pe.wait_ge(y_read, NP * (m - 1) + q + 1)
                        for k in range(KT):
                            for part, (w, a) in enumerate(((w_hi, mix_hi), (w_hi, mix_lo), (w_lo, mix_hi))):
                                last = nc.tensor.matmul(p_y[:, q, 0:PIECE], w[:, m % SLOTS, k, :], a[:, k, c0:c0 + PIECE],
                                                        start=(k == 0 and part == 0), stop=(k == KT - 1 and part == 2))
                        last.then_inc(y_done, 1)
                    turn_rows(m + 1)
                    if m == 0:
                        pe.wait_ge(consts_loaded, 96)
                        nc.tensor.transpose(p_sum[:, 0:4 * KT], gains_in[:, :], sh["ident"][:4 * KT, :4 * KT])
                        for j in range(4):
                            last = nc.tensor.transpose(p_sum[:, 64 + j * UT:64 + (j + 1) * UT], taps_in[:, j, :],
                                                       sh["ident"][:UT, :UT])
                        last.then_inc(const_pe, 1)
                turn_rows(NT)
                pe.wait_ge(const_act, 1)
                for q in range(NP):
                    pe.wait_ge(added, 1 + NP * (KT - 1) + q + 1)
                    if q > 0:
                        pe.wait_ge(rms_ready, q)
                    nc.tensor.matmul(p_sum[:, 0:PIECE], sh["ones"][:, :], sum_sq[:, q, :],
                                     start=True, stop=True).then_inc(sum_done, 1)

            @block.scalar
            def _(act):
                def split_w(m):
                    act.wait_ge(w_loaded[m % SLOTS], 16 * (m // SLOTS + 1))
                    if m >= SLOTS:
                        act.wait_ge(y_done, NP * (m - SLOTS + 1))
                    nc.scalar.activation(w_hi[:, m % SLOTS], w_raw[:, m % SLOTS], ACT.Copy).then_inc(w_hi_ready, 1)

                def read_rows(n):
                    t0, rows = TILES[NT - 1 if n == 0 else n - 1]
                    act.wait_ge(turned, n + 1)
                    nc.scalar.activation(x_t[:, :, t0:t0 + rows],
                                         p_turn[:, n % 2, :].rearrange("p (k m) -> p k m", k=KT)[:, :, 0:rows],
                                         ACT.Copy).then_inc(turn_read, 1)

                split_w(0)
                read_rows(0)
                act.wait_ge(turn_read, 1)
                for k in range(KT):
                    nc.scalar.activation(mix_hi[:, k, :], sh["rows_t"][:, k, :], ACT.Copy).then_inc(mix_hi_ready, 1)
                for m in range(1, SLOTS):
                    split_w(m)
                for m in range(KT):
                    for q in range(NP):
                        n = NP * m + q
                        act.wait_ge(y_done, n + 1)
                        if n >= 2:
                            act.wait_ge(added, n)
                        nc.scalar.activation(square[:, n % 2, :], p_y[:, q, 0:PIECE], ACT.Square).then_inc(squared, 1)
                        nc.scalar.activation(piece(y, m, q), p_y[:, q, 0:PIECE], ACT.Copy).then_inc(y_read, 1)
                    if m == 0:
                        act.wait_ge(const_pe, 1)
                        nc.scalar.copy(gains[:, :, :].rearrange("p a k -> p (a k)"), p_sum[:, 0:4 * KT])
                        nc.scalar.copy(taps[:, :, :].rearrange("p a k -> p (a k)"),
                                       p_sum[:, 64:64 + 4 * UT]).then_inc(const_act, 1)
                    read_rows(m + 1)
                    if m + SLOTS < KT:
                        split_w(m + SLOTS)
                read_rows(NT)
                act.wait_ge(eps_ready, 1)
                for q in range(NP):
                    act.wait_ge(sum_done, q + 1)
                    nc.scalar.activation(sum_sq[:, q, :], p_sum[:, 0:PIECE], ACT.Sqrt, scale=1.0 / D_MODEL,
                                         bias=sh["eps"][:, :]).then_inc(rms_ready, 1)

            @block.vector
            def _(dve):
                nc.vector.memset(sh["eps"][:, :], EPS).then_inc(eps_ready, 1)

                def split_w(m):
                    dve.wait_ge(w_hi_ready, m + 1)
                    nc.vector.tensor_tensor(w_lo[:, m % SLOTS], w_raw[:, m % SLOTS], w_hi[:, m % SLOTS].bitcast(F32),
                                            ALU.subtract).then_inc(w_lo_ready, 1)

                split_w(0)
                for k in range(KT):
                    dve.wait_ge(mix_hi_ready, k + 1)
                    nc.vector.tensor_tensor(mix_lo[:, k, :], sh["rows_t"][:, k, :], mix_hi[:, k, :].bitcast(F32),
                                            ALU.subtract).then_inc(mix_lo_ready, 1)
                for m in range(1, KT):
                    split_w(m)
                dve.wait_ge(turn_read, NT + 1)
                dve.wait_ge(const_act, 1)
                for q in range(NP):
                    dve.wait_ge(rms_ready, q + 1)
                    nc.vector.reciprocal(sum_sq[:, q, :], sum_sq[:, q, :]).then_inc(rstd_ready, 1)
                    dve.wait_ge(rstd_ready, q + 1)
                    for k in range(KT):
                        nc.vector.scalar_tensor_tensor(out=piece(y, k, q), in0=piece(y, k, q), scalar=gains[:, 0, k:k + 1],
                                                       in1=sum_sq[:, q, :], op0=ALU.mult, op1=ALU.mult).then_inc(gained, 1)
                    for k in range(KT):
                        dve.wait_ge(gained, q * KT + k + 1)
                        ins = nc.vector.tensor_tensor(piece(x_t, k, q), piece(x_t, k, q), piece(y, k, q), ALU.add)
                    ins.then_inc(scaled, 1)


def conv_ffn(nc, d, sh):
    N_TILES = UT + 3 * KT
    BLOCKS = [(0, 8), (8, 8), (16, 6)]
    PRE = [0] + [2 * p - 1 for p in range(1, NP)]
    POST = [2 * p + 2 if p < NP - 1 else 2 * p + 1 for p in range(NP)]
    ROUNDS = 4
    QT = UT // ROUNDS
    STATE = 2 * DEC_BATCH
    with ExitStack() as ctx:
        sb = lambda n, s, t=F32: ctx.enter_context(nc.sbuf_tensor("f_" + n, s, t))
        pb = lambda n, s, t=F32: ctx.enter_context(nc.psum_tensor("f_" + n, s, t))
        sem = lambda n: nc.alloc_semaphore("f_" + n)
        xn_hi = sb("xn_hi", [P, KT, PIECE], F32R)
        xn_lo = sb("xn_lo", [P, KT, PIECE], F32R)
        xn = sb("xn", [P, 2, PIECE])
        h_hi = sb("h_hi", [P, FT, PIECE], F32R)
        h_lo = sb("h_lo", [P, FT, PIECE], F32R)
        w_raw = sb("w_raw", [P, SLOTS, KT, P])
        w_hi = sb("w_hi", [P, SLOTS, KT, P], F32R)
        w_lo = sb("w_lo", [P, SLOTS, KT, P], F32R)
        work = sb("work", [P, KT, 2 + PIECE])
        new_up = sb("new_up", [P, SLOTS, DEC_BATCH, 2 + DEC_SEQ])
        square = sb("square", [P, 2, PIECE])
        sum_sq = sb("sum_sq", [P, PIECE])
        rstd = sb("rstd", [P, PIECE])
        before = sb("before", [P, UT, 2 + STATE])
        rows_io = sb("rows_io", [2 + STATE, QT, P])
        p_up = pb("p_up", [P, SLOTS, CH])
        p_y = pb("p_y", [P, 2, CH])
        p_sum = pb("p_sum", [P, CH])
        p_turn = pb("p_turn", [P, CH])
        x_t, gains, taps = sh["rows_t"], sh["gains"], sh["taps"]
        up = lambda j, c0, c1: work[:, j, c0:c1]
        conv = lambda j: work[:, SLOTS + j, 0:PIECE]

        w_loaded = [sem(f"w_loaded{s}") for s in range(SLOTS)]
        w_hi_ready = sem("w_hi_ready")
        w_lo_ready = sem("w_lo_ready")
        w_used = sem("w_used")
        up_read = sem("up_read")
        haloed = sem("haloed")
        carried = sem("carried")
        convolved = sem("convolved")
        tap_added = sem("tap_added")
        gelued, hid_ready, hid_hi = sem("gelued"), sem("hid_ready"), sem("hid_hi")
        hid_lo = sem("hid_lo")
        y_read = sem("y_read")
        squared, added = sem("squared"), sem("added")
        sum_done, rms_ready, rstd_ready = sem("sum_done"), sem("rms_ready"), sem("rstd_ready")
        xn_ready, xn_hi_ready, xn_lo_ready = sem("xn_ready"), sem("xn_hi_ready"), sem("xn_lo_ready")
        gained, residual = sem("gained"), sem("residual")
        rows_loaded, rows_stored, rows_out = sem("rows_loaded"), sem("rows_stored"), sem("rows_out")
        turned, turn_read, cleared = sem("turned"), sem("turn_read"), sem("cleared")
        spare = sem("spare")

        def wait_loaded(eng, p, base, per, i, j):
            n = N_TILES * p + base + j
            eng.wait_ge(w_loaded[j % SLOTS], 16 * (n // SLOTS + 1) + 16 * (per // SLOTS) * i)

        with nc.Block() as block:
            @block.sync
            def _(sp):
                w_up = d["w_up"][0].rearrange("(k p) n -> p k n", p=P)
                w_down = d["w_down"][0].rearrange("(k p) n -> p k n", p=P)
                for p in range(NP + 1):
                    with sp.Fori(0, FT // 2 if p < NP else 1) as i:
                        for j in range(SLOTS if p < NP else AHEAD):
                            s, half = divmod(j, 2)
                            sp.wait_ge(w_lo_ready, N_TILES * p + SLOTS * i + j + 1)
                            sp.sem_inc(spare, 1)
                            sp.dma_start(w_raw[:, j], w_up[:, :, ds((2 * i + s + half * FT) * P, P)])\
                                .then_inc(w_loaded[j], 16)
                    if p == NP:
                        break
                    with sp.Fori(0, KT // 4) as i:
                        for j in range(12):
                            m, b = divmod(j, 3)
                            f0, fn = BLOCKS[b]
                            sp.wait_ge(w_lo_ready, N_TILES * p + UT + 12 * i + j + 1)
                            sp.sem_inc(spare, 1)
                            sp.dma_start(w_raw[:, j % SLOTS, 0:fn], w_down[:, f0:f0 + fn, ds((4 * i + m) * P, P)])\
                                .then_inc(w_loaded[j % SLOTS], 16)
                for s in range(SLOTS):
                    sp.wait_ge(w_loaded[s], 16 * (NP * N_TILES // SLOTS + (s < AHEAD)))

            @block.gpsimd
            def _(pool):
                def load_state(r):
                    pool.dma_start(rows_io[:STATE], d["state_conv"][0].rearrange("b j (t p) -> (b j) t p", p=P)
                                   [:, r * QT:(r + 1) * QT]).then_inc(rows_loaded, 16)

                def next_state(r):
                    if r + 1 < ROUNDS:
                        pool.wait_ge(turned, r + 1)
                        load_state(r + 1)

                def clear_sum(q):
                    if q > 0:
                        pool.wait_ge(sum_done, q)
                    nc.gpsimd.memset(sum_sq[:, :], 0.0).then_inc(added, 1)

                def add_square(q, k, slot):
                    pool.wait_ge(squared, KT * q + k + 1)
                    pool.wait_ge(added, ADDS * q + k + 1)
                    nc.gpsimd.tensor_tensor(sum_sq[:, :], sum_sq[:, :], square[:, slot, :], ALU.add).then_inc(added, 1)

                def add_squares(q):
                    clear_sum(q)
                    for k in range(KT):
                        add_square(q, k, k % 2)

                pool.sem_inc(carried, 4)
                load_state(0)
                nc.gpsimd.memset(before[:, :, 0:2], 0.0).then_inc(cleared, 1)
                pool.wait_ge(cleared, 1)
                add_squares(PRE[0])
                for p in range(NP):
                    last_piece = p == NP - 1
                    if not last_piece:
                        add_squares(PRE[p + 1])
                    else:
                        pool.wait_ge(turn_read, ROUNDS)
                    if p > 0:
                        pool.wait_ge(residual, p)
                        pool.wait_ge(carried, 4 + UT * p)
                    with pool.Fori(0, FT // 2) as i:
                        for j in range(SLOTS):
                            s, half = divmod(j, 2)
                            u = UT * p + SLOTS * i + j
                            tile = 2 * i + s + half * FT
                            pool.wait_ge(convolved, u + 1)
                            pool.sem_inc(spare, 1)
                            ins = nc.gpsimd.tensor_copy(up(j, 0, 2), before[:, ds(tile, 1), 0:2].rearrange("p o c -> p (o c)"))
                            if last_piece:
                                ins = nc.gpsimd.tensor_copy(
                                    new_up[:, j, :, 0:2],
                                    before[:, ds(tile, 1), 2:].rearrange("p o (b c) -> p (o b) c", c=2))
                            ins.then_inc(haloed, 1)
                            pool.wait_ge(up_read, 4 + u + 1)
                            pool.wait_ge(haloed, u + 1)
                            pool.sem_inc(spare, 1)
                            last = LAST_P if last_piece else PIECE
                            ins = nc.gpsimd.tensor_copy(before[:, ds(tile, 1), 0:2].rearrange("p o c -> p (o c)"),
                                                        up(j, last, last + 2))
                            if last_piece:
                                ins = nc.gpsimd.tensor_copy(
                                    before[:, ds(tile, 1), 2:].rearrange("p o (b c) -> p (o b) c", c=2),
                                    new_up[:, j, :, DEC_SEQ:DEC_SEQ + 2])
                            ins.then_inc(carried, 1)
                    next_state(2 * p)
                    clear_sum(POST[p])
                    with pool.Fori(0, KT // 4) as i:
                        for m in range(4):
                            add_square(POST[p], 4 * i + m, m % 2)
                    next_state(2 * p + 1)
                for r in range(ROUNDS):
                    pool.wait_ge(rows_out, r + 1)
                    pool.dma_start(d["cv_p"][0, 0].rearrange("j (t p) -> j t p", p=P)[:, r * QT:(r + 1) * QT],
                                   rows_io[0:2]).then_inc(rows_stored, 16)
                    pool.dma_start(d["cv_s"][0].rearrange("b j (t p) -> (b j) t p", p=P)[:, r * QT:(r + 1) * QT],
                                   rows_io[2:2 + STATE]).then_inc(rows_stored, 16)
                pool.wait_ge(rows_stored, 32 * ROUNDS)

            @block.tensor
            def _(pe):
                pe.sem_inc(w_used, 4)

                def turn_state(r):
                    if r < ROUNDS:
                        pe.wait_ge(rows_loaded, 16 * (r + 1))
                        if r > 0:
                            pe.wait_ge(turn_read, r)
                        for t in range(QT):
                            last = nc.tensor.transpose(p_turn[:, t * STATE:(t + 1) * STATE], rows_io[:STATE, t, :],
                                                       sh["ident"][:STATE, :STATE])
                        last.then_inc(turned, 1)

                def sum_squares(q):
                    pe.wait_ge(added, ADDS * (q + 1))
                    if q > 0:
                        pe.wait_ge(rms_ready, q)
                    nc.tensor.matmul(p_sum[:, 0:PIECE], sh["ones"][:, :], sum_sq[:, :], start=True, stop=True)\
                        .then_inc(sum_done, 1)

                sum_squares(PRE[0])
                for p in range(NP):
                    pe.wait_ge(xn_lo_ready, KT * (p + 1))
                    with pe.Fori(0, FT // 2) as i:
                        for j in range(SLOTS):
                            pe.wait_ge(w_lo_ready, 4 + N_TILES * p + SLOTS * i + j + 1)
                            pe.wait_ge(up_read, UT * p + SLOTS * i + j + 1)
                            for k in range(KT):
                                for part, (w, a) in enumerate(((w_hi, xn_hi), (w_hi, xn_lo), (w_lo, xn_hi))):
                                    last = nc.tensor.matmul(p_up[:, j, 0:PIECE], w[:, j, k, :], a[:, k, :],
                                                            start=(k == 0 and part == 0), stop=(k == KT - 1 and part == 2))
                            last.then_inc(w_used, 1)
                    turn_state(2 * p)
                    if p < NP - 1:
                        sum_squares(PRE[p + 1])
                    with pe.Fori(0, KT // 4) as i:
                        for j in range(12):
                            m, b = divmod(j, 3)
                            f0, fn = BLOCKS[b]
                            pe.wait_ge(w_lo_ready, 4 + N_TILES * p + UT + 12 * i + j + 1)
                            if j < 3:
                                pe.wait_ge(hid_lo, 2 + FT * p + f0 + fn)
                            if b == 0:
                                pe.wait_ge(y_read, KT * p + 4 * i + m + 1)
                            for f in range(fn):
                                for part, (w, a) in enumerate(((w_hi, h_hi), (w_hi, h_lo), (w_lo, h_hi))):
                                    last = nc.tensor.matmul(
                                        p_y[:, m % 2, 0:PIECE], w[:, j % SLOTS, f, :], a[:, f0 + f, :],
                                        start=(b == 0 and f == 0 and part == 0), stop=(b == 2 and f == fn - 1 and part == 2))
                            last.then_inc(w_used, 1)
                    turn_state(2 * p + 1)
                    sum_squares(POST[p])
                pe.wait_ge(carried, 4 + NP * UT)
                for r in range(ROUNDS):
                    if r > 0:
                        pe.wait_ge(rows_out, r)
                    for t in range(QT):
                        last = nc.tensor.transpose(p_up[:2 + STATE, t // 4, t % 4 * P:(t % 4 + 1) * P],
                                                   before[:, r * QT + t, :], sh["ident"][:, :])
                    last.then_inc(turned, 1)

            @block.scalar
            def _(act):
                def split_w(p, base, per, i, j):
                    wait_loaded(act, p, base, per, i, j)
                    act.wait_ge(w_used, N_TILES * p + base + per * i + j + 1)
                    nc.scalar.activation(w_hi[:, j % SLOTS], w_raw[:, j % SLOTS], ACT.Copy).then_inc(w_hi_ready, 1)

                def state_read(r):
                    if r < ROUNDS:
                        act.wait_ge(turned, r + 1)
                        nc.scalar.activation(before[:, r * QT:(r + 1) * QT, 2:],
                                             p_turn[:, 0:QT * STATE].rearrange("p (t c) -> p t c", t=QT),
                                             ACT.Copy).then_inc(turn_read, 1)

                def squares(p, q):
                    for k in range(KT):
                        n = ADDS * q + k
                        if n > 0:
                            act.wait_ge(added, n)
                        nc.scalar.activation(square[:, k % 2, :], x_t[:, k, p * PIECE:(p + 1) * PIECE],
                                             ACT.Square).then_inc(squared, 1)

                def root(q):
                    act.wait_ge(sum_done, q + 1)
                    nc.scalar.activation(rstd[:, :], p_sum[:, 0:PIECE], ACT.Sqrt, scale=1.0 / D_MODEL,
                                         bias=sh["eps"][:, :]).then_inc(rms_ready, 1)

                def normed_hi(p):
                    for k in range(KT):
                        act.wait_ge(xn_ready, KT * p + k + 1)
                        nc.scalar.activation(xn_hi[:, k, :], xn[:, k % 2, :], ACT.Copy).then_inc(xn_hi_ready, 1)

                act.sem_inc(up_read, 4)
                act.sem_inc(y_read, 2)
                squares(0, PRE[0])
                for j in range(AHEAD):
                    split_w(0, 0, SLOTS, 0, j)
                root(PRE[0])
                normed_hi(0)
                for p in range(NP):
                    last_piece = p == NP - 1
                    if not last_piece:
                        squares(p + 1, PRE[p + 1])
                    if p > 0:
                        act.wait_ge(residual, p)
                    with act.Fori(0, FT // 2) as i:
                        def read_up(j):
                            s, half = divmod(j, 2)
                            n, u = N_TILES * p + SLOTS * i + j, UT * p + SLOTS * i + j
                            tile = 2 * i + s + half * FT
                            split_w(p, 0, SLOTS, i, j + AHEAD)
                            act.wait_ge(w_used, 4 + n + 1)
                            act.wait_ge(convolved, u + 1)
                            act.wait_ge(carried, u + 1)
                            act.wait_ge(hid_lo, FT * p + 2 * i + s + 1)
                            if last_piece:
                                nc.scalar.activation(up(j, 2, 2 + LAST_P), p_up[:, j, 0:LAST_P], ACT.Copy)
                                nc.scalar.activation(new_up[:, j, :, 2:],
                                                     p_up[:, j, LAST_P:PIECE].rearrange("p (b t) -> p b t", b=DEC_BATCH),
                                                     ACT.Copy)
                            else:
                                nc.scalar.activation(up(j, 2, 2 + PIECE), p_up[:, j, 0:PIECE], ACT.Copy)
                            nc.scalar.activation(conv(j), p_up[:, j, 0:PIECE], ACT.Identity,
                                                 scale=taps[:, 2, ds(tile, 1)], bias=taps[:, 3, ds(tile, 1)])\
                                .then_inc(up_read, 1)

                        def gelu(s):
                            act.wait_ge(convolved, 4 + UT * p + SLOTS * i + 2 * s + 1)
                            nc.scalar.activation(conv(2 * s), conv(2 * s), ACT.Gelu_apprx_tanh).then_inc(gelued, 1)

                        def hidden_hi(s):
                            act.wait_ge(hid_ready, FT * p + 2 * i + s + 1)
                            nc.scalar.activation(h_hi[:, ds(2 * i + s, 1), :].rearrange("p o c -> p (o c)"),
                                                 conv(2 * s + 1), ACT.Copy).then_inc(hid_hi, 1)

                        read_up(0)
                        read_up(1)
                        read_up(2)
                        gelu(0)
                        read_up(3)
                        hidden_hi(0)
                        gelu(1)
                        hidden_hi(1)
                    state_read(2 * p)
                    if not last_piece:
                        root(PRE[p + 1])
                        normed_hi(p + 1)
                    act.wait_ge(carried, 4 + UT * (p + 1))
                    with act.Fori(0, KT // 4) as i:
                        for j in range(12):
                            m, b = divmod(j, 3)
                            split_w(p, UT, 12, i, j + AHEAD)
                            if b == 2:
                                act.wait_ge(w_used, 4 + N_TILES * p + UT + 12 * i + j + 1)
                                act.wait_ge(added, ADDS * POST[p] + 4 * i + m)
                                nc.scalar.activation(square[:, m % 2, :], p_y[:, m % 2, 0:PIECE], ACT.Square)\
                                    .then_inc(squared, 1)
                                nc.scalar.activation(work[:, ds(4 * i + m, 1), 0:PIECE].rearrange("p o c -> p (o c)"),
                                                     p_y[:, m % 2, 0:PIECE], ACT.Copy).then_inc(y_read, 1)
                    state_read(2 * p + 1)
                    root(POST[p])
                for r in range(ROUNDS):
                    act.wait_ge(turned, ROUNDS + r + 1)
                    if r > 0:
                        act.wait_ge(rows_stored, 32 * r)
                    nc.scalar.activation(rows_io[:, :, :], p_up[:2 + STATE, 0:3, :].rearrange("p a (t c) -> p (a t) c", c=P)
                                         [:, 0:QT, :], ACT.Copy).then_inc(rows_out, 1)

            @block.vector
            def _(dve):
                def split_w(p, base, per, i, j):
                    dve.wait_ge(w_hi_ready, N_TILES * p + base + per * i + j + 1)
                    nc.vector.tensor_tensor(w_lo[:, j % SLOTS], w_raw[:, j % SLOTS], w_hi[:, j % SLOTS].bitcast(F32),
                                            ALU.subtract).then_inc(w_lo_ready, 1)

                def invert(q):
                    dve.wait_ge(rms_ready, q + 1)
                    nc.vector.reciprocal(rstd[:, :], rstd[:, :]).then_inc(rstd_ready, 1)
                    dve.wait_ge(rstd_ready, q + 1)

                def normalise(p):
                    def low(k):
                        dve.wait_ge(xn_hi_ready, KT * p + k + 1)
                        nc.vector.tensor_tensor(xn_lo[:, k, :], xn[:, k % 2, :], xn_hi[:, k, :].bitcast(F32),
                                                ALU.subtract).then_inc(xn_lo_ready, 1)

                    for k in range(KT):
                        if k >= 2:
                            dve.wait_ge(xn_lo_ready, KT * p + k - 1)
                        nc.vector.scalar_tensor_tensor(out=xn[:, k % 2, :], in0=x_t[:, k, p * PIECE:(p + 1) * PIECE],
                                                       scalar=gains[:, 1, k:k + 1], in1=rstd[:, :],
                                                       op0=ALU.mult, op1=ALU.mult).then_inc(xn_ready, 1)
                        if k >= 1:
                            low(k - 1)
                    low(KT - 1)

                dve.sem_inc(w_lo_ready, 4)
                dve.sem_inc(convolved, 4)
                dve.sem_inc(hid_lo, 2)
                for j in range(AHEAD):
                    split_w(0, 0, SLOTS, 0, j)
                invert(PRE[0])
                normalise(0)
                for p in range(NP):
                    last_piece = p == NP - 1
                    with dve.Fori(0, FT // 2) as i:
                        def add_tap(j, tap, done):
                            s, half = divmod(j, 2)
                            tile = 2 * i + s + half * FT
                            rows = LAST_P if last_piece else PIECE
                            ins = nc.vector.scalar_tensor_tensor(
                                out=conv(j)[:, 0:rows], in0=up(j, tap, tap + rows), scalar=taps[:, tap, ds(tile, 1)],
                                in1=conv(j)[:, 0:rows], op0=ALU.mult, op1=ALU.add)
                            if last_piece:
                                new = conv(j)[:, rows:PIECE].rearrange("p (b t) -> p b t", b=DEC_BATCH)
                                ins = nc.vector.scalar_tensor_tensor(
                                    out=new, in0=new_up[:, j, :, tap:tap + DEC_SEQ], scalar=taps[:, tap, ds(tile, 1)],
                                    in1=new, op0=ALU.mult, op1=ALU.add)
                            ins.then_inc(done, 1)

                        def convolve(j):
                            u = UT * p + SLOTS * i + j
                            split_w(p, 0, SLOTS, i, j + AHEAD)
                            dve.wait_ge(haloed, u + 1)
                            dve.wait_ge(up_read, 4 + u + 1)
                            add_tap(j, 1, tap_added)
                            dve.wait_ge(tap_added, u + 1)
                            add_tap(j, 0, convolved)

                        def gate(s):
                            h = FT * p + 2 * i + s
                            dve.wait_ge(gelued, h + 1)
                            dve.wait_ge(convolved, 4 + UT * p + SLOTS * i + 2 * s + 2)
                            nc.vector.tensor_tensor(conv(2 * s + 1), conv(2 * s), conv(2 * s + 1), ALU.mult)\
                                .then_inc(hid_ready, 1)

                        def hidden_lo(s):
                            dve.wait_ge(hid_hi, FT * p + 2 * i + s + 1)
                            nc.vector.tensor_tensor(h_lo[:, ds(2 * i + s, 1), :].rearrange("p o c -> p (o c)"),
                                                    conv(2 * s + 1),
                                                    h_hi[:, ds(2 * i + s, 1), :].rearrange("p o c -> p (o c)").bitcast(F32),
                                                    ALU.subtract).then_inc(hid_lo, 1)

                        convolve(0)
                        convolve(1)
                        convolve(2)
                        gate(0)
                        convolve(3)
                        hidden_lo(0)
                        gate(1)
                        hidden_lo(1)
                    if not last_piece:
                        invert(PRE[p + 1])
                        normalise(p + 1)
                    with dve.Fori(0, KT // 4) as i:
                        for j in range(12):
                            split_w(p, UT, 12, i, j + AHEAD)
                    invert(POST[p])
                    for k in range(KT):
                        if k == 0:
                            dve.wait_ge(y_read, 2 + KT * (p + 1))
                        nc.vector.scalar_tensor_tensor(out=work[:, k, 0:PIECE], in0=work[:, k, 0:PIECE],
                                                       scalar=gains[:, 2, k:k + 1], in1=rstd[:, :],
                                                       op0=ALU.mult, op1=ALU.mult).then_inc(gained, 1)
                    for k in range(KT):
                        dve.wait_ge(gained, KT * p + k + 1)
                        ins = nc.vector.tensor_tensor(x_t[:, k, p * PIECE:(p + 1) * PIECE],
                                                      x_t[:, k, p * PIECE:(p + 1) * PIECE], work[:, k, 0:PIECE], ALU.add)
                    ins.then_inc(residual, 1)


def embed_and_store(nc, d, sh):
    IT = PLE // P
    with ExitStack() as ctx:
        sb = lambda n, s, t=F32: ctx.enter_context(nc.sbuf_tensor("g_" + n, s, t))
        pb = lambda n, s, t=F32: ctx.enter_context(nc.psum_tensor("g_" + n, s, t))
        sem = lambda n: nc.alloc_semaphore("g_" + n)
        xn_hi = sb("xn_hi", [P, KT, TOK], F32R)
        xn_lo = sb("xn_lo", [P, KT, TOK], F32R)
        e_hi = sb("e_hi", [P, IT, TOK], F32R)
        e_lo = sb("e_lo", [P, IT, TOK], F32R)
        xn = sb("xn", [P, 2, PIECE])
        w_raw = sb("w_raw", [P, SLOTS, KT + IT, P])
        w_hi = sb("w_hi", [P, SLOTS, KT + IT, P], F32R)
        w_lo = sb("w_lo", [P, SLOTS, KT + IT, P], F32R)
        square = sb("square", [P, 2, PIECE])
        sum_sq = sb("sum_sq", [P, NP, PIECE])
        gate = sb("gate", [P, 2, PIECE])
        rows_io = sb("rows_io", [P, 2, D_MODEL])
        p_gate = pb("p_gate", [P, NP, CH])
        p_emb = pb("p_emb", [P, NP, CH])
        p_sum = pb("p_sum", [P, CH])
        x_t, gains = sh["rows_t"], sh["gains"]

        e_loaded = [sem("e_loaded0"), sem("e_loaded1")]
        w_loaded = [sem(f"w_loaded{s}") for s in range(SLOTS)]
        e_turned, e_hi_ready, e_lo_ready = sem("e_turned"), sem("e_hi_ready"), sem("e_lo_ready")
        w_hi_ready, w_lo_ready = sem("w_hi_ready"), sem("w_lo_ready")
        squared, added = sem("squared"), sem("added")
        sum_done, rms_ready, rstd_ready = sem("sum_done"), sem("rms_ready"), sem("rstd_ready")
        xn_ready, xn_hi_ready, xn_lo_ready = sem("xn_ready"), sem("xn_hi_ready"), sem("xn_lo_ready")
        products, gated, embedded, residual = sem("products"), sem("gated"), sem("embedded"), sem("residual")
        turned, out_act, out_dve = sem("turned"), sem("out_act"), sem("out_dve")
        stored = [sem("stored0"), sem("stored1")]

        with nc.Block() as block:
            @block.sync
            def _(sp):
                def load_e(t):
                    t0, rows = TILES[t]
                    src = d["p_prompt"][0, 0][t0:t0 + rows, :] if t < NPT else d["p_sample"][0].rearrange("b s e -> (b s) e")
                    if t >= 2:
                        sp.wait_ge(e_turned, t - 1)
                    sp.dma_start(rows_io[:rows, t % 2, 0:PLE], src).then_inc(e_loaded[t % 2], 16)

                def load_w(m):
                    if m >= SLOTS:
                        sp.wait_ge(w_lo_ready, m - SLOTS + 1)
                    for k0, kn, name in ((0, KT, "w_ple_gate"), (KT, IT, "w_ple")):
                        sp.dma_start(w_raw[:, m % SLOTS, k0:k0 + kn],
                                     d[name][0].rearrange("(k p) n -> p k n", p=P)[:, :, m * P:(m + 1) * P])\
                            .then_inc(w_loaded[m % SLOTS], 16)

                load_e(0)
                load_e(1)
                for m in range(SLOTS):
                    load_w(m)
                for t in range(2, NT):
                    load_e(t)
                for m in range(SLOTS, KT):
                    load_w(m)
                for t in range(NT):
                    t0, rows = TILES[t]
                    sp.wait_ge(out_act, t + 1)
                    sp.wait_ge(out_dve, t + 1)
                    sp.dma_start(d["y_p"][t0:t0 + rows, :] if t < NPT else d["y_s"], rows_io[:rows, t % 2, :])\
                        .then_inc(stored[t % 2], 16)
                for s in range(2):
                    sp.wait_ge(stored[s], 16 * len(range(s, NT, 2)))

            @block.gpsimd
            def _(pool):
                nc.gpsimd.memset(sum_sq[:, :, :], 0.0).then_inc(added, 1)
                for n in range(NP * KT):
                    pool.wait_ge(squared, n + 1)
                    pool.wait_ge(added, n + 1)
                    nc.gpsimd.tensor_tensor(sum_sq[:, n // KT, :], sum_sq[:, n // KT, :], square[:, n % 2, :], ALU.add)\
                        .then_inc(added, 1)

            @block.tensor
            def _(pe):
                for t in range(NT):
                    t0, rows = TILES[t]
                    pe.wait_ge(e_loaded[t % 2], 16 * (t // 2 + 1))
                    if t >= NP:
                        pe.wait_ge(e_lo_ready, t - NP + 1)
                    for k in range(IT):
                        last = nc.tensor.transpose(p_gate[:, t % NP, k * P:k * P + rows],
                                                   rows_io[:rows, t % 2, k * P:(k + 1) * P], sh["ident"][:rows, :rows])
                    last.then_inc(e_turned, 1)
                for q in range(NP):
                    pe.wait_ge(added, 1 + KT * (q + 1))
                    if q > 0:
                        pe.wait_ge(rms_ready, q)
                    nc.tensor.matmul(p_sum[:, 0:PIECE], sh["ones"][:, :], sum_sq[:, q, :], start=True, stop=True)\
                        .then_inc(sum_done, 1)
                pe.wait_ge(e_lo_ready, NT)
                for m in range(KT):
                    pe.wait_ge(w_lo_ready, m + 1)
                    for q in range(NP):
                        if m == 0:
                            pe.wait_ge(xn_lo_ready, KT * (q + 1))
                        else:
                            pe.wait_ge(embedded, NP * (m - 1) + q + 1)
                        for out, w0, kn, hi, lo in ((p_gate, 0, KT, xn_hi, xn_lo), (p_emb, KT, IT, e_hi, e_lo)):
                            for k in range(kn):
                                for part, (w, a) in enumerate(((w_hi, hi), (w_hi, lo), (w_lo, hi))):
                                    last = nc.tensor.matmul(out[:, q, 0:PIECE], w[:, m % SLOTS, w0 + k, :], piece(a, k, q),
                                                            start=(k == 0 and part == 0), stop=(k == kn - 1 and part == 2))
                        last.then_inc(products, 1)
                pe.wait_ge(residual, NP * KT)
                for t in range(NT):
                    t0, rows = TILES[t]
                    bank = p_gate if t % 2 == 0 else p_emb
                    if t >= 2:
                        pe.wait_ge(out_act, t - 1)
                        pe.wait_ge(out_dve, t - 1)
                    for k in range(KT):
                        last = nc.tensor.transpose(bank[:rows, k // 4, k % 4 * P:(k % 4 + 1) * P],
                                                   x_t[:, k, t0:t0 + rows], sh["ident"][:, :])
                    last.then_inc(turned, 1)

            @block.scalar
            def _(act):
                def split_w(m):
                    act.wait_ge(w_loaded[m % SLOTS], 32 * (m // SLOTS + 1))
                    if m >= SLOTS:
                        act.wait_ge(products, NP * (m - SLOTS + 1))
                    nc.scalar.activation(w_hi[:, m % SLOTS], w_raw[:, m % SLOTS], ACT.Copy).then_inc(w_hi_ready, 1)

                def e_split(t):
                    t0, rows = TILES[t]
                    act.wait_ge(e_turned, t + 1)
                    nc.scalar.activation(e_hi[:, :, t0:t0 + rows],
                                         p_gate[:, t % NP, 0:PLE].rearrange("p (k m) -> p k m", k=IT)[:, :, 0:rows],
                                         ACT.Copy).then_inc(e_hi_ready, 1)

                for n in range(NP * KT):
                    if n >= 2:
                        act.wait_ge(added, n)
                    nc.scalar.activation(square[:, n % 2, :], piece(x_t, n % KT, n // KT), ACT.Square).then_inc(squared, 1)
                for t in range(NT):
                    e_split(t)
                for q in range(NP):
                    act.wait_ge(sum_done, q + 1)
                    nc.scalar.activation(sum_sq[:, q, :], p_sum[:, 0:PIECE], ACT.Sqrt, scale=1.0 / D_MODEL,
                                         bias=sh["eps"][:, :]).then_inc(rms_ready, 1)
                for m in range(SLOTS):
                    split_w(m)
                for n in range(NP * KT):
                    act.wait_ge(xn_ready, n + 1)
                    nc.scalar.activation(piece(xn_hi, n % KT, n // KT), xn[:, n % 2, :], ACT.Copy).then_inc(xn_hi_ready, 1)
                for m in range(KT):
                    for q in range(NP):
                        n = NP * m + q
                        act.wait_ge(products, n + 1)
                        if n >= 2:
                            act.wait_ge(residual, n - 1)
                        nc.scalar.activation(gate[:, n % 2, :], p_gate[:, q, 0:PIECE], ACT.Sigmoid).then_inc(gated, 1)
                    if m + SLOTS < KT:
                        split_w(m + SLOTS)
                for t in range(NT):
                    rows = TILES[t][1]
                    bank = p_gate if t % 2 == 0 else p_emb
                    act.wait_ge(turned, t + 1)
                    if t >= 2:
                        act.wait_ge(stored[t % 2], 16 * (t // 2))
                    nc.scalar.copy(rows_io[:rows, t % 2, 0:CH], bank[:rows, 0, :]).then_inc(out_act, 1)

            @block.vector
            def _(dve):
                def split_w(m):
                    dve.wait_ge(w_hi_ready, m + 1)
                    nc.vector.tensor_tensor(w_lo[:, m % SLOTS], w_raw[:, m % SLOTS], w_hi[:, m % SLOTS].bitcast(F32),
                                            ALU.subtract).then_inc(w_lo_ready, 1)

                for t in range(NT):
                    t0, rows = TILES[t]
                    dve.wait_ge(e_hi_ready, t + 1)
                    nc.vector.tensor_tensor(e_lo[:, :, t0:t0 + rows],
                                            p_gate[:, t % NP, 0:PLE].rearrange("p (k m) -> p k m", k=IT)[:, :, 0:rows],
                                            e_hi[:, :, t0:t0 + rows].bitcast(F32), ALU.subtract).then_inc(e_lo_ready, 1)

                def low(n):
                    dve.wait_ge(xn_hi_ready, n + 1)
                    nc.vector.tensor_tensor(piece(xn_lo, n % KT, n // KT), xn[:, n % 2, :],
                                            piece(xn_hi, n % KT, n // KT).bitcast(F32), ALU.subtract).then_inc(xn_lo_ready, 1)

                for n in range(NP * KT):
                    q, k = divmod(n, KT)
                    if k == 0:
                        dve.wait_ge(rms_ready, q + 1)
                        nc.vector.reciprocal(sum_sq[:, q, :], sum_sq[:, q, :]).then_inc(rstd_ready, 1)
                        dve.wait_ge(rstd_ready, q + 1)
                    if n == 2:
                        for m in range(SLOTS):
                            split_w(m)
                    if n >= 2:
                        dve.wait_ge(xn_lo_ready, n - 1)
                    nc.vector.scalar_tensor_tensor(out=xn[:, n % 2, :], in0=piece(x_t, k, q), scalar=gains[:, 3, k:k + 1],
                                                   in1=sum_sq[:, q, :], op0=ALU.mult, op1=ALU.mult).then_inc(xn_ready, 1)
                    if n >= 1:
                        low(n - 1)
                low(NP * KT - 1)
                for m in range(KT):
                    for q in range(NP):
                        n = NP * m + q
                        dve.wait_ge(gated, n + 1)
                        nc.vector.tensor_tensor(gate[:, n % 2, :], gate[:, n % 2, :], p_emb[:, q, 0:PIECE], ALU.mult)\
                            .then_inc(embedded, 1)
                        dve.wait_ge(embedded, n + 1)
                        nc.vector.tensor_tensor(piece(x_t, m, q), piece(x_t, m, q), gate[:, n % 2, :], ALU.add)\
                            .then_inc(residual, 1)
                    if m + SLOTS < KT:
                        split_w(m + SLOTS)
                for t in range(NT):
                    rows = TILES[t][1]
                    bank = p_gate if t % 2 == 0 else p_emb
                    dve.wait_ge(turned, t + 1)
                    if t >= 2:
                        dve.wait_ge(stored[t % 2], 16 * (t // 2))
                    nc.vector.tensor_copy(rows_io[:rows, t % 2, CH:2 * CH], bank[:rows, 1, :]).then_inc(out_dve, 1)


def hymba_step(nc, d, stages=9):
    with ExitStack() as ctx:
        def tensors(stack, shapes):
            return {n: stack.enter_context(nc.sbuf_tensor(n, s, (t or [F32])[0])) for n, (s, *t) in shapes.items()}

        sh = tensors(ctx, {"ident": ([P, P],), "ones": ([P, P],), "logf": ([P, NT, HEADS_A],)})
        first = nc.snapshot_sems()
        norm_and_project(nc, d, sh)
        sh |= tensors(ctx, {"rows_t": ([P, KT, TOK],), "gains": ([P, 4, KT],), "taps": ([P, 4, UT],), "eps": ([P, 1],)})
        with ExitStack() as attention:
            sh |= tensors(attention, {
                "tri": ([P, P],), "ident_bf": ([P, P], BF16), "mask_bf": ([P, P], BF16),
                "neg_slope": ([P, HEADS_B],)})
            with ExitStack() as prompt:
                sh |= tensors(prompt, {"dist": ([P, SEQ],), "log_count": ([P, SEQ],), "neg_c": ([P, HEADS_A, NPT],)})
                if stages >= 2:
                    build_tables(nc, d, sh)
                    prompt_attention(nc, d, sh, "A")
                    prompt_attention(nc, d, sh, "B")
            with ExitStack() as sample:
                rows = [N_NEW, DEC_BATCH, HEADS_A, DEC_SEQ]
                sh |= tensors(sample, {
                    "neg_c_past": ([P, DEC_BATCH, N_PAGES, HEADS_A],), "win_bias": ([P, WIN_ROWS, HEADS_B, DEC_SEQ],),
                    "new_mask": (rows,), "new_count": (rows,), "new_bias_a": (rows,), "new_bias_b": (rows,)})
                if stages >= 3:
                    sample_tables(nc, d, sh)
                    sample_attention(nc, d, sh, "A")
                    sample_attention(nc, d, sh, "B")
        nc.clear_and_free_semaphores(nc.allocated_since(first))
        nc.all_engine_barrier()
        if stages >= 4:
            project_out(nc, d, sh)
            conv_ffn(nc, d, sh)
            embed_and_store(nc, d, sh)


_INS = ['x_prompt', 'x_sample', 'p_prompt', 'p_sample', 'cache_fox_k', 'cache_fox_v', 'cache_fox_logf',
        'cache_win_k', 'cache_win_v', 'state_conv', 'page_table', 'g_attn_pre', 'w_in', 'b_forget', 'w_out',
        'g_attn_post', 'g_ffn_pre', 'w_up', 'conv_w', 'conv_b', 'w_down', 'g_ffn_post', 'g_ple', 'w_ple_gate',
        'w_ple']
_OUTS = [('y_p', (1, SEQ, D_MODEL)), ('y_s', (DEC_BATCH, DEC_SEQ, D_MODEL)),
         ('fk_p', (1, 1, SEQ, KV_A, HEAD)), ('fv_p', (1, 1, SEQ, KV_A, HEAD)), ('fl_p', (1, 1, SEQ, HEADS_A)),
         ('wk_p', (1, 1, SEQ, HEADS_B, HEAD)), ('wv_p', (1, 1, SEQ, HEADS_B, HEAD)), ('cv_p', (1, 1, 2, 2 * D_FF)),
         ('fk_s', (1, DEC_BATCH, DEC_SEQ, KV_A, HEAD)), ('fv_s', (1, DEC_BATCH, DEC_SEQ, KV_A, HEAD)),
         ('fl_s', (1, DEC_BATCH, DEC_SEQ, HEADS_A)),
         ('wk_s', (1, DEC_BATCH, DEC_SEQ, HEADS_B, HEAD)), ('wv_s', (1, DEC_BATCH, DEC_SEQ, HEADS_B, HEAD)),
         ('cv_s', (1, DEC_BATCH, 2, 2 * D_FF))]


def build(nc, args, outs, stages=9):
    d = dict(args)
    for name, shape in _OUTS:
        a = outs[name]
        if name in ('y_p',):
            d[name] = a.rearrange("b s d -> (b s) d")
        elif name == 'y_s':
            d[name] = a.rearrange("b s d -> (b s) d")
        elif name[:2] in ('fk', 'fv', 'wk', 'wv'):
            d[name] = a.rearrange("l b s h e -> (l b s) (h e)")
        elif name[:2] == 'fl':
            d[name] = a.rearrange("l b s h -> (l b s) h")
        else:
            d[name] = a.rearrange("l b s f -> l b s f")
    x_p = args['x_prompt'].rearrange("b s d -> (b s) d")
    x_s = args['x_sample'].rearrange("b s d -> (b s) d")
    d["x"] = lambda t: x_p[t * P:(t + 1) * P, :] if t < NPT else x_s
    d["q_scratch"] = nc.dram_tensor("q_scratch", (TOK, 2 * CH), F32, kind="Internal").ap()
    d["mix_scratch"] = nc.dram_tensor("mix_scratch", (TOK, 2 * CH), F32, kind="Internal").ap()
    hymba_step(nc, d, stages)


def kernel(**inputs):
    import numpy as _np
    import concourse.bacc as _bacc
    from concourse import mybir as _mybir
    from concourse.bass_utils import run_bass_kernel_spmd as _run

    nc = _bacc.Bacc("TRN2", target_bir_lowering=False, num_devices=1)
    arrays, args, outs = {}, {}, {}
    for name in _INS:
        a = _np.ascontiguousarray(inputs[name])
        arrays[f"in_{name}"] = a
        args[name] = nc.dram_tensor(f"in_{name}", a.shape, _mybir.dt.from_np(a.dtype), kind="ExternalInput").ap()
    for name, shape in _OUTS:
        outs[name] = nc.dram_tensor(f"out_{name}", shape, F32, kind="ExternalOutput").ap()
    build(nc, args, outs)
    r = _run(nc, [arrays], core_ids=[0])
    return tuple(r.results[0][f"out_{name}"] for name, _ in _OUTS)
```

```python
import numpy as np
import concourse.bass as bass
from concourse import mybir
from contextlib import ExitStack

F32 = mybir.dt.float32
F32R = mybir.dt.float32r
BF16 = mybir.dt.bfloat16
I32 = mybir.dt.int32
ALU = mybir.AluOpType
ACT = mybir.ActivationFunctionType
AX = mybir.AxisListType
ds = bass.ds

D_MODEL = 1024
SEQ = 1024
DEC_BATCH = 8
DEC_SEQ = 4
PAST_LEN = 4096
PAGE = 128
HEAD = 64
HEADS_A = 8
KV_A = 4
GROUP_A = HEADS_A // KV_A
HEADS_B = 8
WINDOW = 2048
D_FF = 2816
PLE = 256
EPS = 1e-6
SCALE = HEAD ** -0.5
NEG = -1e30
N_PAGES = PAST_LEN // PAGE
GROUPS = DEC_BATCH * N_PAGES // PAGE

P = 128
N_NEW = DEC_BATCH * DEC_SEQ
TOK = SEQ + N_NEW
KT = D_MODEL // P
TILES = [(t * P, P) for t in range(SEQ // P)] + [(SEQ, N_NEW)]
NT = len(TILES)
NPT = SEQ // P
CH = 512
LOGF_COL = 2 * CH
CHUNK_COLS = [0, CH, LOGF_COL + HEADS_A, LOGF_COL + HEADS_A + CH, LOGF_COL + HEADS_A + 2 * CH]
NC = len(CHUNK_COLS)
LOGF_AT = NC - 2
DENSE_ROWS = 4
WIN_ROWS = DENSE_ROWS + (WINDOW - DENSE_ROWS * P) // (P * 16 // DEC_SEQ)
HALF = 2 * P
QB_ORDER = [4, 0, 5, 1, 6, 2, 7, 3]
RMAX = bass.bass_isa.ReduceOp.max


def norm_and_project(nc, d, sh):
    with ExitStack() as ctx:
        sb = lambda n, s, t=F32: ctx.enter_context(nc.sbuf_tensor(n, s, t))
        pb = lambda n, s, t=F32: ctx.enter_context(nc.psum_tensor(n, s, t))
        sem = lambda n: nc.alloc_semaphore(n)
        x_in = sb("p_x_in", [P, 2, D_MODEL])
        gain = sb("p_gain", [P, D_MODEL])
        x_norm = sb("p_x_norm", [P, 2, D_MODEL])
        square = sb("p_square", [P, D_MODEL])
        mean_sq = sb("p_mean_sq", [P, NT])
        rms = sb("p_rms", [P, NT])
        rstd = sb("p_rstd", [P, NT])
        xt_hi = sb("p_xt_hi", [P, KT, TOK], F32R)
        xt_lo = sb("p_xt_lo", [P, KT, TOK], F32R)
        w_raw = sb("p_w_raw", [P, 2, KT, CH])
        w_hi = sb("p_w_hi", [P, 2, KT, CH], F32R)
        w_lo = sb("p_w_lo", [P, 2, KT, CH], F32R)
        wf_raw = sb("p_wf_raw", [P, KT, HEADS_A])
        wf_hi = sb("p_wf_hi", [P, KT, HEADS_A], F32R)
        wf_lo = sb("p_wf_lo", [P, KT, HEADS_A], F32R)
        z_out = sb("p_z_out", [P, 3, CH])
        b_f = sb("p_b_f", [P, HEADS_A])
        lf_pre = sb("p_lf_pre", [P, NT, HEADS_A])
        lf_tmp = sb("p_lf_tmp", [P, NT, HEADS_A])
        lf_min = sb("p_lf_min", [P, NT, HEADS_A])
        pt = pb("p_pt", [P, 2, D_MODEL])
        pz = pb("p_pz", [P, 3, CH])
        pf = pb("p_pf", [P, NT, HEADS_A])

        x_loaded = [sem(f"p_x_loaded{i}") for i in range(2)]
        gain_loaded = sem("p_gain_loaded")
        w_loaded = [sem(f"p_w_loaded{i}") for i in range(2)]
        wf_loaded = sem("p_wf_loaded")
        bf_loaded = sem("p_bf_loaded")
        stored = [sem(f"p_stored{i}") for i in range(3)]
        lf_stored = sem("p_lf_stored")
        squared = sem("p_squared")
        mean_ready = sem("p_mean_ready")
        rooted = sem("p_rooted")
        rstd_ready = sem("p_rstd_ready")
        normed = sem("p_normed")
        transposed = sem("p_transposed")
        hi_ready = sem("p_hi_ready")
        lo_ready = sem("p_lo_ready")
        w_hi_ready = sem("p_w_hi_ready")
        w_lo_ready = sem("p_w_lo_ready")
        wf_hi_ready = sem("p_wf_hi_ready")
        wf_lo_ready = sem("p_wf_lo_ready")
        z_done = sem("p_z_done")
        z_act = sem("p_z_act")
        z_dve = sem("p_z_dve")
        pf_done = sem("p_pf_done")
        lf_step = sem("p_lf_step")
        lf_act = sem("p_lf_act")
        ident_ready = sem("p_ident_ready")

        w_in = d["w_in"][0].rearrange("(k p) n -> p k n", p=P)
        act_tiles = [t for t in range(NT) if t % 2 == 0]
        dve_tiles = [t for t in range(NT) if t % 2 == 1]

        def evacuated(eng, c, t):
            if t % 2 == 0:
                eng.wait_ge(z_act, len(act_tiles) * c + t // 2 + 1)
            else:
                eng.wait_ge(z_dve, len(dve_tiles) * c + t // 2 + 1)

        def rows_of(name_p, name_s, t, c0, cols):
            t0, n = TILES[t]
            return d[name_p][t0:t0 + n, c0:c0 + cols] if t < NPT else d[name_s][0:n, c0:c0 + cols]

        def destinations(c, t):
            if c == 0 or c == 2:
                t0, n = TILES[t]
                return [(0, CH, d["q_scratch"][t0:t0 + n, (c // 2) * CH:(c // 2 + 1) * CH])]
            if c == 1:
                return [(0, CH // 2, rows_of("fk_p", "fk_s", t, 0, CH // 2)),
                        (CH // 2, CH // 2, rows_of("fv_p", "fv_s", t, 0, CH // 2))]
            pair = ("wk_p", "wk_s") if c == 3 else ("wv_p", "wv_s")
            return [(0, CH, rows_of(*pair, t, 0, CH))]

        def store_count(c, t, through):
            n = 0
            for cc in range(c + 1):
                for tt in range(t % 3, NT, 3):
                    if (cc, tt) < (c, t) or (through and (cc, tt) == (c, t)):
                        n += 16 * len(destinations(cc, tt))
            return n

        with nc.Block() as block:
            @block.sync
            def _(sp):
                def load_x(t):
                    t0, n = TILES[t]
                    if t >= 2:
                        sp.wait_ge(normed, t - 1)
                    sp.dma_start(x_in[:n, t % 2, :], d["x"](t)).then_inc(x_loaded[t % 2], 16)

                def load_w(c):
                    if c >= 2:
                        sp.wait_ge(w_hi_ready, c - 1)
                        sp.wait_ge(w_lo_ready, c - 1)
                    sp.dma_start(w_raw[:, c % 2], w_in[:, :, CHUNK_COLS[c]:CHUNK_COLS[c] + CH])\
                        .then_inc(w_loaded[c % 2], 16)

                load_x(0)
                sp.dma_start(gain[:, :], d["g_attn_pre"][0].partition_broadcast(P)).then_inc(gain_loaded, 16)
                load_w(0)
                load_x(1)
                load_x(2)
                load_w(1)
                load_x(3)
                sp.dma_start(wf_raw[:, :, :], w_in[:, :, LOGF_COL:LOGF_COL + HEADS_A]).then_inc(wf_loaded, 16)
                sp.dma_start(b_f[:, :], d["b_forget"][0].partition_broadcast(P)).then_inc(bf_loaded, 16)
                for c in range(NC):
                    for t in range(NT):
                        if t == 4 and c + 2 < NC:
                            load_w(c + 2)
                        evacuated(sp, c, t)
                        for c0, cols, rows in destinations(c, t):
                            sp.dma_start(rows, z_out[:TILES[t][1], t % 3, c0:c0 + cols]).then_inc(stored[t % 3], 16)
                        if c == 0 and t + 4 < NT:
                            load_x(t + 4)
                sp.wait_ge(lf_step, 4)
                sp.dma_start(d["fl_p"].rearrange("(t p) h -> p t h", p=P), sh["logf"][:, 0:NPT, :])\
                    .then_inc(lf_stored, 16)
                sp.dma_start(d["fl_s"], sh["logf"][:N_NEW, NPT, :]).then_inc(lf_stored, 16)
                for s in range(3):
                    sp.wait_ge(stored[s], store_count(NC - 1, NT - 3 + s, True))
                sp.wait_ge(lf_stored, 32)

            @block.gpsimd
            def _(pool):
                nc.gpsimd.memset(sh["ident"][:, :], 0.0).then_inc(ident_ready, 1)
                pool.wait_ge(ident_ready, 1)
                nc.gpsimd.affine_select(out=sh["ident"][:, :], in_=sh["ident"][:, :], compare_op=ALU.not_equal,
                                        fill=1.0, base=0, pattern=[[-1, P]], channel_multiplier=1)\
                    .then_inc(ident_ready, 1)

            @block.scalar
            def _(act):
                def split_w(c):
                    act.wait_ge(w_loaded[c % 2], 16 * (c // 2 + 1))
                    if c >= 2:
                        act.wait_ge(z_done, NT * (c - 1))
                    nc.scalar.activation(w_hi[:, c % 2], w_raw[:, c % 2], ACT.Copy).then_inc(w_hi_ready, 1)

                def evacuate_z(c, t):
                    n = TILES[t][1]
                    act.wait_ge(z_done, NT * c + t + 1)
                    if store_count(c, t, False):
                        act.wait_ge(stored[t % 3], store_count(c, t, False))
                    nc.scalar.copy(z_out[:n, t % 3, :], pz[:n, t % 3, :]).then_inc(z_act, 1)

                def square_tile(t):
                    n = TILES[t][1]
                    act.wait_ge(x_loaded[t % 2], 16 * (t // 2 + 1))
                    nc.scalar.activation(square[:n, :], x_in[:n, t % 2, :], ACT.Square,
                                         accum_out=mean_sq[:n, t:t + 1]).then_inc(squared, 1)
                    act.wait_ge(mean_ready, t + 1)
                    nc.scalar.activation(rstd[:n, t:t + 1], rms[:n, t:t + 1], ACT.Sqrt).then_inc(rooted, 1)

                def split_hi(t):
                    t0, n = TILES[t]
                    act.wait_ge(transposed, t + 1)
                    nc.scalar.activation(xt_hi[:, :, t0:t0 + n],
                                         pt[:, t % 2, :].rearrange("p (k m) -> p k m", k=KT)[:, :, 0:n],
                                         ACT.Copy).then_inc(hi_ready, 1)

                def log_forget():
                    act.wait_ge(lf_step, 2)
                    nc.scalar.activation(lf_tmp[:, :, :], lf_pre[:, :, :], ACT.Abs).then_inc(lf_act, 1)
                    act.wait_ge(lf_act, 1)
                    nc.scalar.activation(lf_tmp[:, :, :], lf_tmp[:, :, :], ACT.Exp, scale=-1.0).then_inc(lf_act, 1)
                    act.wait_ge(lf_act, 2)
                    nc.scalar.activation(lf_tmp[:, :, :], lf_tmp[:, :, :], ACT.Ln, bias=1.0).then_inc(lf_act, 1)

                square_tile(0)
                split_w(0)
                square_tile(1)
                split_hi(0)
                for c in range(NC):
                    for t in range(NT):
                        if c == 0 and t + 2 < NT:
                            square_tile(t + 2)
                        if c == 0 and t + 1 < NT:
                            split_hi(t + 1)
                        if c == 1 and t == 0:
                            act.wait_ge(wf_loaded, 16)
                            nc.scalar.activation(wf_hi[:, :, :], wf_raw[:, :, :], ACT.Copy).then_inc(wf_hi_ready, 1)
                        if t == 2 and c + 1 < NC:
                            split_w(c + 1)
                        if t % 2 == 0:
                            evacuate_z(c, t)
                        if (c, t) == (LOGF_AT, 4):
                            log_forget()

            @block.vector
            def _(dve):
                def split_w(c):
                    dve.wait_ge(w_hi_ready, c + 1)
                    if c >= 2:
                        dve.wait_ge(z_done, NT * (c - 1))
                    nc.vector.tensor_tensor(w_lo[:, c % 2], w_raw[:, c % 2], w_hi[:, c % 2].bitcast(F32),
                                            ALU.subtract).then_inc(w_lo_ready, 1)

                def norm_tile(t):
                    n = TILES[t][1]
                    dve.wait_ge(squared, t + 1)
                    nc.vector.tensor_scalar(rms[:n, t:t + 1], mean_sq[:n, t:t + 1], 1.0 / D_MODEL, EPS,
                                            ALU.mult, ALU.add).then_inc(mean_ready, 1)
                    dve.wait_ge(rooted, t + 1)
                    nc.vector.reciprocal(rstd[:n, t:t + 1], rstd[:n, t:t + 1]).then_inc(rstd_ready, 1)
                    dve.wait_ge(rstd_ready, t + 1)
                    if t == 0:
                        dve.wait_ge(gain_loaded, 16)
                    if t >= 2:
                        dve.wait_ge(transposed, t - 1)
                    nc.vector.scalar_tensor_tensor(out=x_norm[:n, t % 2, :], in0=x_in[:n, t % 2, :],
                                                   scalar=rstd[:n, t:t + 1], in1=gain[:n, :],
                                                   op0=ALU.mult, op1=ALU.mult).then_inc(normed, 1)

                def split_lo(t):
                    t0, n = TILES[t]
                    dve.wait_ge(hi_ready, t + 1)
                    nc.vector.tensor_tensor(xt_lo[:, :, t0:t0 + n],
                                            pt[:, t % 2, :].rearrange("p (k m) -> p k m", k=KT)[:, :, 0:n],
                                            xt_hi[:, :, t0:t0 + n].bitcast(F32), ALU.subtract).then_inc(lo_ready, 1)

                def evacuate_z(c, t):
                    n = TILES[t][1]
                    dve.wait_ge(z_done, NT * c + t + 1)
                    if store_count(c, t, False):
                        dve.wait_ge(stored[t % 3], store_count(c, t, False))
                    nc.vector.tensor_copy(z_out[:n, t % 3, :], pz[:n, t % 3, :]).then_inc(z_dve, 1)

                def log_forget_sum():
                    dve.wait_ge(pf_done, 1)
                    dve.wait_ge(bf_loaded, 16)
                    dve.wait_ge(lf_step, 1)
                    bias = b_f[:, None, :].broadcast_to([P, NT, HEADS_A])
                    nc.vector.tensor_tensor(lf_pre[:, 0:NPT, :], pf[:, 0:NPT, :], bias[:, 0:NPT, :], ALU.add)
                    nc.vector.tensor_tensor(lf_pre[:N_NEW, NPT, :], pf[:N_NEW, NPT, :], bias[:N_NEW, NPT, :], ALU.add)\
                        .then_inc(lf_step, 1)
                    dve.wait_ge(lf_step, 2)
                    nc.vector.tensor_scalar(lf_min[:, :, :], lf_pre[:, :, :], 0.0, None, ALU.min).then_inc(lf_step, 1)

                def log_forget():
                    dve.wait_ge(lf_step, 3)
                    dve.wait_ge(lf_act, 3)
                    nc.vector.tensor_tensor(sh["logf"][:, :, :], lf_min[:, :, :], lf_tmp[:, :, :], ALU.subtract)\
                        .then_inc(lf_step, 1)

                nc.vector.memset(lf_pre[:, :, :], 0.0).then_inc(lf_step, 1)
                norm_tile(0)
                split_w(0)
                norm_tile(1)
                split_lo(0)
                for c in range(NC):
                    for t in range(NT):
                        if c == 0 and t + 2 < NT:
                            norm_tile(t + 2)
                        if c == 0 and t + 1 < NT:
                            split_lo(t + 1)
                        if c == 1 and t == 0:
                            dve.wait_ge(wf_hi_ready, 1)
                            nc.vector.tensor_tensor(wf_lo[:, :, :], wf_raw[:, :, :], wf_hi[:, :, :].bitcast(F32),
                                                    ALU.subtract).then_inc(wf_lo_ready, 1)
                        if t == 3 and c + 1 < NC:
                            split_w(c + 1)
                        if t % 2 == 1:
                            evacuate_z(c, t)
                        if (c, t) == (LOGF_AT, 3):
                            log_forget_sum()
                        if (c, t) == (LOGF_AT, 7):
                            log_forget()

            @block.tensor
            def _(pe):
                def transpose_tile(t):
                    n = TILES[t][1]
                    pe.wait_ge(normed, t + 1)
                    if t >= 2:
                        pe.wait_ge(lo_ready, t - 1)
                    for k in range(KT):
                        last = nc.tensor.transpose(pt[:, t % 2, k * P:k * P + n], x_norm[:n, t % 2, k * P:(k + 1) * P],
                                                   sh["ident"][:n, :n])
                    last.then_inc(transposed, 1)

                def project(c, t, hi, lo, out):
                    t0, n = TILES[t]
                    for k in range(KT):
                        for a, b, part in ((xt_hi, hi, 0), (xt_hi, lo, 1), (xt_lo, hi, 2)):
                            last = nc.tensor.matmul(out, a[:, k, t0:t0 + n], b[:, k, :],
                                                    start=(k == 0 and part == 0), stop=(k == KT - 1 and part == 2))
                    return last

                pe.wait_ge(ident_ready, 2)
                transpose_tile(0)
                for c in range(NC):
                    if c == LOGF_AT:
                        pe.wait_ge(wf_lo_ready, 1)
                        for t in range(NT):
                            last = project(NC, t, wf_hi, wf_lo, pf[:TILES[t][1], t, :])
                        last.then_inc(pf_done, 1)
                    pe.wait_ge(w_lo_ready, c + 1)
                    for t in range(NT):
                        if c == 0:
                            if t + 1 < NT:
                                transpose_tile(t + 1)
                            pe.wait_ge(lo_ready, t + 1)
                        if (c, t) >= (0, 3):
                            evacuated(pe, c if t >= 3 else c - 1, t - 3 if t >= 3 else NT - 3 + t)
                        project(c, t, w_hi[:, c % 2], w_lo[:, c % 2], pz[:TILES[t][1], t % 3, :]).then_inc(z_done, 1)


def build_tables(nc, d, sh):
    with ExitStack() as ctx:
        sb = lambda n, s, t=F32: ctx.enter_context(nc.sbuf_tensor(n, s, t))
        sem = lambda n: nc.alloc_semaphore(n)
        carry = sb("t_carry", [P, HEADS_A, NPT])
        totals = sb("t_totals", [P, HEADS_A, NPT])
        sums = sb("t_sums", [P, HEADS_A, NPT])
        p_within = ctx.enter_context(nc.psum_tensor("t_p_within", [P, HEADS_A, NPT], F32))
        p_totals = ctx.enter_context(nc.psum_tensor("t_p_totals", [P, HEADS_A, NPT], F32))
        pool_step = sem("t_pool_step")
        dve_step = sem("t_dve_step")
        sums_ready = sem("t_sums_ready")

        with nc.Block() as block:
            @block.gpsimd
            def _(pool):
                nc.gpsimd.memset(sh["ones"][:, :], 1.0).then_inc(pool_step, 1)
                nc.gpsimd.memset(sh["ident_bf"][:, :], 0.0).then_inc(pool_step, 1)
                nc.gpsimd.memset(sh["mask_bf"][:, :], 0.0).then_inc(pool_step, 1)
                pool.wait_ge(pool_step, 3)
                nc.gpsimd.affine_select(out=sh["ident_bf"][:, :], in_=sh["ident_bf"][:, :], compare_op=ALU.not_equal,
                                        fill=1.0, base=0, pattern=[[-1, P]], channel_multiplier=1).then_inc(pool_step, 1)
                nc.gpsimd.affine_select(out=sh["tri"][:, :], in_=sh["ones"][:, :], compare_op=ALU.is_ge,
                                        fill=0.0, base=0, pattern=[[1, P]], channel_multiplier=-1).then_inc(pool_step, 1)
                nc.gpsimd.affine_select(out=sh["mask_bf"][:, :], in_=sh["mask_bf"][:, :], compare_op=ALU.is_ge,
                                        fill=NEG, base=0, pattern=[[-1, P]], channel_multiplier=1).then_inc(pool_step, 1)

            @block.tensor
            def _(pe):
                pe.wait_ge(pool_step, 5)
                lf = sh["logf"][:, 0:NPT, :].rearrange("p t h -> p h t")
                nc.tensor.matmul(p_within[:, :, :], sh["tri"][:, :], lf, start=True, stop=True)
                nc.tensor.matmul(p_totals[:, :, :], sh["ones"][:, :], lf, start=True, stop=True).then_inc(sums_ready, 1)

            @block.vector
            def _(dve):
                steps = [0]

                def chained(ins):
                    steps[0] += 1
                    ins.then_inc(dve_step, 1)
                    dve.wait_ge(dve_step, steps[0])

                for h in range(HEADS_B):
                    last = nc.vector.memset(sh["neg_slope"][:, h:h + 1], -2.0 ** (-8.0 * (h + 1) / HEADS_B))
                chained(last)
                chained(nc.vector.memset(carry[:, :, :], 1.0))
                chained(nc.vector.memset(carry[:, :, 0:1], 0.0))
                dve.wait_ge(sums_ready, 1)
                chained(nc.vector.tensor_copy(totals[:, :, :], p_totals[:, :, :]))
                flat = lambda a: a[:, :, :].rearrange("p h t -> p (h t)")
                chained(nc.vector.tensor_tensor_scan(flat(sums), flat(carry), flat(totals), 0.0, ALU.mult, ALU.add))
                chained(nc.vector.tensor_tensor(totals[:, :, :], totals[:, :, :], sums[:, :, :], ALU.subtract))
                chained(nc.vector.tensor_tensor(sh["neg_c"][:, :, :], totals[:, :, :], p_within[:, :, :], ALU.subtract))


def key_tables(nc, sh, kind, scratch, steps_done, measured, masked, clamped, logged):
    g_ = nc.gpsimd
    dist_i, dist, near, term, count = (scratch[n] for n in ("dist_i", "dist", "near", "term", "count"))

    def pool_part(pool):
        steps = [0]

        def chained(ins):
            steps[0] += 1
            ins.then_inc(steps_done, 1)
            pool.wait_ge(steps_done, steps[0])

        if kind == "A":
            chained(g_.iota(dist_i, pattern=[[-1, SEQ]], base=SEQ - P, channel_multiplier=1))
        else:
            new, win = sh["new_mask"], [[0, HEADS_B], [1, DEC_SEQ]]
            res_i, new_dist_i, new_dist = scratch["res_i"], scratch["new_dist_i"], scratch["new_dist"]
            rows = lambda a, r0, r1: a[:, r0 * HEADS_B * DEC_SEQ:r1 * HEADS_B * DEC_SEQ]\
                .rearrange("p (r h j) -> p r h j", h=HEADS_B, j=DEC_SEQ)
            chained(g_.memset(new[:, :, :, :], 0.0))
            chained(g_.iota(rows(dist_i, 0, DENSE_ROWS), pattern=[[-P, DENSE_ROWS]] + win, base=DENSE_ROWS * P,
                            channel_multiplier=-1))
            chained(g_.iota(rows(dist_i, DENSE_ROWS, WIN_ROWS),
                            pattern=[[-CH, WIN_ROWS - DENSE_ROWS], [0, HEADS_B], [DEC_SEQ, DEC_SEQ]],
                            base=WINDOW, channel_multiplier=-DEC_SEQ))
            chained(g_.iota(rows(res_i, 0, WIN_ROWS), pattern=[[0, WIN_ROWS], [0, HEADS_B], [-1, DEC_SEQ]], base=P,
                            channel_multiplier=1))
            chained(g_.iota(new_dist_i, pattern=[[DEC_SEQ, DEC_BATCH]] + win, base=0, channel_multiplier=-1))
            chained(g_.affine_select(out=new[:, :, :, :], in_=new[:, :, :, :], compare_op=ALU.is_ge, fill=NEG, base=0,
                                     pattern=[[DEC_SEQ, DEC_BATCH]] + win, channel_multiplier=-1))
            chained(g_.affine_select(out=new[:, :, :, :], in_=new[:, :, :, :], compare_op=ALU.is_ge, fill=NEG, base=0,
                                     pattern=[[-DEC_SEQ, DEC_BATCH], [0, HEADS_B], [0, DEC_SEQ]], channel_multiplier=1))
            chained(g_.affine_select(out=sh["new_count"][:, :, :, :], in_=new[:, :, :, :], compare_op=ALU.not_equal,
                                     fill=float(np.log(3.0)), base=0, pattern=[[DEC_SEQ, DEC_BATCH]] + win,
                                     channel_multiplier=-1))
            chained(g_.tensor_copy(new_dist, new_dist_i))
        pool.sem_inc(measured, 1)
        chained(g_.tensor_copy(dist, dist_i))
        pool.wait_ge(masked, 1)
        chained(g_.tensor_scalar(count, dist, 128.0, None, ALU.is_le))
        for n, reach in ((3, 512.0), (15, 2048.0)):
            chained(g_.tensor_scalar(near, scratch[f"low_{n}"], 0.0, None, ALU.is_equal))
            chained(g_.tensor_scalar(term, dist, reach, None, ALU.is_le))
            chained(g_.tensor_tensor(term, term, near, ALU.mult))
            chained(g_.tensor_tensor(count, count, term, ALU.add))
        if kind == "A":
            chained(g_.tensor_scalar(term, dist, 0.0, None, ALU.is_ge))
            chained(g_.tensor_tensor(count, count, term, ALU.mult))
        else:
            c0 = DENSE_ROWS * HEADS_B * DEC_SEQ
            chained(g_.tensor_scalar(term, scratch["low_res"], 0.0, None, ALU.is_equal))
            chained(g_.tensor_tensor(count[:, c0:], count[:, c0:], term[:, c0:], ALU.mult))
        chained(g_.tensor_scalar(near, count, 1.0, None, ALU.max))
        pool.sem_inc(clamped, 1)
        chained(g_.tensor_scalar(term, count, 0.0, NEG, ALU.is_equal, ALU.mult))
        pool.wait_ge(logged, 1)
        if kind == "A":
            chained(g_.tensor_tensor(sh["log_count"][:, :], near, term, ALU.add))
            return
        chained(g_.tensor_tensor(count, near, term, ALU.add))
        for h in range(HEADS_B):
            view = lambda a: a.rearrange("p (r h j) -> p r h j", h=HEADS_B, j=DEC_SEQ)[:, :, h, :]
            new_view = lambda a: a[:, :, h, :]
            chained(g_.tensor_scalar(view(term), view(dist), sh["neg_slope"][:, h:h + 1], None, ALU.mult))
            chained(g_.tensor_tensor(sh["win_bias"][:, :, h, :], view(term), view(count), ALU.add))
            chained(g_.tensor_scalar(new_view(new_dist), new_view(new_dist), sh["neg_slope"][:N_NEW, h:h + 1], None,
                                     ALU.mult))
            chained(g_.tensor_tensor(sh["new_bias_b"][:, :, h, :], new_view(new_dist),
                                     sh["new_count"][:, :, h, :], ALU.add))

    def dve_part(dve):
        dve.wait_ge(measured, 1)
        masks = [("low_3", dist_i, 3), ("low_15", dist_i, 15)] + ([("low_res", scratch["res_i"], 3)] if kind == "B" else [])
        for name, src, mask in masks:
            ins = nc.vector.tensor_scalar(scratch[name], src, mask, None, ALU.bitwise_and)
        ins.then_inc(masked, 1)

    def act_part(act):
        act.wait_ge(clamped, 1)
        nc.scalar.activation(near, near, ACT.Ln).then_inc(logged, 1)

    return pool_part, act_part, dve_part


def prompt_attention(nc, d, sh, kind):
    NK = 1 if kind == "A" else 2
    KW = NK * HEAD
    PAIRS = 4
    UNITS = 2 * NPT
    ALL = PAIRS * UNITS
    ORDER = QB_ORDER
    COPIES = 2 // NK
    TILE0 = 0 if kind == "A" else CH // P
    col0 = 0 if kind == "A" else CH
    with ExitStack() as ctx:
        n_ = kind.lower() + "_"
        sb = lambda n, s, t=F32: ctx.enter_context(nc.sbuf_tensor(n_ + n, s, t))
        pb = lambda n, s, t=F32: ctx.enter_context(nc.psum_tensor(n_ + n, s, t))
        sem = lambda n: nc.alloc_semaphore(n_ + n)
        q_raw = sb("q_raw", [P, NPT, 2, HEAD])
        k_raw = sb("k_raw", [P, NPT, NK, HEAD])
        v_raw = sb("v_raw", [P, 2, NPT, 2 * HEAD])
        q_parts = sb("q_parts", [P, NPT, 2, 2, HEAD])
        k_high = sb("k_high", [P, NPT, NK, 2, HEAD])
        k_low = sb("k_low", [P, NPT, NK, 2, HEAD])
        diag = sb("diag", [P, 2, NPT, P]) if kind == "A" else None
        q_t = sb("q_t", [P, 2, 2, SEQ], F32R)
        kh_t = sb("kh_t", [P, 2, NK, SEQ], F32R)
        kl_t = sb("kl_t", [P, 2, NK, SEQ], F32R)
        bias = sb("bias", [P, 2, 2, SEQ])
        probs = sb("probs", [P, 4, SEQ])
        probs_t = sb("probs_t", [P, 2, NPT, 2, P])
        neg_max = sb("neg_max", [P, 4])
        denom = sb("denom", [P, 4])
        recip = sb("recip", [P, 4])
        p_scores = pb("p_scores", [P, 2, SEQ])
        p_turn = pb("p_turn", [P, 2, CH])
        p_out = pb("p_out", [P, 2, CH])

        q_loaded, k_loaded, v_loaded = sem("q_loaded"), sem("k_loaded"), sem("v_loaded")
        high_ready, low_ready = sem("high_ready"), sem("low_ready")
        diag_ready = sem("diag_ready")
        turned = sem("turned")
        turn_act, turn_dve = sem("turn_act"), sem("turn_dve")
        scored, biased, exped = sem("scored"), sem("biased"), sem("exped")
        summed = sem("summed")
        normed = sem("normed")
        weighed = sem("weighed")
        out_read = sem("out_read")
        ids_loaded = sem("ids_loaded")
        if kind == "A":
            flat = lambda n, t=F32: sb(n, [P, SEQ], t)[:, :]
            scratch = {"dist": sh["dist"][:, :]}
        else:
            flat = lambda n, t=F32: sb(n, [P, WIN_ROWS * HEADS_B * DEC_SEQ], t)[:, :]
            scratch = {"dist": flat("table_dist"), "res_i": flat("res_i", I32),
                       "low_res": flat("low_res", I32)}
            for n, t in (("new_dist_i", I32), ("new_dist", F32)):
                scratch[n] = sb(n, [N_NEW, DEC_BATCH, HEADS_B, DEC_SEQ], t)[:, :, :, :]
        scratch |= {"dist_i": flat("dist_i", I32), "low_3": flat("low_3", I32), "low_15": flat("low_15", I32), "near": flat("near"),
                    "term": flat("term"), "count": flat("count")}
        pool_tables, act_tables, dve_tables = key_tables(nc, sh, kind, scratch, sem("table_steps"), sem("measured"),
                                                         sem("masked"), sem("clamped"), sem("logged"))

        stack_events = [("q", h, half) for h in range(2) for half in range(2)]
        stack_events += [(part, h, half) for part in ("kh", "kl") for h in range(NK) for half in range(2)]
        if kind == "A":
            stack_events += [("bias", h, half) for h in range(2) for half in range(2)]
        NS = len(stack_events)

        def unit(u):
            i, v = divmod(u, UNITS)
            return i, v % 2, ORDER[v // 2], u // 2

        events, step_events, stack_end = [], [], {}
        STACK_STEPS = (3, 3, 4, 5, 5, 6, 7, 7, 8, 9, 10, 11)
        for s in stack_events:
            events.append((0,) + s)
        stack_end[0] = len(events) - 1
        for u in range(ALL):
            i, h, qb, _ = unit(u)
            mine = []
            for b0 in range(0, qb + 1, 4):
                mine.append(len(events))
                events.append((u, b0, min(4, qb + 1 - b0)))
            for s, step in enumerate(STACK_STEPS):
                if i + 1 < PAIRS and step == u % UNITS:
                    mine.append(len(events))
                    events.append((i + 1,) + stack_events[s])
                    stack_end[i + 1] = len(events) - 1
            step_events.append(mine)
        assert NS == len(STACK_STEPS)
        groups_of = lambda u: [e for e in step_events[u] if len(events[e]) == 3]

        def wait_read(eng, e):
            eng.wait_ge(turn_act if e % 2 == 0 else turn_dve, e // 2 + 1)

        def wait_stacks(eng, i):
            wait_read(eng, stack_end[i])
            wait_read(eng, stack_end[i] - 1)

        def evacuate(eng, e, copy):
            eng.wait_ge(turned, e + 1)
            if len(events[e]) == 3:
                u, b0, nb = events[e]
                _, h, _, block = unit(u)
                if block >= 2:
                    eng.wait_ge(weighed, block - 1)
                ins = copy(probs_t[:, block % 2, b0:b0 + nb, h, :],
                           p_turn[:, e % 2, 0:nb * P].rearrange("p (b q) -> p b q", q=P))
            else:
                i, what, h, half = events[e]
                to = {"q": q_t, "kh": kh_t, "kl": kl_t, "bias": bias}[what]
                ins = copy(to[:, i % 2, h, half * CH:(half + 1) * CH], p_turn[:, e % 2, :])
            ins.then_inc(turn_act if e % 2 == 0 else turn_dve, 1)

        with nc.Block() as block:
            @block.sync
            def _(sp):
                kv = ("fk_p", "fv_p") if kind == "A" else ("wk_p", "wv_p")
                for i in range(PAIRS):
                    if i >= 1:
                        sp.wait_ge(high_ready, 2 * i)
                        sp.wait_ge(low_ready, 2 * i)
                    sp.dma_start(q_raw[:, :, :, :].rearrange("p t h e -> p t (h e)"),
                                 d["q_scratch"][0:SEQ, col0 + i * P:col0 + (i + 1) * P]
                                 .rearrange("(t p) e -> p t e", p=P)).then_inc(q_loaded, 16)
                    sp.dma_start(k_raw[:, :, :, :].rearrange("p t h e -> p t (h e)"),
                                 d[kv[0]][:, i * KW:(i + 1) * KW].rearrange("(t p) e -> p t e", p=P))\
                        .then_inc(k_loaded, 16)
                    if i >= 1:
                        sp.wait_ge(v_loaded, 16 * COPIES * i)
                    if i >= 2:
                        sp.wait_ge(weighed, NPT * (i - 1))
                    for c in range(COPIES):
                        sp.dma_start(v_raw[:, i % 2, :, c * KW:(c + 1) * KW],
                                     d[kv[1]][:, i * KW:(i + 1) * KW].rearrange("(t p) e -> p t e", p=P))\
                            .then_inc(v_loaded, 16)

            @block.gpsimd
            def _(pool):
                if kind == "B":
                    seqs = DEC_BATCH // GROUPS
                    for g in range(GROUPS):
                        pool.dma_start(sh["page_ids"][:, g:g + 1], d["page_table"][g * seqs:(g + 1) * seqs, :]
                                       .rearrange("b (j o) -> (b j) o", o=1)).then_inc(ids_loaded, 16)
                    pool.wait_ge(ids_loaded, 16 * GROUPS)
                    for g in range(GROUPS):
                        nc.gpsimd.indirect_dma_start(
                            out=sh["pages"][:, g, :], out_offset=None,
                            in_=d["cache_fox_logf"][0].rearrange("n s h -> n (s h)"),
                            in_offset=bass.IndirectOffsetOnAxis(ap=sh["page_ids"][:, g:g + 1], axis=0),
                            bounds_check=d["cache_fox_logf"].shape[1] - 1).then_inc(sh["pages_loaded"][g], 16)
                pool_tables(pool)

            @block.scalar
            def _(act):
                def split_q(i):
                    act.wait_ge(q_loaded, 16 * (i + 1))
                    if i >= 1:
                        act.wait_ge(turned, stack_end[i - 1] + 1)
                    nc.scalar.activation(q_parts[:, :, :, 0, :].bitcast(F32R), q_raw[:, :, :, :], ACT.Copy, scale=SCALE)\
                        .then_inc(high_ready, 1)

                def split_k(i):
                    act.wait_ge(k_loaded, 16 * (i + 1))
                    for t in range(2):
                        ins = nc.scalar.activation(k_high[:, :, :, t, :].bitcast(F32R), k_raw[:, :, :, :], ACT.Copy)
                    ins.then_inc(high_ready, 1)

                def exp(u):
                    n = (unit(u)[2] + 1) * P
                    act.wait_ge(biased, u + 1)
                    nc.scalar.activation(probs[:, u % 4, 0:n], probs[:, u % 4, 0:n], ACT.Exp,
                                         bias=neg_max[:, u % 4:u % 4 + 1], scale=-1.0,
                                         accum_out=denom[:, u % 4:u % 4 + 1]).then_inc(exped, 1)

                def read_out(n):
                    i, _, qb, _ = unit(2 * n)
                    act.wait_ge(weighed, n + 1)
                    for h in range(2):
                        part = slice(h * HEAD, (h + 1) * HEAD)
                        ins = nc.scalar.activation(sh["rows_t"][part, TILE0 + i, qb * P:(qb + 1) * P],
                                                   p_out[part, n % 2, h * P:(h + 1) * P], ACT.Copy)
                    ins.then_inc(out_read, 1)

                split_q(0)
                split_k(0)
                for e in range(0, NS, 2):
                    evacuate(act, e, nc.scalar.copy)
                for u in range(ALL + 2):
                    if u < ALL:
                        exp(u)
                        i, v = divmod(u, UNITS)
                        if u == ALL - UNITS:
                            act_tables(act)
                        if v == 0 and i + 1 < PAIRS:
                            split_q(i + 1)
                        if v == 1 and i + 1 < PAIRS:
                            split_k(i + 1)
                    if u >= 2:
                        for e in step_events[u - 2]:
                            if e % 2 == 0:
                                evacuate(act, e, nc.scalar.copy)
                    if u >= 5 and u % 2 == 1:
                        read_out((u - 5) // 2)
                for n in range((ALL + 1 - 5) // 2 + 1, ALL // 2):
                    read_out(n)

            @block.vector
            def _(dve):
                def split_q(i):
                    dve.wait_ge(high_ready, 2 * i + 1)
                    nc.vector.scalar_tensor_tensor(out=q_parts[:, :, :, 1, :].bitcast(F32R), in0=q_raw[:, :, :, :],
                                                   scalar=SCALE, in1=q_parts[:, :, :, 0, :], op0=ALU.mult,
                                                   op1=ALU.subtract).then_inc(low_ready, 1)

                def split_k(i):
                    dve.wait_ge(high_ready, 2 * i + 2)
                    for t in range(2):
                        ins = nc.vector.tensor_tensor(k_low[:, :, :, t, :].bitcast(F32R), k_raw[:, :, :, :],
                                                      k_high[:, :, :, t, :], ALU.subtract)
                    ins.then_inc(low_ready, 1)

                def make_bias(i, h):
                    if kind == "A":
                        ins = nc.vector.tensor_tensor(
                            diag[:, h], sh["ident"][:, None, :].broadcast_to([P, NPT, P]),
                            sh["neg_c"][:, 2 * i + h, :][:, :, None].broadcast_to([P, NPT, P]), ALU.mult)
                    else:
                        ins = nc.vector.scalar_tensor_tensor(
                            out=bias[:, i % 2, h, :], in0=sh["dist"][:, :],
                            scalar=sh["neg_slope"][:, 2 * i + h:2 * i + h + 1],
                            in1=sh["log_count"][:, :], op0=ALU.mult, op1=ALU.add)
                    ins.then_inc(diag_ready, 1)

                def bias_unit(u):
                    i, h, qb, _ = unit(u)
                    n = (qb + 1) * P
                    b0 = 0 if kind == "A" else SEQ - n
                    if u % UNITS == 0:
                        wait_stacks(dve, i)
                        dve.wait_ge(diag_ready, 2 * (i + 1))
                    if u >= 4:
                        dve.wait_ge(turned, groups_of(u - 4)[-1] + 1)
                    dve.wait_ge(scored, u + 1)
                    nc.vector.tensor_tensor_reduce(out=probs[:, u % 4, 0:n], in0=p_scores[:, u % 2, 0:n],
                                                   in1=bias[:, i % 2, h, b0:b0 + n], scale=-1.0, scalar=3e38,
                                                   op0=ALU.add, op1=ALU.min,
                                                   accum_out=neg_max[:, u % 4:u % 4 + 1]).then_inc(biased, 1)

                def normalise(u):
                    n = (unit(u)[2] + 1) * P
                    dve.wait_ge(exped, u + 1)
                    nc.vector.reciprocal(recip[:, u % 4:u % 4 + 1], denom[:, u % 4:u % 4 + 1]).then_inc(summed, 1)
                    dve.wait_ge(summed, u + 1)
                    nc.vector.tensor_scalar(probs[:, u % 4, 0:n], probs[:, u % 4, 0:n], recip[:, u % 4:u % 4 + 1],
                                            None, ALU.mult).then_inc(normed, 1)

                split_q(0)
                split_k(0)
                make_bias(0, 0)
                make_bias(0, 1)
                for e in range(1, NS, 2):
                    evacuate(dve, e, nc.vector.tensor_copy)
                for u in range(ALL + 2):
                    i, v = divmod(u, UNITS)
                    if u < ALL:
                        bias_unit(u)
                    if 1 <= u <= ALL:
                        normalise(u - 1)
                    if u == UNITS:
                        dve_tables(dve)
                    if i + 1 < PAIRS:
                        if v == 1:
                            split_q(i + 1)
                        if v == 2:
                            split_k(i + 1)
                        if v in (4, 6):
                            if v == 4 and kind == "A":
                                dve.wait_ge(turned, stack_end[i] + 1)
                            make_bias(i + 1, (v - 4) // 2)
                    if u >= 2:
                        for e in step_events[u - 2]:
                            if e % 2 == 1:
                                evacuate(dve, e, nc.vector.tensor_copy)

            @block.tensor
            def _(pe):
                def stack(e):
                    i, what, h, half = events[e]
                    if e >= 2:
                        wait_read(pe, e - 2)
                    if what == "bias":
                        pe.wait_ge(diag_ready, 2 * i + h + 1)
                        nc.tensor.matmul(p_turn[:, e % 2, :], sh["ones"][:, :],
                                         diag[:, h, half * 4:(half + 1) * 4, :].rearrange("p t m -> p (t m)"),
                                         start=True, stop=True).then_inc(turned, 1)
                        return
                    pe.wait_ge(low_ready, 2 * i + (1 if what == "q" else 2))
                    src = {"q": q_parts, "kh": k_high, "kl": k_low}[what]
                    for j in range(4):
                        last = nc.tensor.transpose(p_turn[:, e % 2, j * P:(j + 1) * P],
                                                   src[:, half * 4 + j, h].rearrange("p s e -> p (s e)"),
                                                   sh["ident"][:, :])
                    last.then_inc(turned, 1)

                def score(u):
                    i, h, qb, _ = unit(u)
                    n = (qb + 1) * P
                    if u % UNITS == 0:
                        wait_stacks(pe, i)
                    if u >= 2:
                        pe.wait_ge(biased, u - 1)
                    for c0 in range(0, n, CH):
                        c1 = min(n, c0 + CH)
                        masked = kind == "A" and c1 == n
                        for part, k_t in enumerate((kh_t, kl_t)):
                            last = nc.tensor.matmul(p_scores[:, u % 2, c0:c1], q_t[:, i % 2, h, qb * P:(qb + 1) * P],
                                                    k_t[:, i % 2, h % NK, c0:c1], start=(part == 0),
                                                    stop=(part == 1 and not masked))
                        if masked:
                            last = nc.tensor.matmul(p_scores[:, u % 2, n - P:n], sh["ident_bf"][:, :],
                                                    sh["mask_bf"][:, :], start=False, stop=True)
                    last.then_inc(scored, 1)

                def turn(u):
                    pe.wait_ge(normed, u + 1)
                    for e in groups_of(u):
                        _, b0, nb = events[e]
                        if e >= 2:
                            wait_read(pe, e - 2)
                        for j in range(nb):
                            last = nc.tensor.transpose(p_turn[:, e % 2, j * P:(j + 1) * P],
                                                       probs[:, u % 4, (b0 + j) * P:(b0 + j + 1) * P],
                                                       sh["ident"][:, :])
                        last.then_inc(turned, 1)

                def weigh(n, half):
                    i, _, qb, _ = unit(2 * n)
                    blocks = range(qb + 1)
                    if half == 0:
                        if n % NPT == 0:
                            pe.wait_ge(v_loaded, 16 * COPIES * (i + 1))
                        if n >= 2:
                            pe.wait_ge(out_read, n - 1)
                        for e in groups_of(2 * n) + groups_of(2 * n + 1):
                            wait_read(pe, e)
                    for b in blocks[:qb // 2 + 1] if half == 0 else blocks[qb // 2 + 1:]:
                        last = nc.tensor.matmul(p_out[:, n % 2, 0:2 * P], v_raw[:, i % 2, b, :],
                                                probs_t[:, n % 2, b, :, :], start=(b == 0), stop=(b == qb))
                        if b == qb:
                            last.then_inc(weighed, 1)

                for e in range(NS):
                    stack(e)
                score(0)
                score(1)
                for u in range(ALL):
                    if u + 2 < ALL:
                        score(u + 2)
                    if u >= 3:
                        weigh((u - 3) // 2, (u - 3) % 2)
                    turn(u)
                    for e in step_events[u]:
                        if len(events[e]) == 4:
                            stack(e)
                weigh(ALL // 2 - 2, 1)
                weigh(ALL // 2 - 1, 0)
                weigh(ALL // 2 - 1, 1)


def sample_tables(nc, d, sh):
    SEQS = DEC_BATCH // GROUPS
    RUNS = GROUPS * HEADS_A * SEQS
    with ExitStack() as ctx:
        sb = lambda n, s, t=F32: ctx.enter_context(nc.sbuf_tensor("c_" + n, s, t))
        pb = lambda n, s, t=F32: ctx.enter_context(nc.psum_tensor("c_" + n, s, t))
        sem = lambda n: nc.alloc_semaphore("c_" + n)
        pages, pages_loaded = sh["pages"], sh["pages_loaded"]
        by_pos = sb("by_pos", [P, GROUPS, HEADS_A, P])
        totals = sb("totals", [P, RUNS, N_PAGES])
        sums = sb("sums", [P, RUNS, N_PAGES])
        carry = sb("carry", [P, RUNS, N_PAGES])
        same = sb("same", [N_NEW, N_NEW])
        own = sb("own", [N_NEW, DEC_BATCH])
        past = sb("past", [N_NEW, HEADS_A, DEC_BATCH])
        past_sum = sb("past_sum", [N_NEW, HEADS_A])
        neg_new = sb("neg_new", [N_NEW, HEADS_A])
        p_big = pb("p_big", [P, 4 * CH])
        p_sum = pb("p_sum", [P, 4 * CH])
        pool_step, dve_step, act_step, pe_step = sem("pool_step"), sem("dve_step"), sem("act_step"), sem("pe_step")

        with nc.Block() as block:
            @block.gpsimd
            def _(pool):
                g_ = nc.gpsimd
                g_.memset(same[:, :], 1.0).then_inc(pool_step, 1)
                g_.memset(own[:, :], 1.0).then_inc(pool_step, 1)
                pool.wait_ge(pool_step, 2)
                g_.affine_select(out=same[:, :], in_=same[:, :], compare_op=ALU.is_ge, fill=0.0, base=0,
                                 pattern=[[1, N_NEW]], channel_multiplier=-1).then_inc(pool_step, 1)
                g_.affine_select(out=own[:, :], in_=own[:, :], compare_op=ALU.is_ge, fill=0.0, base=0,
                                 pattern=[[-DEC_SEQ, DEC_BATCH]], channel_multiplier=1).then_inc(pool_step, 1)
                pool.wait_ge(pool_step, 4)
                g_.affine_select(out=same[:, :], in_=same[:, :], compare_op=ALU.is_ge, fill=0.0, base=0,
                                 pattern=[[-DEC_SEQ, DEC_BATCH], [0, DEC_SEQ]], channel_multiplier=1).then_inc(pool_step, 1)
                g_.affine_select(out=own[:, :], in_=own[:, :], compare_op=ALU.is_ge, fill=0.0, base=DEC_SEQ - 1,
                                 pattern=[[DEC_SEQ, DEC_BATCH]], channel_multiplier=-1).then_inc(pool_step, 1)

            @block.tensor
            def _(pe):
                for g in range(GROUPS):
                    pe.wait_ge(pages_loaded[g], 16)
                    for h in range(HEADS_A):
                        e = g * HEADS_A + h
                        last = nc.tensor.transpose(p_big[:, e * P:(e + 1) * P], pages[:, g, h::HEADS_A],
                                                   sh["ident"][:, :])
                last.then_inc(pe_step, 1)
                pe.wait_ge(act_step, 1)
                for m, out in ((sh["ones"], p_sum), (sh["tri"], p_big)):
                    for j in range(4):
                        last = nc.tensor.matmul(out[:, j * CH:(j + 1) * CH], m[:, :],
                                                by_pos[:, :, :, :].rearrange("p g h n -> p (g h n)")[:, j * CH:(j + 1) * CH],
                                                start=True, stop=True)
                    last.then_inc(pe_step, 1)
                pe.wait_ge(dve_step, 2)
                pe.wait_ge(pool_step, 6)
                nc.tensor.matmul(p_sum[:N_NEW, 0:HEADS_A], same[:, :], sh["logf"][:N_NEW, NPT, :],
                                 start=True, stop=True).then_inc(pe_step, 1)

            @block.scalar
            def _(act):
                act.wait_ge(pe_step, 1)
                nc.scalar.copy(by_pos[:, :, :, :].rearrange("p g h n -> p (g h n)"),
                               p_big[:, :]).then_inc(act_step, 1)

            @block.vector
            def _(dve):
                steps = [0]

                def chained(ins):
                    steps[0] += 1
                    ins.then_inc(dve_step, 1)
                    dve.wait_ge(dve_step, steps[0])

                chained(nc.vector.memset(carry[:, :, :], 1.0))
                dve.wait_ge(pe_step, 2)
                chained(nc.vector.tensor_copy(totals[:, :, :].rearrange("p r n -> p (r n)"),
                                              p_sum[:, :]))
                chained(nc.vector.memset(carry[:, :, 0:1], 0.0))
                flat = lambda a: a[:, :, :].rearrange("p r n -> p (r n)")
                chained(nc.vector.tensor_tensor_scan(flat(sums), flat(carry), flat(totals), 0.0, ALU.mult, ALU.add))
                chained(nc.vector.tensor_tensor(totals[:, :, :], totals[:, :, :], sums[:, :, :], ALU.subtract))
                dve.wait_ge(pe_step, 3)
                view = "p (g h b) n -> p g h b n"
                tot_v = totals[:, :, :].rearrange(view, g=GROUPS, h=HEADS_A)
                sum_v = sums[:, :, :].rearrange(view, g=GROUPS, h=HEADS_A)
                in_v = p_big[:, :].rearrange("p (g h b n) -> p g h b n", g=GROUPS, h=HEADS_A, n=N_PAGES)
                for g in range(GROUPS):
                    for b in range(SEQS):
                        last = nc.vector.tensor_tensor(
                            sh["neg_c_past"][:, g * SEQS + b, :, :].rearrange("p n h -> p h n"),
                            tot_v[:, g, :, b, :], in_v[:, g, :, b, :], ALU.subtract)
                chained(last)
                dve.wait_ge(pool_step, 6)
                for g in range(GROUPS):
                    last = nc.vector.tensor_tensor(
                        past[:, :, g * SEQS:(g + 1) * SEQS], sum_v[:N_NEW, g, :, :, N_PAGES - 1],
                        own[:, None, g * SEQS:(g + 1) * SEQS].broadcast_to([N_NEW, HEADS_A, SEQS]), ALU.mult)
                chained(last)
                chained(nc.vector.tensor_reduce(past_sum[:, :], past[:, :, :], AX.X, ALU.add))
                dve.wait_ge(pe_step, 4)
                chained(nc.vector.scalar_tensor_tensor(out=neg_new[:, :], in0=p_sum[:N_NEW, 0:HEADS_A], scalar=-1.0,
                                                       in1=past_sum[:, :], op0=ALU.mult, op1=ALU.subtract))
                for b in range(DEC_BATCH):
                    last = nc.vector.tensor_tensor(sh["new_bias_a"][:, b], sh["new_mask"][:, b],
                                                   neg_new[:, :, None].broadcast_to([N_NEW, HEADS_A, DEC_SEQ]), ALU.add)
                chained(last)


def sample_attention(nc, d, sh, kind):
    A = kind == "A"
    ROWS = N_PAGES // 2 if A else WIN_ROWS
    KEYSETS = N_PAGES if A else WIN_ROWS
    PAIRS = KV_A // 2 if A else HEADS_B // 2
    G = GROUP_A if A else 1
    QC = 2 * G * DEC_SEQ
    QN = PAIRS * QC
    KW = PAIRS * P
    HALVES = KW // HALF
    col0 = 0 if A else CH
    TURNS = DEC_BATCH // 2
    with ExitStack() as ctx:
        n_ = "d" + kind.lower() + "_"
        sb = lambda n, s, t=F32: ctx.enter_context(nc.sbuf_tensor(n_ + n, s, t))
        pb = lambda n, s, t=F32: ctx.enter_context(nc.psum_tensor(n_ + n, s, t))
        sem = lambda n: nc.alloc_semaphore(n_ + n)
        K_RING = ROWS if A else 2 * ROWS
        k_in = sb("k_in", [P, K_RING, CH])
        v_in = sb("v_in", [P, 2, KEYSETS, HALVES, HALF + 1])
        k_t = sb("k_t", [P, 2, CH])
        table = sb("table", [1, DEC_BATCH * N_PAGES], I32)
        q_in = sb("q_in", [N_NEW, CH])
        k_new = sb("k_new", [N_NEW, KW])
        v_new = sb("v_new", [N_NEW, HALVES, HALF + 1])
        k_new_t = sb("k_new_t", [P, PAIRS, N_NEW])
        QW = QN if A else QC
        q_blocks = sb("q_blocks", [P, DEC_BATCH, PAIRS, QW])
        if A:
            q_now = sb("q_now", [P, 2, PAIRS, QN])
            by_query = sb("by_query", [QN, 2, 2 * P])
        logits = sb("logits", [P, 2, KEYSETS + 1, QN])
        probs = sb("probs", [P, 2, KEYSETS + 1, QN])
        part_max = sb("part_max", [P, 2, QN])
        all_max = sb("all_max", [P, 2, QN])
        recip = sb("recip", [QN, 2, HALVES])
        out_all = sb("out_all", [QN, DEC_BATCH, HALVES, HALF])
        p_scores = pb("p_scores", [P, 1 if A else 2, KEYSETS * QN if A else CH])
        p_query = pb("p_query", [P, 2, CH]) if A else None
        p_turn = pb("p_turn", [P, 2, CH])
        p_side = pb("p_side", [P, 2, CH])
        p_outs = [p_side] + [pb(f"p_out{f}", [P, 2, CH]) for f in range(1, HALVES)]

        setup_loaded, table_loaded = sem("setup_loaded"), sem("table_loaded")
        BATCH = ROWS // 4 if A else ROWS
        k_loaded = [sem(f"k_loaded{s}") for s in range(K_RING // BATCH)]
        v_loaded = [sem(f"v_loaded{s}") for s in range(2)]
        set_pe, set_dve = sem("set_pe"), sem("set_dve")
        turned = sem("turned")
        turn_act, turn_dve = sem("turn_act"), sem("turn_dve")
        scored = sem("scored")
        q_ready = sem("q_ready")
        row_scored = sem("row_scored")
        row_read = sem("row_read")
        row_back = sem("row_back")
        biased = sem("biased")
        maxed = sem("maxed")
        max_spread = sem("max_spread")
        shifted = sem("shifted")
        exped = sem("exped")
        ones_ready = sem("ones_ready")
        weighed = sem("weighed")
        recip_ready = sem("recip_ready")
        out_ready = sem("out_ready")
        spare = sem("spare")
        stored = sem("stored")
        K_LOADS = 16 * (2 * BATCH if A else ROWS)
        V_LOADS = 16 * (2 * ROWS if A else DENSE_ROWS + HALVES * (ROWS - DENSE_ROWS))

        q0 = lambda pair: pair * QC if A else 0

        def block_of(r, i):
            return (i % PAIRS, 2 * r + i // PAIRS) if A else (i, r)

        def load_pages(eng, i, b, cache):
            keys = cache == "cache_fox_k"
            for r0 in range(0, ROWS, BATCH):
                n = b * ROWS + r0
                if keys:
                    eng.wait_ge(turned, 2 * ROWS * i + n + BATCH)
                    eng.sem_inc(spare, 1)
                elif r0 == 0:
                    eng.wait_ge(weighed, 2 * i + b + 1)
                    eng.sem_inc(spare, 1)
                _, ids = nc.values_load_multi_w_load_instructions(
                    table[0:1, ds(2 * N_PAGES * i + 2 * n, 2 * BATCH)], engines=[eng.engine],
                    min_val=0, max_val=d[cache].shape[1] - 1)
                for e in range(2 * BATCH):
                    row, half = n + e // 2, e % 2
                    dst = k_in[:, row % K_RING, half * KW:(half + 1) * KW] if keys else v_in[:, b, row % ROWS * 2 + half, 0, 0:HALF]
                    done = k_loaded[n % K_RING // BATCH] if keys else v_loaded[b]
                    src = d[cache][0].rearrange("n s h e -> n s (h e)")[ds(ids[e], 1)].rearrange("o s e -> (o s) e")
                    eng.dma_start(dst, src).then_inc(done, 16)

        def load_window(eng, i, b, cache):
            keys = cache == "cache_win_k"
            if keys:
                eng.wait_ge(turned, 2 * ROWS * i + (b + 1) * ROWS)
            else:
                eng.wait_ge(weighed, 2 * i + b + 1)
            eng.sem_inc(spare, 1)
            src = d[cache][0].rearrange("b s h e -> b s (h e)")[ds(2 * i + b, 1)].rearrange("o s e -> (o s) e")
            for c in range(ROWS):
                if c < DENSE_ROWS:
                    r0 = WINDOW - (DENSE_ROWS - c) * P
                    rows = src[r0:r0 + P, :]
                else:
                    r0 = (c - DENSE_ROWS) * CH
                    rows = src[r0:r0 + CH, :].rearrange("(m r) e -> m r e", r=16)[:, 0:DEC_SEQ, :]
                if keys:
                    eng.dma_start(k_in[:, b * ROWS + c], rows).then_inc(k_loaded[b], 16)
                elif c < DENSE_ROWS:
                    eng.dma_start(v_in[:, b, c, :, 0:HALF], rows.rearrange("p (f e) -> p f e", f=HALVES))\
                        .then_inc(v_loaded[b], 16)
                else:
                    for f in range(HALVES):
                        eng.dma_start(v_in[:, b, c, f, 0:HALF], rows[:, :, f * HALF:(f + 1) * HALF])\
                            .then_inc(v_loaded[b], 16)

        with nc.Block() as block:
            @block.sync
            def _(sp):
                if A:
                    sp.dma_start(table[:, :], d["page_table"].rearrange("(o b) j -> o (b j)", o=1)).then_inc(table_loaded, 16)
                sp.dma_start(q_in[:, :], d["q_scratch"][SEQ:TOK, col0:col0 + CH]).then_inc(setup_loaded, 16)
                sp.dma_start(k_new[:, :], d["fk_s" if A else "wk_s"]).then_inc(setup_loaded, 16)
                sp.dma_start(v_new[:, :, 0:HALF], d["fv_s" if A else "wv_s"].rearrange("n (f e) -> n f e", e=HALF))\
                    .then_inc(setup_loaded, 16)
                if A:
                    sp.wait_ge(table_loaded, 16)
                with sp.Fori(0, TURNS) as i:
                    for b in range(2):
                        if A:
                            load_pages(sp, i, b, "cache_fox_k")
                        else:
                            load_window(sp, i, b, "cache_win_k")
                            load_window(sp, i, b, "cache_win_v")
                sp.wait_ge(out_ready, 2 + DEC_BATCH)
                for h in range(QN // DEC_SEQ):
                    f, c0 = divmod(h // G * HEAD, HALF)
                    sp.dma_start(d["mix_scratch"][SEQ:TOK, col0 + h * HEAD:col0 + (h + 1) * HEAD]
                                 .rearrange("(b t) e -> t b e", t=DEC_SEQ),
                                 out_all[h * DEC_SEQ:(h + 1) * DEC_SEQ, :, f, c0:c0 + HEAD]).then_inc(stored, 16)
                sp.wait_ge(stored, 16 * (QN // DEC_SEQ))

            @block.gpsimd
            def _(pool):
                nc.gpsimd.memset(v_in[:, :, :, :, HALF:], 1.0)
                nc.gpsimd.memset(v_new[:, :, HALF:], 1.0).then_inc(ones_ready, 1)
                if A:
                    pool.wait_ge(table_loaded, 16)
                with pool.Fori(0, TURNS) as i:
                    def spread(ready, src, dst, op, done, b):
                        pool.wait_ge(ready, 2 * i + b + 1)
                        pool.sem_inc(spare, 1)
                        nc.gpsimd.partition_all_reduce(dst[:, b], src[:, b], P, op).then_inc(done, 1)

                    if A:
                        load_pages(pool, i, 0, "cache_fox_v")
                    spread(maxed, part_max, all_max, RMAX, max_spread, 0)
                    if A:
                        load_pages(pool, i, 1, "cache_fox_v")
                    spread(maxed, part_max, all_max, RMAX, max_spread, 1)

            @block.tensor
            def _(pe):
                pe.sem_inc(turned, K_RING)
                pe.sem_inc(scored, 2)
                if A:
                    pe.sem_inc(row_back, 2)
                pe.sem_inc(weighed, 2)
                pe.wait_ge(setup_loaded, 48)
                for j in range(4):
                    nc.tensor.transpose(p_turn[:, 0, j * N_NEW:(j + 1) * N_NEW], q_in[:, j * P:(j + 1) * P],
                                        sh["ident"][:N_NEW, :N_NEW])
                for j in range(PAIRS):
                    last = nc.tensor.transpose(p_turn[:, 1, j * N_NEW:(j + 1) * N_NEW], k_new[:, j * P:(j + 1) * P],
                                               sh["ident"][:N_NEW, :N_NEW])
                last.then_inc(set_pe, 1)
                pe.wait_ge(ones_ready, 1)
                pe.wait_ge(set_dve, 3 + 2 * PAIRS * G)
                with pe.Fori(0, TURNS) as i:
                    def turn(n):
                        b, r = divmod(n, ROWS)
                        if r % BATCH == 0:
                            uses = 2 * ROWS // K_RING
                            pe.wait_ge(k_loaded[n % K_RING // BATCH], K_LOADS * (uses * i + n // K_RING + 1))
                        pe.wait_ge(turn_act if n % 2 == 0 else turn_dve, ROWS * i + n // 2 + 1)
                        for j in range(4):
                            last = nc.tensor.transpose(p_turn[:, n % 2, j * P:(j + 1) * P],
                                                       k_in[:, n % K_RING, j * P:(j + 1) * P], sh["ident"][:, :])
                        last.then_inc(turned, 1)

                    def score(n):
                        b, r = divmod(n, ROWS)
                        pe.wait_ge(turn_act if n % 2 == 0 else turn_dve, ROWS * i + n // 2 + 2)
                        for j in range(4):
                            pair, keys = block_of(r, j)
                            c0 = keys * QN + pair * QC
                            nc.tensor.matmul(p_scores[:, b, c0:c0 + QC], k_t[:, n % 2, j * P:(j + 1) * P],
                                             q_blocks[:, ds(2 * i + b, 1), pair, :], start=True, stop=True)

                    def new_scores(b):
                        pe.wait_ge(out_ready, 2 * i + b + 1)
                        pe.sem_inc(spare, 1)
                        for pair in range(PAIRS):
                            last = nc.tensor.matmul(p_side[:N_NEW, b, pair * QC:(pair + 1) * QC],
                                                    k_new_t[:, pair, :],
                                                    q_blocks[:, ds(2 * i + b, 1), pair, q0(pair):q0(pair) + QC],
                                                    start=True, stop=True)
                        last.then_inc(scored, 1)

                    def score_row(n):
                        b, r = divmod(n, ROWS)
                        if r == 0:
                            pe.wait_ge(q_ready, 2 * i + b + 1)
                        pe.wait_ge(turn_act if n % 2 == 0 else turn_dve, ROWS * i + n // 2 + 2)
                        pe.wait_ge(row_read, 2 * ROWS * i + n + 1)
                        keys = k_t[:, n % 2, :].rearrange("p (s a c) -> p a s c", s=2, a=PAIRS)
                        for pair in range(PAIRS):
                            last = nc.tensor.matmul(p_query[:QN, n % 2, 0:2 * P], q_now[:, b, pair, :], keys[:, pair],
                                                    start=(pair == 0), stop=(pair == PAIRS - 1))
                        last.then_inc(row_scored, 1)

                    def back(n):
                        b, r = divmod(n, ROWS)
                        if r == 0:
                            pe.wait_ge(biased, 2 * i + b + 2)
                        pe.wait_ge(row_read, 2 + 2 * ROWS * i + n + 1)
                        pe.sem_inc(spare, 1)
                        for e in range(2):
                            c0 = (2 * r + e) * QN
                            last = nc.tensor.transpose(p_scores[:, 0, c0:c0 + QN], by_query[:, n % 2, e * P:(e + 1) * P],
                                                       sh["ident"][:QN, :QN])
                        last.then_inc(row_back, 1)

                    if A:
                        turn(0)
                    for b in range(2):
                        if A:
                            for r in range(ROWS):
                                n = b * ROWS + r
                                if n + 1 < 2 * ROWS:
                                    turn(n + 1)
                                score_row(n)
                                if r > 0:
                                    back(n - 1)
                            back(b * ROWS + ROWS - 1)
                            new_scores(b)
                            continue
                        turn(b * ROWS)
                        pe.wait_ge(biased, 2 * i + b + 1)
                        for r in range(ROWS):
                            if r + 1 < ROWS:
                                turn(b * ROWS + r + 1)
                            score(b * ROWS + r)
                        new_scores(b)
                    for b in range(2):
                        pe.wait_ge(exped, 2 * i + b + 1)
                        pe.wait_ge(v_loaded[b], V_LOADS * (i + 1))
                        for f, p_out in enumerate(p_outs):
                            out = p_out[:QN, b, 64:64 + HALF + 1]
                            for keys in range(KEYSETS):
                                nc.tensor.matmul(out, probs[:, b, keys, :], v_in[:, b, keys, f, :],
                                                 start=(keys == 0), stop=False)
                            last = nc.tensor.matmul(out, probs[:N_NEW, b, KEYSETS, :], v_new[:, f, :],
                                                    start=False, stop=True)
                        last.then_inc(weighed, 1)

            @block.scalar
            def _(act):
                act.sem_inc(turn_act, 1)
                if A:
                    act.sem_inc(row_read, 2)
                with act.Fori(0, TURNS) as i:
                    def evacuate(n):
                        act.wait_ge(turned, K_RING + 2 * ROWS * i + n + 1)
                        nc.scalar.copy(k_t[:, n % 2, :], p_turn[:, n % 2, :]).then_inc(turn_act, 1)

                    def exp(b):
                        act.wait_ge(shifted, 2 * i + b + 1)
                        act.wait_ge(weighed, 2 * i + b + 1)
                        nc.scalar.activation(probs[:, b], logits[:, b], ACT.Exp).then_inc(exped, 1)

                    def read_row(n):
                        act.wait_ge(row_scored, 2 * ROWS * i + n + 1)
                        act.wait_ge(row_back, 2 * ROWS * i + n + 1)
                        nc.scalar.copy(by_query[:, n % 2, :], p_query[:QN, n % 2, 0:2 * P]).then_inc(row_read, 1)

                    for n in range(2 * ROWS):
                        if n == ROWS + ROWS // 2 + 1:
                            exp(0)
                        if n % 2 == 0:
                            evacuate(n)
                        if A and n > 0:
                            read_row(n - 1)
                    if A:
                        read_row(2 * ROWS - 1)
                    exp(1)

            @block.vector
            def _(dve):
                dve.sem_inc(turn_dve, 1)
                dve.sem_inc(biased, 2)
                dve.sem_inc(out_ready, 2)
                nc.vector.memset(q_blocks[:, :, :, :], 0.0).then_inc(set_dve, 1)
                nc.vector.memset(logits[:, :, KEYSETS, :], NEG).then_inc(set_dve, 1)
                dve.wait_ge(set_pe, 1)
                dve.wait_ge(set_dve, 2)
                copies = 0
                for kv in range(2 * PAIRS):
                    pair, kh = divmod(kv, 2)
                    for g in range(G):
                        tile, row = (kv, g * HEAD) if A else (pair, kh * HEAD)
                        src = p_turn[row:row + HEAD, 0, tile * N_NEW:(tile + 1) * N_NEW]\
                            .rearrange("p (b t) -> p b t", b=DEC_BATCH)
                        c0 = (kh * G + g) * DEC_SEQ + (pair * QC if A else 0)
                        nc.vector.tensor_scalar(q_blocks[kh * HEAD:(kh + 1) * HEAD, :, pair, c0:c0 + DEC_SEQ], src,
                                                SCALE, None, ALU.mult).then_inc(set_dve, 1)
                        copies += 1
                nc.vector.tensor_copy(k_new_t[:, :, :].rearrange("p a n -> p (a n)"),
                                      p_turn[:, 1, 0:PAIRS * N_NEW]).then_inc(set_dve, 1)
                assert copies == 2 * PAIRS * G
                dve.wait_ge(set_dve, 3 + copies)
                with dve.Fori(0, TURNS) as i:
                    def evacuate(n):
                        dve.wait_ge(turned, K_RING + 2 * ROWS * i + n + 1)
                        nc.vector.tensor_copy(k_t[:, n % 2, :], p_turn[:, n % 2, :]).then_inc(turn_dve, 1)

                    def add_bias(b):
                        dve.wait_ge(scored, 2 + 2 * i + b + 1)
                        scores = p_scores[:, 0 if A else b, 0:KEYSETS * QN]
                        if A:
                            nc.vector.tensor_tensor(
                                logits[:, b, 0:KEYSETS, :].rearrange("p n (h t) -> p (n h) t", t=DEC_SEQ),
                                scores.rearrange("p (n t) -> p n t", t=DEC_SEQ),
                                sh["neg_c_past"][:, ds(2 * i + b, 1), :, :].rearrange("p o n h -> p (o n h)")[:, :, None]
                                .broadcast_to([P, KEYSETS * HEADS_A, DEC_SEQ]), ALU.add)
                        else:
                            nc.vector.tensor_tensor(
                                logits[:, b, 0:KEYSETS, :].rearrange("p n q -> p (n q)"), scores,
                                sh["win_bias"][:, :, :, :].rearrange("p n h t -> p (n h t)"), ALU.add)
                        new_bias = sh["new_bias_a" if A else "new_bias_b"]
                        nc.vector.tensor_tensor(logits[:N_NEW, b, KEYSETS, :], p_side[:N_NEW, b, 0:QN],
                                                new_bias[:, ds(2 * i + b, 1)].rearrange("p o h t -> p (o h t)"),
                                                ALU.add).then_inc(biased, 1)
                        dve.wait_ge(biased, 2 + 2 * i + b + 1)
                        nc.vector.tensor_reduce(part_max[:, b], logits[:, b].rearrange("p n q -> p q n"), AX.X, ALU.max)\
                            .then_inc(maxed, 1)

                    def shift(b):
                        dve.wait_ge(max_spread, 2 * i + b + 1)
                        nc.vector.tensor_tensor(logits[:, b], logits[:, b],
                                                all_max[:, b, None, :].broadcast_to([P, KEYSETS + 1, QN]),
                                                ALU.subtract).then_inc(shifted, 1)

                    def normalise(b):
                        dve.wait_ge(weighed, 2 + 2 * i + b + 1)
                        for f, p_out in enumerate(p_outs):
                            last = nc.vector.reciprocal(recip[:, b, f:f + 1], p_out[:QN, b, 64 + HALF:64 + HALF + 1])
                        last.then_inc(recip_ready, 1)
                        dve.wait_ge(recip_ready, 2 * i + b + 1)
                        for f, p_out in enumerate(p_outs):
                            last = nc.vector.tensor_scalar(
                                out_all[:, ds(2 * i + b, 1), f, :].rearrange("p o e -> p (o e)"),
                                p_out[:QN, b, 64:64 + HALF], recip[:, b, f:f + 1], None, ALU.mult)
                        last.then_inc(out_ready, 1)

                    if A:
                        for b in range(2):
                            dve.wait_ge(scored, 2 * i + b + 1)
                            nc.vector.tensor_copy(q_now[:, b], q_blocks[:, ds(2 * i + b, 1), :, :]
                                                  .rearrange("p o a q -> p (o a) q")).then_inc(q_ready, 1)
                    for n in range(2 * ROWS):
                        if n == ROWS:
                            add_bias(0)
                        if n == ROWS + ROWS // 2:
                            shift(0)
                        if n % 2 == 1:
                            evacuate(n)
                    add_bias(1)
                    shift(1)
                    normalise(0)
                    normalise(1)


PIECE = TOK // 3
NP = TOK // PIECE
LAST_P = SEQ - (NP - 1) * PIECE
FT = D_FF // P
UT = 2 * FT
SLOTS = 4
ADDS = KT + 1
AHEAD = SLOTS - 1


def piece(a, k, q):
    return a[:, k, q * PIECE:(q + 1) * PIECE]


def project_out(nc, d, sh):
    with ExitStack() as ctx:
        sb = lambda n, s, t=F32: ctx.enter_context(nc.sbuf_tensor("o_" + n, s, t))
        pb = lambda n, s, t=F32: ctx.enter_context(nc.psum_tensor("o_" + n, s, t))
        sem = lambda n: nc.alloc_semaphore("o_" + n)
        rows_in = sb("rows_in", [P, 2, D_MODEL])
        mix_hi = sb("mix_hi", [P, KT, TOK], F32R)
        mix_lo = sb("mix_lo", [P, KT, TOK], F32R)
        y = sb("y", [P, KT, TOK])
        w_raw = sb("w_raw", [P, SLOTS, KT, P])
        w_hi = sb("w_hi", [P, SLOTS, KT, P], F32R)
        w_lo = sb("w_lo", [P, SLOTS, KT, P], F32R)
        square = sb("square", [P, 2, PIECE])
        sum_sq = sb("sum_sq", [P, NP, PIECE])
        gains_in = sb("gains_in", [4 * KT, P])
        taps_in = sb("taps_in", [UT, 4, P])
        p_turn = pb("p_turn", [P, 2, D_MODEL])
        p_y = pb("p_y", [P, NP, CH])
        p_sum = pb("p_sum", [P, CH])
        x_t, gains, taps = sh["rows_t"], sh["gains"], sh["taps"]

        rows_loaded = [sem("rows_loaded0"), sem("rows_loaded1")]
        consts_loaded = sem("consts_loaded")
        w_loaded = [sem(f"w_loaded{s}") for s in range(SLOTS)]
        turned, turn_read = sem("turned"), sem("turn_read")
        mix_hi_ready, mix_lo_ready = sem("mix_hi_ready"), sem("mix_lo_ready")
        w_hi_ready = sem("w_hi_ready")
        w_lo_ready = sem("w_lo_ready")
        y_done = sem("y_done")
        y_read = sem("y_read")
        squared = sem("squared")
        added = sem("added")
        sum_done, rms_ready, rstd_ready = sem("sum_done"), sem("rms_ready"), sem("rstd_ready")
        scaled_pool, scaled_dve = sem("scaled_pool"), sem("scaled_dve")
        PIECES = (2, 0, 1)

        def add_scaled(eng, ops, q, scaled, before):
            for k in range(KT):
                ops.tensor_tensor(piece(y, k, q), piece(y, k, q), sum_sq[:, q, :], ALU.mult).then_inc(scaled, 1)
            for k in range(KT):
                eng.wait_ge(scaled, before + k + 1)
                ops.tensor_tensor(piece(x_t, k, q), piece(x_t, k, q), piece(y, k, q), ALU.add)

        const_pe, const_act, eps_ready = sem("const_pe"), sem("const_act"), sem("eps_ready")

        with nc.Block() as block:
            @block.sync
            def _(sp):
                def load_rows(n):
                    t0, rows = TILES[NT - 1 if n == 0 else n - 1]
                    if n >= 2:
                        sp.wait_ge(turned, n - 1)
                    sp.dma_start(rows_in[:rows, n % 2, :], d["mix_scratch"][t0:t0 + rows, :] if n == 0 else d["x"](n - 1))\
                        .then_inc(rows_loaded[n % 2], 16)

                def load_w(m):
                    if m >= SLOTS:
                        sp.wait_ge(w_lo_ready, m - SLOTS + 1)
                    sp.dma_start(w_raw[:, m % SLOTS],
                                 d["w_out"][0].rearrange("(k p) n -> p k n", p=P)[:, :, m * P:(m + 1) * P])\
                        .then_inc(w_loaded[m % SLOTS], 16)

                load_rows(0)
                for m in range(SLOTS):
                    load_w(m)
                load_rows(1)
                for j, name in enumerate(("g_attn_post", "g_ffn_pre", "g_ffn_post", "g_ple")):
                    sp.dma_start(gains_in[j * KT:(j + 1) * KT, :], d[name].rearrange("o (k p) -> (o k) p", p=P))\
                        .then_inc(consts_loaded, 16)
                sp.dma_start(taps_in[:, 0:3, :], d["conv_w"][0].rearrange("j (t p) -> t j p", p=P))\
                    .then_inc(consts_loaded, 16)
                sp.dma_start(taps_in[:, 3, :], d["conv_b"][0].rearrange("(t p) -> t p", p=P)).then_inc(consts_loaded, 16)
                for n in range(2, NT + 1):
                    load_rows(n)
                    if SLOTS + n - 2 < KT:
                        load_w(SLOTS + n - 2)

            @block.gpsimd
            def _(pool):
                nc.gpsimd.memset(sum_sq[:, :, :], 0.0).then_inc(added, 1)
                for n in range(NP * KT):
                    q = n % NP
                    pool.wait_ge(squared, n + 1)
                    pool.wait_ge(added, n + 1)
                    nc.gpsimd.tensor_tensor(sum_sq[:, q, :], sum_sq[:, q, :], square[:, n % 2, :], ALU.add)\
                        .then_inc(added, 1)
                pool.wait_ge(turn_read, NT + 1)
                pool.wait_ge(rstd_ready, 1)
                add_scaled(pool, nc.gpsimd, PIECES[0], scaled_pool, 0)

            @block.tensor
            def _(pe):
                def turn_rows(n):
                    t0, rows = TILES[NT - 1 if n == 0 else n - 1]
                    pe.wait_ge(rows_loaded[n % 2], 16 * (n // 2 + 1))
                    if n >= 2:
                        pe.wait_ge(turn_read, n - 1)
                    for k in range(KT):
                        last = nc.tensor.transpose(p_turn[:, n % 2, k * P:k * P + rows],
                                                   rows_in[:rows, n % 2, k * P:(k + 1) * P], sh["ident"][:rows, :rows])
                    last.then_inc(turned, 1)

                turn_rows(0)
                pe.wait_ge(mix_lo_ready, KT)
                for m in range(KT):
                    pe.wait_ge(w_lo_ready, m + 1)
                    for q in range(NP):
                        c0 = q * PIECE
                        if m > 0:
                            pe.wait_ge(y_read, NP * (m - 1) + q + 1)
                        for k in range(KT):
                            for part, (w, a) in enumerate(((w_hi, mix_hi), (w_hi, mix_lo), (w_lo, mix_hi))):
                                last = nc.tensor.matmul(p_y[:, q, 0:PIECE], w[:, m % SLOTS, k, :], a[:, k, c0:c0 + PIECE],
                                                        start=(k == 0 and part == 0), stop=(k == KT - 1 and part == 2))
                        last.then_inc(y_done, 1)
                        if m == 0 and q == 0:
                            pe.wait_ge(consts_loaded, 96)
                            nc.tensor.transpose(p_sum[:, 0:4 * KT], gains_in[:, :], sh["ident"][:4 * KT, :4 * KT])
                            for j in range(4):
                                last = nc.tensor.transpose(p_sum[:, 64 + j * UT:64 + (j + 1) * UT], taps_in[:, j, :],
                                                           sh["ident"][:UT, :UT])
                            last.then_inc(const_pe, 1)
                    turn_rows(m + 1)
                turn_rows(NT)
                pe.wait_ge(const_act, 1)
                for n, q in enumerate(PIECES):
                    if n == 0:
                        pe.wait_ge(added, 1 + NP * KT)
                    else:
                        pe.wait_ge(rms_ready, n)
                    nc.tensor.matmul(p_sum[:, 0:PIECE], sh["ones"][:, :], sum_sq[:, q, :],
                                     start=True, stop=True).then_inc(sum_done, 1)

            @block.scalar
            def _(act):
                def split_w(m):
                    act.wait_ge(w_loaded[m % SLOTS], 16 * (m // SLOTS + 1))
                    if m >= SLOTS:
                        act.wait_ge(y_done, NP * (m - SLOTS + 1))
                    nc.scalar.activation(w_hi[:, m % SLOTS], w_raw[:, m % SLOTS], ACT.Copy).then_inc(w_hi_ready, 1)

                def read_rows(n):
                    t0, rows = TILES[NT - 1 if n == 0 else n - 1]
                    act.wait_ge(turned, n + 1)
                    nc.scalar.activation(x_t[:, :, t0:t0 + rows],
                                         p_turn[:, n % 2, :].rearrange("p (k m) -> p k m", k=KT)[:, :, 0:rows],
                                         ACT.Copy).then_inc(turn_read, 1)

                split_w(0)
                read_rows(0)
                act.wait_ge(turn_read, 1)
                for k in range(KT):
                    nc.scalar.activation(mix_hi[:, k, :], sh["rows_t"][:, k, :], ACT.Copy).then_inc(mix_hi_ready, 1)
                for m in range(1, SLOTS):
                    split_w(m)
                act.wait_ge(const_pe, 1)
                nc.scalar.copy(gains[:, :, :].rearrange("p a k -> p (a k)"), p_sum[:, 0:4 * KT])
                nc.scalar.copy(taps[:, :, :].rearrange("p a k -> p (a k)"), p_sum[:, 64:64 + 4 * UT]).then_inc(const_act, 1)
                act.wait_ge(const_act, 1)
                for m in range(KT):
                    for q in range(NP):
                        n = NP * m + q
                        act.wait_ge(y_done, n + 1)
                        if n >= 2:
                            act.wait_ge(added, n)
                        nc.scalar.activation(square[:, n % 2, :], p_y[:, q, 0:PIECE], ACT.Square).then_inc(squared, 1)
                        nc.scalar.activation(piece(y, m, q), p_y[:, q, 0:PIECE], ACT.Copy, scale=gains[:, 0, m:m + 1])\
                            .then_inc(y_read, 1)
                    read_rows(m + 1)
                    if m + SLOTS < KT:
                        split_w(m + SLOTS)
                read_rows(NT)
                act.wait_ge(eps_ready, 1)
                for n, q in enumerate(PIECES):
                    act.wait_ge(sum_done, n + 1)
                    nc.scalar.activation(sum_sq[:, q, :], p_sum[:, 0:PIECE], ACT.Sqrt, scale=1.0 / D_MODEL,
                                         bias=sh["eps"][:, :]).then_inc(rms_ready, 1)

            @block.vector
            def _(dve):
                nc.vector.memset(sh["eps"][:, :], EPS).then_inc(eps_ready, 1)

                def split_w(m):
                    dve.wait_ge(w_hi_ready, m + 1)
                    nc.vector.tensor_tensor(w_lo[:, m % SLOTS], w_raw[:, m % SLOTS], w_hi[:, m % SLOTS].bitcast(F32),
                                            ALU.subtract).then_inc(w_lo_ready, 1)

                split_w(0)
                for k in range(KT):
                    dve.wait_ge(mix_hi_ready, k + 1)
                    nc.vector.tensor_tensor(mix_lo[:, k, :], sh["rows_t"][:, k, :], mix_hi[:, k, :].bitcast(F32),
                                            ALU.subtract).then_inc(mix_lo_ready, 1)
                for m in range(1, KT):
                    split_w(m)
                dve.wait_ge(turn_read, NT + 1)
                for n, q in enumerate(PIECES):
                    dve.wait_ge(rms_ready, n + 1)
                    nc.vector.reciprocal(sum_sq[:, q, :], sum_sq[:, q, :]).then_inc(rstd_ready, 1)
                    dve.wait_ge(rstd_ready, n + 1)
                    if n > 0:
                        add_scaled(dve, nc.vector, q, scaled_dve, KT * (n - 1))


def conv_ffn(nc, d, sh):
    N_TILES = UT + 3 * KT
    BLOCKS = [(0, 8), (8, 8), (16, 6)]
    PRE = [0] + [2 * p - 1 for p in range(1, NP)]
    POST = [2 * p + 2 if p < NP - 1 else 2 * p + 1 for p in range(NP)]
    ROUNDS = 4
    QT = UT // ROUNDS
    STATE = 2 * DEC_BATCH
    with ExitStack() as ctx:
        sb = lambda n, s, t=F32: ctx.enter_context(nc.sbuf_tensor("f_" + n, s, t))
        pb = lambda n, s, t=F32: ctx.enter_context(nc.psum_tensor("f_" + n, s, t))
        sem = lambda n: nc.alloc_semaphore("f_" + n)
        xn_hi = sb("xn_hi", [P, KT, PIECE], F32R)
        xn_lo = sb("xn_lo", [P, KT, PIECE], F32R)
        xn = sb("xn", [P, 2, PIECE])
        h_hi = sb("h_hi", [P, FT, PIECE], F32R)
        h_lo = sb("h_lo", [P, FT, PIECE], F32R)
        w_raw = sb("w_raw", [P, SLOTS, KT, P])
        w_hi = sb("w_hi", [P, SLOTS, KT, P], F32R)
        w_lo = sb("w_lo", [P, SLOTS, KT, P], F32R)
        work = sb("work", [P, KT, 2 + PIECE])
        new_up = sb("new_up", [P, SLOTS, DEC_BATCH, 2 + DEC_SEQ])
        square = sb("square", [P, 2, PIECE])
        sum_sq = sb("sum_sq", [P, PIECE])
        rms = sb("rms", [P, PIECE])
        before = sb("before", [P, UT, 2 + STATE])
        rows_io = sb("rows_io", [2 + STATE, 2, QT, P])
        p_up = pb("p_up", [P, SLOTS, CH])
        p_y = pb("p_y", [P, 2, CH])
        p_sum = pb("p_sum", [P, CH])
        p_turn = pb("p_turn", [P, CH])
        x_t, gains, taps = sh["rows_t"], sh["gains"], sh["taps"]
        up = lambda j, c0, c1: work[:, j, c0:c1]
        conv = lambda j: work[:, SLOTS + j, 0:PIECE]

        w_loaded = [sem(f"w_loaded{s}") for s in range(SLOTS)]
        w_hi_ready = sem("w_hi_ready")
        w_lo_ready = sem("w_lo_ready")
        w_used = sem("w_used")
        up_read = sem("up_read")
        haloed = sem("haloed")
        carried = sem("carried")
        convolved = sem("convolved")
        tap_added = sem("tap_added")
        gelued, hid_ready, hid_hi = sem("gelued"), sem("hid_ready"), sem("hid_hi")
        hid_lo = sem("hid_lo")
        y_read = sem("y_read")
        squared, added = sem("squared"), sem("added")
        first_summed = sem("first_summed")
        sum_done, rms_ready, rstd_ready = sem("sum_done"), sem("rms_ready"), sem("rstd_ready")
        xn_ready, xn_hi_ready, xn_lo_ready = sem("xn_ready"), sem("xn_hi_ready"), sem("xn_lo_ready")
        gained, residual = sem("gained"), sem("residual")
        rows_loaded, rows_stored, rows_out = sem("rows_loaded"), sem("rows_stored"), sem("rows_out")
        turned, turn_read, cleared = sem("turned"), sem("turn_read"), sem("cleared")
        spare = sem("spare")

        def wait_loaded(eng, p, base, per, i, j):
            n = N_TILES * p + base + j
            eng.wait_ge(w_loaded[j % SLOTS], 16 * (n // SLOTS + 1) + 16 * (per // SLOTS) * i)

        with nc.Block() as block:
            @block.sync
            def _(sp):
                w_up = d["w_up"][0].rearrange("(k p) n -> p k n", p=P)
                w_down = d["w_down"][0].rearrange("(k p) n -> p k n", p=P)
                for p in range(NP + 1):
                    with sp.Fori(0, FT // 2 if p < NP else 1) as i:
                        for j in range(SLOTS if p < NP else AHEAD):
                            s, half = divmod(j, 2)
                            sp.wait_ge(w_lo_ready, N_TILES * p + SLOTS * i + j + 1)
                            sp.sem_inc(spare, 1)
                            sp.dma_start(w_raw[:, j], w_up[:, :, ds((2 * i + s + half * FT) * P, P)])\
                                .then_inc(w_loaded[j], 16)
                    if p == NP:
                        break
                    with sp.Fori(0, KT // 4) as i:
                        for j in range(12):
                            m, b = divmod(j, 3)
                            f0, fn = BLOCKS[b]
                            sp.wait_ge(w_lo_ready, N_TILES * p + UT + 12 * i + j + 1)
                            sp.sem_inc(spare, 1)
                            sp.dma_start(w_raw[:, j % SLOTS, 0:fn], w_down[:, f0:f0 + fn, ds((4 * i + m) * P, P)])\
                                .then_inc(w_loaded[j % SLOTS], 16)
                for s in range(SLOTS):
                    sp.wait_ge(w_loaded[s], 16 * (NP * N_TILES // SLOTS + (s < AHEAD)))

            @block.gpsimd
            def _(pool):
                def load_state(r):
                    pool.dma_start(rows_io[:STATE, 0], d["state_conv"][0].rearrange("b j (t p) -> (b j) t p", p=P)
                                   [:, r * QT:(r + 1) * QT]).then_inc(rows_loaded, 16)

                def next_state(r):
                    if r + 1 < ROUNDS:
                        pool.wait_ge(turned, r + 1)
                        load_state(r + 1)

                def store_state(r):
                    pool.wait_ge(rows_out, r + 1)
                    pool.dma_start(d["cv_p"][0, 0].rearrange("j (t p) -> j t p", p=P)[:, r * QT:(r + 1) * QT],
                                   rows_io[0:2, r % 2]).then_inc(rows_stored, 16)
                    pool.dma_start(d["cv_s"][0].rearrange("b j (t p) -> (b j) t p", p=P)[:, r * QT:(r + 1) * QT],
                                   rows_io[2:2 + STATE, r % 2]).then_inc(rows_stored, 16)

                def clear_sum(q):
                    if q > 0:
                        pool.wait_ge(sum_done, q)
                    nc.gpsimd.memset(sum_sq[:, :], 0.0).then_inc(added, 1)

                def add_square(q, k, slot):
                    pool.wait_ge(squared, KT * q + k + 1)
                    pool.wait_ge(added, ADDS * q + k + 1)
                    nc.gpsimd.tensor_tensor(sum_sq[:, :], sum_sq[:, :], square[:, slot, :], ALU.add).then_inc(added, 1)

                def add_squares(q):
                    clear_sum(q)
                    for k in range(KT):
                        add_square(q, k, k % 2)

                pool.sem_inc(carried, 4)
                pool.sem_inc(added, ADDS)
                load_state(0)
                nc.gpsimd.memset(before[:, :, 0:2], 0.0).then_inc(cleared, 1)
                pool.wait_ge(cleared, 1)
                for p in range(NP):
                    last_piece = p == NP - 1
                    if not last_piece:
                        add_squares(PRE[p + 1])
                    else:
                        pool.wait_ge(turn_read, ROUNDS)
                    if p > 0:
                        pool.wait_ge(residual, p)
                        pool.wait_ge(carried, 4 + UT * p)
                    with pool.Fori(0, FT // 2) as i:
                        for j in range(SLOTS):
                            s, half = divmod(j, 2)
                            u = UT * p + SLOTS * i + j
                            tile = 2 * i + s + half * FT
                            pool.wait_ge(convolved, u + 1)
                            pool.sem_inc(spare, 1)
                            ins = nc.gpsimd.tensor_copy(up(j, 0, 2), before[:, ds(tile, 1), 0:2].rearrange("p o c -> p (o c)"))
                            if last_piece:
                                ins = nc.gpsimd.tensor_copy(
                                    new_up[:, j, :, 0:2],
                                    before[:, ds(tile, 1), 2:].rearrange("p o (b c) -> p (o b) c", c=2))
                            ins.then_inc(haloed, 1)
                            pool.wait_ge(up_read, 4 + u + 1)
                            pool.wait_ge(haloed, u + 1)
                            pool.sem_inc(spare, 1)
                            last = LAST_P if last_piece else PIECE
                            ins = nc.gpsimd.tensor_copy(before[:, ds(tile, 1), 0:2].rearrange("p o c -> p (o c)"),
                                                        up(j, last, last + 2))
                            if last_piece:
                                ins = nc.gpsimd.tensor_copy(
                                    before[:, ds(tile, 1), 2:].rearrange("p o (b c) -> p (o b) c", c=2),
                                    new_up[:, j, :, DEC_SEQ:DEC_SEQ + 2])
                            ins.then_inc(carried, 1)
                    next_state(2 * p)
                    if last_piece:
                        store_state(0)
                        store_state(1)
                    clear_sum(POST[p])
                    with pool.Fori(0, KT // 4) as i:
                        for m in range(4):
                            add_square(POST[p], 4 * i + m, m % 2)
                    next_state(2 * p + 1)
                store_state(2)
                store_state(3)
                pool.wait_ge(rows_stored, 32 * ROUNDS)

            @block.tensor
            def _(pe):
                pe.sem_inc(w_used, 4)

                def turn_state(r):
                    if r < ROUNDS:
                        pe.wait_ge(rows_loaded, 16 * (r + 1))
                        if r > 0:
                            pe.wait_ge(turn_read, r)
                        for t in range(QT):
                            last = nc.tensor.transpose(p_turn[:, t * STATE:(t + 1) * STATE], rows_io[:STATE, 0, t, :],
                                                       sh["ident"][:STATE, :STATE])
                        last.then_inc(turned, 1)

                def turn_back(r):
                    if r == 0:
                        pe.wait_ge(carried, 4 + NP * UT)
                    else:
                        pe.wait_ge(rows_out, r)
                    for t in range(QT):
                        last = nc.tensor.transpose(p_up[:2 + STATE, t // 4, t % 4 * P:(t % 4 + 1) * P],
                                                   before[:, r * QT + t, :], sh["ident"][:, :])
                    last.then_inc(turned, 1)

                def sum_first():
                    for k in range(KT):
                        pe.wait_ge(squared, k + 1)
                        last = nc.tensor.matmul(p_sum[:, 0:PIECE], sh["ones"][:, :], square[:, k % 2, :],
                                                start=(k == 0), stop=(k == KT - 1))
                        last.then_inc(first_summed, 1)
                    pe.wait_ge(first_summed, KT)
                    pe.sem_inc(sum_done, 1)

                def sum_squares(q):
                    pe.wait_ge(added, ADDS * (q + 1))
                    if q > 0:
                        pe.wait_ge(rms_ready, q)
                    nc.tensor.matmul(p_sum[:, 0:PIECE], sh["ones"][:, :], sum_sq[:, :], start=True, stop=True)\
                        .then_inc(sum_done, 1)

                sum_first()
                for p in range(NP):
                    pe.wait_ge(xn_lo_ready, KT * (p + 1))
                    with pe.Fori(0, FT // 2) as i:
                        for j in range(SLOTS):
                            pe.wait_ge(w_lo_ready, 4 + N_TILES * p + SLOTS * i + j + 1)
                            pe.wait_ge(up_read, UT * p + SLOTS * i + j + 1)
                            for k in range(KT):
                                for part, (w, a) in enumerate(((w_hi, xn_hi), (w_hi, xn_lo), (w_lo, xn_hi))):
                                    last = nc.tensor.matmul(p_up[:, j, 0:PIECE], w[:, j, k, :], a[:, k, :],
                                                            start=(k == 0 and part == 0), stop=(k == KT - 1 and part == 2))
                            last.then_inc(w_used, 1)
                    turn_state(2 * p)
                    if p < NP - 1:
                        sum_squares(PRE[p + 1])
                    else:
                        turn_back(0)
                        turn_back(1)
                    with pe.Fori(0, KT // 4) as i:
                        for j in range(12):
                            m, b = divmod(j, 3)
                            f0, fn = BLOCKS[b]
                            pe.wait_ge(w_lo_ready, 4 + N_TILES * p + UT + 12 * i + j + 1)
                            if j < 3:
                                pe.wait_ge(hid_lo, 2 + FT * p + f0 + fn)
                            if b == 0:
                                pe.wait_ge(y_read, KT * p + 4 * i + m + 1)
                            for f in range(fn):
                                for part, (w, a) in enumerate(((w_hi, h_hi), (w_hi, h_lo), (w_lo, h_hi))):
                                    last = nc.tensor.matmul(
                                        p_y[:, m % 2, 0:PIECE], w[:, j % SLOTS, f, :], a[:, f0 + f, :],
                                        start=(b == 0 and f == 0 and part == 0), stop=(b == 2 and f == fn - 1 and part == 2))
                            last.then_inc(w_used, 1)
                    turn_state(2 * p + 1)
                    sum_squares(POST[p])
                turn_back(2)
                turn_back(3)

            @block.scalar
            def _(act):
                def split_w(p, base, per, i, j):
                    wait_loaded(act, p, base, per, i, j)
                    act.wait_ge(w_used, N_TILES * p + base + per * i + j + 1)
                    nc.scalar.activation(w_hi[:, j % SLOTS], w_raw[:, j % SLOTS], ACT.Copy).then_inc(w_hi_ready, 1)

                def state_read(r):
                    if r < ROUNDS:
                        act.wait_ge(turned, r + 1)
                        nc.scalar.activation(before[:, r * QT:(r + 1) * QT, 2:],
                                             p_turn[:, 0:QT * STATE].rearrange("p (t c) -> p t c", t=QT),
                                             ACT.Copy).then_inc(turn_read, 1)

                def rows_back(r):
                    act.wait_ge(turned, ROUNDS + r + 1)
                    if r >= 2:
                        act.wait_ge(rows_stored, 64)
                    nc.scalar.activation(rows_io[:, r % 2], p_up[:2 + STATE, 0:3, :].rearrange("p a (t c) -> p (a t) c", c=P)
                                         [:, 0:QT, :], ACT.Copy).then_inc(rows_out, 1)

                def squares(p, q):
                    for k in range(KT):
                        if q > 0:
                            act.wait_ge(added, ADDS * q + k)
                        elif k >= 2:
                            act.wait_ge(first_summed, k - 1)
                        nc.scalar.activation(square[:, k % 2, :], x_t[:, k, p * PIECE:(p + 1) * PIECE],
                                             ACT.Square).then_inc(squared, 1)

                def root(q):
                    act.wait_ge(sum_done, q + 1)
                    nc.scalar.activation(rms[:, :], p_sum[:, 0:PIECE], ACT.Sqrt, scale=1.0 / D_MODEL,
                                         bias=sh["eps"][:, :]).then_inc(rms_ready, 1)

                def normed_hi(p):
                    for k in range(KT):
                        act.wait_ge(xn_ready, KT * p + k + 1)
                        nc.scalar.activation(xn_hi[:, k, :], xn[:, k % 2, :], ACT.Copy).then_inc(xn_hi_ready, 1)

                act.sem_inc(up_read, 4)
                act.sem_inc(y_read, 2)
                squares(0, PRE[0])
                root(PRE[0])
                split_w(0, 0, SLOTS, 0, 0)
                normed_hi(0)
                for j in range(1, AHEAD):
                    split_w(0, 0, SLOTS, 0, j)
                for p in range(NP):
                    last_piece = p == NP - 1
                    if not last_piece:
                        squares(p + 1, PRE[p + 1])
                    if p > 0:
                        act.wait_ge(residual, p)
                    with act.Fori(0, FT // 2) as i:
                        def read_up(j):
                            s, half = divmod(j, 2)
                            n, u = N_TILES * p + SLOTS * i + j, UT * p + SLOTS * i + j
                            tile = 2 * i + s + half * FT
                            split_w(p, 0, SLOTS, i, j + AHEAD)
                            act.wait_ge(w_used, 4 + n + 1)
                            act.wait_ge(convolved, u + 1)
                            act.wait_ge(carried, u + 1)
                            act.wait_ge(hid_lo, FT * p + 2 * i + s + 1)
                            if last_piece:
                                nc.scalar.activation(up(j, 2, 2 + LAST_P), p_up[:, j, 0:LAST_P], ACT.Copy)
                                nc.scalar.activation(new_up[:, j, :, 2:],
                                                     p_up[:, j, LAST_P:PIECE].rearrange("p (b t) -> p b t", b=DEC_BATCH),
                                                     ACT.Copy)
                            else:
                                nc.scalar.activation(up(j, 2, 2 + PIECE), p_up[:, j, 0:PIECE], ACT.Copy)
                            nc.scalar.activation(conv(j), p_up[:, j, 0:PIECE], ACT.Identity,
                                                 scale=taps[:, 2, ds(tile, 1)], bias=taps[:, 3, ds(tile, 1)])\
                                .then_inc(up_read, 1)

                        def gelu(s):
                            act.wait_ge(convolved, 4 + UT * p + SLOTS * i + 2 * s + 1)
                            nc.scalar.activation(conv(2 * s), conv(2 * s), ACT.Gelu_apprx_tanh).then_inc(gelued, 1)

                        def hidden_hi(s):
                            act.wait_ge(hid_ready, FT * p + 2 * i + s + 1)
                            nc.scalar.activation(h_hi[:, ds(2 * i + s, 1), :].rearrange("p o c -> p (o c)"),
                                                 conv(2 * s + 1), ACT.Copy).then_inc(hid_hi, 1)

                        read_up(0)
                        read_up(1)
                        read_up(2)
                        gelu(0)
                        read_up(3)
                        hidden_hi(0)
                        gelu(1)
                        hidden_hi(1)
                    state_read(2 * p)
                    if not last_piece:
                        root(PRE[p + 1])
                        normed_hi(p + 1)
                    else:
                        rows_back(0)
                        rows_back(1)
                    act.wait_ge(carried, 4 + UT * (p + 1))
                    with act.Fori(0, KT // 4) as i:
                        for j in range(12):
                            m, b = divmod(j, 3)
                            split_w(p, UT, 12, i, j + AHEAD)
                            if b == 2:
                                act.wait_ge(w_used, 4 + N_TILES * p + UT + 12 * i + j + 1)
                                act.wait_ge(added, ADDS * POST[p] + 4 * i + m)
                                nc.scalar.activation(square[:, m % 2, :], p_y[:, m % 2, 0:PIECE], ACT.Square)\
                                    .then_inc(squared, 1)
                                nc.scalar.activation(work[:, ds(4 * i + m, 1), 0:PIECE].rearrange("p o c -> p (o c)"),
                                                     p_y[:, m % 2, 0:PIECE], ACT.Copy).then_inc(y_read, 1)
                    state_read(2 * p + 1)
                    root(POST[p])
                rows_back(2)
                rows_back(3)

            @block.vector
            def _(dve):
                def split_w(p, base, per, i, j):
                    dve.wait_ge(w_hi_ready, N_TILES * p + base + per * i + j + 1)
                    nc.vector.tensor_tensor(w_lo[:, j % SLOTS], w_raw[:, j % SLOTS], w_hi[:, j % SLOTS].bitcast(F32),
                                            ALU.subtract).then_inc(w_lo_ready, 1)

                def invert(q):
                    dve.wait_ge(rms_ready, q + 1)
                    nc.vector.reciprocal(rms[:, :], rms[:, :]).then_inc(rstd_ready, 1)
                    dve.wait_ge(rstd_ready, q + 1)

                def normalise(p):
                    def low(k):
                        dve.wait_ge(xn_hi_ready, KT * p + k + 1)
                        nc.vector.tensor_tensor(xn_lo[:, k, :], xn[:, k % 2, :], xn_hi[:, k, :].bitcast(F32),
                                                ALU.subtract).then_inc(xn_lo_ready, 1)

                    for k in range(KT):
                        if k >= 2:
                            dve.wait_ge(xn_lo_ready, KT * p + k - 1)
                        nc.vector.scalar_tensor_tensor(out=xn[:, k % 2, :], in0=x_t[:, k, p * PIECE:(p + 1) * PIECE],
                                                       scalar=gains[:, 1, k:k + 1], in1=rms[:, :],
                                                       op0=ALU.mult, op1=ALU.mult).then_inc(xn_ready, 1)
                        if k >= 1:
                            low(k - 1)
                    low(KT - 1)

                dve.sem_inc(w_lo_ready, 4)
                dve.sem_inc(convolved, 4)
                dve.sem_inc(hid_lo, 2)
                invert(PRE[0])
                split_w(0, 0, SLOTS, 0, 0)
                normalise(0)
                for j in range(1, AHEAD):
                    split_w(0, 0, SLOTS, 0, j)
                for p in range(NP):
                    last_piece = p == NP - 1
                    with dve.Fori(0, FT // 2) as i:
                        def add_tap(j, tap, done):
                            s, half = divmod(j, 2)
                            tile = 2 * i + s + half * FT
                            rows = LAST_P if last_piece else PIECE
                            ins = nc.vector.scalar_tensor_tensor(
                                out=conv(j)[:, 0:rows], in0=up(j, tap, tap + rows), scalar=taps[:, tap, ds(tile, 1)],
                                in1=conv(j)[:, 0:rows], op0=ALU.mult, op1=ALU.add)
                            if last_piece:
                                new = conv(j)[:, rows:PIECE].rearrange("p (b t) -> p b t", b=DEC_BATCH)
                                ins = nc.vector.scalar_tensor_tensor(
                                    out=new, in0=new_up[:, j, :, tap:tap + DEC_SEQ], scalar=taps[:, tap, ds(tile, 1)],
                                    in1=new, op0=ALU.mult, op1=ALU.add)
                            ins.then_inc(done, 1)

                        def convolve(j):
                            u = UT * p + SLOTS * i + j
                            split_w(p, 0, SLOTS, i, j + AHEAD)
                            dve.wait_ge(haloed, u + 1)
                            dve.wait_ge(up_read, 4 + u + 1)
                            add_tap(j, 1, tap_added)
                            dve.wait_ge(tap_added, u + 1)
                            add_tap(j, 0, convolved)

                        def gate(s):
                            h = FT * p + 2 * i + s
                            dve.wait_ge(gelued, h + 1)
                            dve.wait_ge(convolved, 4 + UT * p + SLOTS * i + 2 * s + 2)
                            nc.vector.tensor_tensor(conv(2 * s + 1), conv(2 * s), conv(2 * s + 1), ALU.mult)\
                                .then_inc(hid_ready, 1)

                        def hidden_lo(s):
                            dve.wait_ge(hid_hi, FT * p + 2 * i + s + 1)
                            nc.vector.tensor_tensor(h_lo[:, ds(2 * i + s, 1), :].rearrange("p o c -> p (o c)"),
                                                    conv(2 * s + 1),
                                                    h_hi[:, ds(2 * i + s, 1), :].rearrange("p o c -> p (o c)").bitcast(F32),
                                                    ALU.subtract).then_inc(hid_lo, 1)

                        convolve(0)
                        convolve(1)
                        convolve(2)
                        gate(0)
                        convolve(3)
                        hidden_lo(0)
                        gate(1)
                        hidden_lo(1)
                    if not last_piece:
                        invert(PRE[p + 1])
                        normalise(p + 1)
                    with dve.Fori(0, KT // 4) as i:
                        for j in range(12):
                            split_w(p, UT, 12, i, j + AHEAD)
                    invert(POST[p])
                    for k in range(KT):
                        if k == 0:
                            dve.wait_ge(y_read, 2 + KT * (p + 1))
                        nc.vector.scalar_tensor_tensor(out=work[:, k, 0:PIECE], in0=work[:, k, 0:PIECE],
                                                       scalar=gains[:, 2, k:k + 1], in1=rms[:, :],
                                                       op0=ALU.mult, op1=ALU.mult).then_inc(gained, 1)
                    for k in range(KT):
                        dve.wait_ge(gained, KT * p + k + 1)
                        ins = nc.vector.tensor_tensor(x_t[:, k, p * PIECE:(p + 1) * PIECE],
                                                      x_t[:, k, p * PIECE:(p + 1) * PIECE], work[:, k, 0:PIECE], ALU.add)
                    ins.then_inc(residual, 1)


def embed_and_store(nc, d, sh):
    IT = PLE // P
    with ExitStack() as ctx:
        sb = lambda n, s, t=F32: ctx.enter_context(nc.sbuf_tensor("g_" + n, s, t))
        pb = lambda n, s, t=F32: ctx.enter_context(nc.psum_tensor("g_" + n, s, t))
        sem = lambda n: nc.alloc_semaphore("g_" + n)
        xn_hi = sb("xn_hi", [P, KT, TOK], F32R)
        xn_lo = sb("xn_lo", [P, KT, TOK], F32R)
        e_hi = sb("e_hi", [P, IT, TOK], F32R)
        e_lo = sb("e_lo", [P, IT, TOK], F32R)
        xn = sb("xn", [P, 2, PIECE])
        w_raw = sb("w_raw", [P, SLOTS, KT + IT, P])
        w_hi = sb("w_hi", [P, SLOTS, KT + IT, P], F32R)
        w_lo = sb("w_lo", [P, SLOTS, KT + IT, P], F32R)
        square = sb("square", [P, 4, PIECE])
        rms = sb("rms", [P, NP, PIECE])
        gate = sb("gate", [P, 2, PIECE])
        rows_io = sb("rows_io", [P, 2, D_MODEL])
        p_gate = pb("p_gate", [P, NP, CH])
        p_emb = pb("p_emb", [P, NP, CH])
        p_sum = pb("p_sum", [P, CH])
        x_t, gains = sh["rows_t"], sh["gains"]

        e_loaded = [sem("e_loaded0"), sem("e_loaded1")]
        w_loaded = [sem(f"w_loaded{s}") for s in range(SLOTS)]
        e_turned, e_hi_ready, e_lo_ready = sem("e_turned"), sem("e_hi_ready"), sem("e_lo_ready")
        w_hi_ready, w_lo_ready = sem("w_hi_ready"), sem("w_lo_ready")
        squared = sem("squared")
        added = sem("added")
        rms_ready, rstd_ready = sem("rms_ready"), sem("rstd_ready")
        xn_ready, xn_hi_ready, xn_lo_ready = sem("xn_ready"), sem("xn_hi_ready"), sem("xn_lo_ready")
        products, gated, embedded, residual = sem("products"), sem("gated"), sem("embedded"), sem("residual")
        turned, out_act, out_dve = sem("turned"), sem("out_act"), sem("out_dve")
        stored = [sem("stored0"), sem("stored1")]

        with nc.Block() as block:
            @block.sync
            def _(sp):
                def load_e(half):
                    sp.dma_start(rows_io[:, half, :].rearrange("p (t e) -> p t e", e=PLE),
                                 d["p_prompt"][0, 0][half * CH:(half + 1) * CH, :].rearrange("(t p) e -> p t e", p=P))\
                        .then_inc(e_loaded[half], 16)

                def load_w(m):
                    if m >= SLOTS:
                        sp.wait_ge(w_lo_ready, m - SLOTS + 1)
                    for k0, kn, name in ((0, KT, "w_ple_gate"), (KT, IT, "w_ple")):
                        sp.dma_start(w_raw[:, m % SLOTS, k0:k0 + kn],
                                     d[name][0].rearrange("(k p) n -> p k n", p=P)[:, :, m * P:(m + 1) * P])\
                            .then_inc(w_loaded[m % SLOTS], 16)

                load_e(0)
                load_e(1)
                for m in range(SLOTS):
                    load_w(m)
                sp.wait_ge(e_turned, 1)
                sp.wait_ge(e_loaded[0], 16)
                sp.dma_start(rows_io[:N_NEW, 0, 0:PLE], d["p_sample"][0].rearrange("b s e -> (b s) e"))\
                    .then_inc(e_loaded[0], 16)
                for m in range(SLOTS, KT):
                    load_w(m)
                for t in range(NT):
                    t0, rows = TILES[t]
                    sp.wait_ge(out_act, t + 1)
                    sp.wait_ge(out_dve, t + 1)
                    sp.dma_start(d["y_p"][t0:t0 + rows, :] if t < NPT else d["y_s"], rows_io[:rows, t % 2, :])\
                        .then_inc(stored[t % 2], 16)
                for s in range(2):
                    sp.wait_ge(stored[s], 16 * len(range(s, NT, 2)))

            @block.tensor
            def _(pe):
                def sum_squares(q):
                    for k in range(KT):
                        pe.wait_ge(squared, KT * q + k + 1)
                        if k == 0 and q > 0:
                            pe.wait_ge(rms_ready, q)
                        last = nc.tensor.matmul(p_sum[:, 0:PIECE], sh["ones"][:, :], square[:, k % 4, :],
                                                start=(k == 0), stop=(k == KT - 1))
                        last.then_inc(added, 1)

                def turn_e(t):
                    t0, rows = TILES[t]
                    pe.wait_ge(e_loaded[t // 4 % 2], 16 if t < NPT else 32)
                    half, c0 = divmod(t % NPT * PLE, D_MODEL)
                    if t >= NP:
                        pe.wait_ge(e_lo_ready, t - NP + 1)
                    for k in range(IT):
                        last = nc.tensor.transpose(p_emb[:, t % NP, k * P:k * P + rows],
                                                   rows_io[:rows, half, c0 + k * P:c0 + (k + 1) * P],
                                                   sh["ident"][:rows, :rows])
                    last.then_inc(e_turned, 1)

                sum_squares(0)
                for m in range(KT):
                    pe.wait_ge(w_lo_ready, m + 1)
                    for q in range(NP):
                        if m == 0:
                            pe.wait_ge(xn_lo_ready, KT * (q + 1))
                        else:
                            pe.wait_ge(embedded, NP * (m - 1) + q + 1)
                        for out, w0, kn, hi, lo in ((p_gate, 0, KT, xn_hi, xn_lo), (p_emb, KT, IT, e_hi, e_lo)):
                            if m == 0 and q == 0 and out is p_emb:
                                sum_squares(1)
                                for t in range(NT):
                                    turn_e(t)
                                sum_squares(2)
                                pe.wait_ge(e_lo_ready, NT)
                            for k in range(kn):
                                for part, (w, a) in enumerate(((w_hi, hi), (w_hi, lo), (w_lo, hi))):
                                    last = nc.tensor.matmul(out[:, q, 0:PIECE], w[:, m % SLOTS, w0 + k, :], piece(a, k, q),
                                                            start=(k == 0 and part == 0), stop=(k == kn - 1 and part == 2))
                        last.then_inc(products, 1)
                pe.wait_ge(residual, NP * KT)
                for t in range(NT):
                    t0, rows = TILES[t]
                    bank = p_gate if t % 2 == 0 else p_emb
                    if t >= 2:
                        pe.wait_ge(out_act, t - 1)
                        pe.wait_ge(out_dve, t - 1)
                    for k in range(KT):
                        last = nc.tensor.transpose(bank[:rows, k // 4, k % 4 * P:(k % 4 + 1) * P],
                                                   x_t[:, k, t0:t0 + rows], sh["ident"][:, :])
                    last.then_inc(turned, 1)

            @block.scalar
            def _(act):
                def split_w(m):
                    act.wait_ge(w_loaded[m % SLOTS], 32 * (m // SLOTS + 1))
                    if m >= SLOTS:
                        act.wait_ge(products, NP * (m - SLOTS + 1))
                    nc.scalar.activation(w_hi[:, m % SLOTS], w_raw[:, m % SLOTS], ACT.Copy).then_inc(w_hi_ready, 1)

                def e_split(t):
                    t0, rows = TILES[t]
                    act.wait_ge(e_turned, t + 1)
                    nc.scalar.activation(e_hi[:, :, t0:t0 + rows],
                                         p_emb[:, t % NP, 0:PLE].rearrange("p (k m) -> p k m", k=IT)[:, :, 0:rows],
                                         ACT.Copy).then_inc(e_hi_ready, 1)

                def squares(q):
                    for k in range(KT):
                        n = KT * q + k
                        if n >= 4:
                            act.wait_ge(added, n - 3)
                        nc.scalar.activation(square[:, k % 4, :], piece(x_t, k, q), ACT.Square).then_inc(squared, 1)

                def root(q):
                    act.wait_ge(added, KT * (q + 1))
                    nc.scalar.activation(rms[:, q, :], p_sum[:, 0:PIECE], ACT.Sqrt, scale=1.0 / D_MODEL,
                                         bias=sh["eps"][:, :]).then_inc(rms_ready, 1)

                def normed_hi(q):
                    for k in range(KT):
                        n = KT * q + k
                        act.wait_ge(xn_ready, n + 1)
                        nc.scalar.activation(piece(xn_hi, k, q), xn[:, n % 2, :], ACT.Copy).then_inc(xn_hi_ready, 1)

                squares(0)
                root(0)
                split_w(0)
                normed_hi(0)
                squares(1)
                root(1)
                for t in range(NT):
                    e_split(t)
                normed_hi(1)
                squares(2)
                root(2)
                normed_hi(2)
                for m in range(1, SLOTS):
                    split_w(m)
                for m in range(KT):
                    for q in range(NP):
                        n = NP * m + q
                        act.wait_ge(products, n + 1)
                        if n >= 2:
                            act.wait_ge(residual, n - 1)
                        nc.scalar.activation(gate[:, n % 2, :], p_gate[:, q, 0:PIECE], ACT.Sigmoid).then_inc(gated, 1)
                    if m + SLOTS < KT:
                        split_w(m + SLOTS)
                for t in range(NT):
                    rows = TILES[t][1]
                    bank = p_gate if t % 2 == 0 else p_emb
                    act.wait_ge(turned, t + 1)
                    if t >= 2:
                        act.wait_ge(stored[t % 2], 16 * (t // 2))
                    nc.scalar.copy(rows_io[:rows, t % 2, 0:CH], bank[:rows, 0, :]).then_inc(out_act, 1)

            @block.vector
            def _(dve):
                def split_w(m):
                    dve.wait_ge(w_hi_ready, m + 1)
                    nc.vector.tensor_tensor(w_lo[:, m % SLOTS], w_raw[:, m % SLOTS], w_hi[:, m % SLOTS].bitcast(F32),
                                            ALU.subtract).then_inc(w_lo_ready, 1)

                def e_split(t):
                    t0, rows = TILES[t]
                    dve.wait_ge(e_hi_ready, t + 1)
                    nc.vector.tensor_tensor(e_lo[:, :, t0:t0 + rows],
                                            p_emb[:, t % NP, 0:PLE].rearrange("p (k m) -> p k m", k=IT)[:, :, 0:rows],
                                            e_hi[:, :, t0:t0 + rows].bitcast(F32), ALU.subtract).then_inc(e_lo_ready, 1)

                def low(n):
                    dve.wait_ge(xn_hi_ready, n + 1)
                    nc.vector.tensor_tensor(piece(xn_lo, n % KT, n // KT), xn[:, n % 2, :],
                                            piece(xn_hi, n % KT, n // KT).bitcast(F32), ALU.subtract).then_inc(xn_lo_ready, 1)

                def invert(q):
                    dve.wait_ge(rms_ready, q + 1)
                    nc.vector.reciprocal(rms[:, q, :], rms[:, q, :]).then_inc(rstd_ready, 1)
                    dve.wait_ge(rstd_ready, q + 1)

                def normalise(q):
                    for k in range(KT):
                        n = KT * q + k
                        if n >= 2:
                            dve.wait_ge(xn_lo_ready, n - 1)
                        nc.vector.scalar_tensor_tensor(out=xn[:, n % 2, :], in0=piece(x_t, k, q),
                                                       scalar=gains[:, 3, k:k + 1], in1=rms[:, q, :],
                                                       op0=ALU.mult, op1=ALU.mult).then_inc(xn_ready, 1)
                        if k >= 1:
                            low(n - 1)
                    low(KT * q + KT - 1)

                invert(0)
                split_w(0)
                normalise(0)
                for t in range(NT):
                    e_split(t)
                invert(1)
                normalise(1)
                invert(2)
                normalise(2)
                for m in range(1, SLOTS):
                    split_w(m)
                for m in range(KT):
                    for q in range(NP):
                        n = NP * m + q
                        dve.wait_ge(gated, n + 1)
                        nc.vector.tensor_tensor(gate[:, n % 2, :], gate[:, n % 2, :], p_emb[:, q, 0:PIECE], ALU.mult)\
                            .then_inc(embedded, 1)
                        dve.wait_ge(embedded, n + 1)
                        nc.vector.tensor_tensor(piece(x_t, m, q), piece(x_t, m, q), gate[:, n % 2, :], ALU.add)\
                            .then_inc(residual, 1)
                    if m + SLOTS < KT:
                        split_w(m + SLOTS)
                for t in range(NT):
                    rows = TILES[t][1]
                    bank = p_gate if t % 2 == 0 else p_emb
                    dve.wait_ge(turned, t + 1)
                    if t >= 2:
                        dve.wait_ge(stored[t % 2], 16 * (t // 2))
                    nc.vector.tensor_copy(rows_io[:rows, t % 2, CH:2 * CH], bank[:rows, 1, :]).then_inc(out_dve, 1)


def hymba_step(nc, d):
    with ExitStack() as ctx:
        def tensors(stack, shapes):
            return {n: stack.enter_context(nc.sbuf_tensor(n, s, (t or [F32])[0])) for n, (s, *t) in shapes.items()}

        sh = tensors(ctx, {"ident": ([P, P],), "ones": ([P, P],), "logf": ([P, NT, HEADS_A],)})
        first = nc.snapshot_sems()
        norm_and_project(nc, d, sh)
        sh |= tensors(ctx, {"rows_t": ([P, KT, TOK],), "gains": ([P, 4, KT],), "taps": ([P, 4, UT],), "eps": ([P, 1],)})
        sh["pages_loaded"] = [nc.alloc_semaphore(f"pages_loaded{g}") for g in range(GROUPS)]
        with ExitStack() as attention:
            rows = [N_NEW, DEC_BATCH, HEADS_A, DEC_SEQ]
            sh |= tensors(attention, {
                "win_bias": ([P, WIN_ROWS, HEADS_B, DEC_SEQ],),
                "new_mask": (rows,), "new_count": (rows,), "new_bias_a": (rows,), "new_bias_b": (rows,),
                "page_ids": ([P, GROUPS], I32), "pages": ([P, GROUPS, PAGE * HEADS_A],),
                "tri": ([P, P],), "ident_bf": ([P, P], BF16), "mask_bf": ([P, P], BF16),
                "neg_slope": ([P, HEADS_B],)})
            with ExitStack() as prompt:
                sh |= tensors(prompt, {"dist": ([P, SEQ],), "log_count": ([P, SEQ],), "neg_c": ([P, HEADS_A, NPT],)})
                build_tables(nc, d, sh)
                prompt_attention(nc, d, sh, "A")
                prompt_attention(nc, d, sh, "B")
            with ExitStack() as sample:
                sh |= tensors(sample, {"neg_c_past": ([P, DEC_BATCH, N_PAGES, HEADS_A],)})
                sample_tables(nc, d, sh)
                sample_attention(nc, d, sh, "A")
                sample_attention(nc, d, sh, "B")
        nc.clear_and_free_semaphores(nc.allocated_since(first))
        nc.all_engine_barrier()
        project_out(nc, d, sh)
        conv_ffn(nc, d, sh)
        embed_and_store(nc, d, sh)


_INS = ['x_prompt', 'x_sample', 'p_prompt', 'p_sample', 'cache_fox_k', 'cache_fox_v', 'cache_fox_logf',
        'cache_win_k', 'cache_win_v', 'state_conv', 'page_table', 'g_attn_pre', 'w_in', 'b_forget', 'w_out',
        'g_attn_post', 'g_ffn_pre', 'w_up', 'conv_w', 'conv_b', 'w_down', 'g_ffn_post', 'g_ple', 'w_ple_gate',
        'w_ple']
_OUTS = [('y_p', (1, SEQ, D_MODEL)), ('y_s', (DEC_BATCH, DEC_SEQ, D_MODEL)),
         ('fk_p', (1, 1, SEQ, KV_A, HEAD)), ('fv_p', (1, 1, SEQ, KV_A, HEAD)), ('fl_p', (1, 1, SEQ, HEADS_A)),
         ('wk_p', (1, 1, SEQ, HEADS_B, HEAD)), ('wv_p', (1, 1, SEQ, HEADS_B, HEAD)), ('cv_p', (1, 1, 2, 2 * D_FF)),
         ('fk_s', (1, DEC_BATCH, DEC_SEQ, KV_A, HEAD)), ('fv_s', (1, DEC_BATCH, DEC_SEQ, KV_A, HEAD)),
         ('fl_s', (1, DEC_BATCH, DEC_SEQ, HEADS_A)),
         ('wk_s', (1, DEC_BATCH, DEC_SEQ, HEADS_B, HEAD)), ('wv_s', (1, DEC_BATCH, DEC_SEQ, HEADS_B, HEAD)),
         ('cv_s', (1, DEC_BATCH, 2, 2 * D_FF))]


def build(nc, args, outs):
    d = dict(args)
    for name, shape in _OUTS:
        a = outs[name]
        if name in ('y_p', 'y_s'):
            d[name] = a.rearrange("b s d -> (b s) d")
        elif name[:2] in ('fk', 'fv', 'wk', 'wv'):
            d[name] = a.rearrange("l b s h e -> (l b s) (h e)")
        elif name[:2] == 'fl':
            d[name] = a.rearrange("l b s h -> (l b s) h")
        else:
            d[name] = a
    x_p = args['x_prompt'].rearrange("b s d -> (b s) d")
    x_s = args['x_sample'].rearrange("b s d -> (b s) d")
    d["x"] = lambda t: x_p[t * P:(t + 1) * P, :] if t < NPT else x_s
    d["q_scratch"] = nc.dram_tensor("q_scratch", (TOK, 2 * CH), F32, kind="Internal").ap()
    d["mix_scratch"] = nc.dram_tensor("mix_scratch", (TOK, 2 * CH), F32, kind="Internal").ap()
    hymba_step(nc, d)


def kernel(**inputs):
    import numpy as _np
    import concourse.bacc as _bacc
    from concourse import mybir as _mybir
    from concourse.bass_utils import run_bass_kernel_spmd as _run

    nc = _bacc.Bacc("TRN2", target_bir_lowering=False, num_devices=1)
    arrays, args, outs = {}, {}, {}
    for name in _INS:
        a = _np.ascontiguousarray(inputs[name])
        arrays[f"in_{name}"] = a
        args[name] = nc.dram_tensor(f"in_{name}", a.shape, _mybir.dt.from_np(a.dtype), kind="ExternalInput").ap()
    for name, shape in _OUTS:
        outs[name] = nc.dram_tensor(f"out_{name}", shape, F32, kind="ExternalOutput").ap()
    build(nc, args, outs)
    r = _run(nc, [arrays], core_ids=[0])
    return tuple(r.results[0][f"out_{name}"] for name, _ in _OUTS)
```
